# Optimizing a Trainium2 kernel written in Bass

```python
import math
import jax, jax.numpy as jnp
from jax import lax
import numpy as np

D_MODEL = 1024
BATCH = 1
SEQ = 256
DEPTH = 1

GRID_W = 64
CTX_LEN = 256
N_MIXERS = 2
M_HEADS = 4
M_DV = D_MODEL // M_HEADS
M_DK = M_DV // 2
M_CHUNK = 128
M_PROJ = 2 * M_HEADS * M_DK + 2 * M_HEADS * M_DV + 4 * M_HEADS
F_GROUPS = 8
F_GROUP_DIM = D_MODEL // F_GROUPS
FFN_DIM = 2816
CONV_W = 3
EPS = 1e-6


def rmsnorm(x, g):
    x32 = x.astype(jnp.float32)
    y = x32 * lax.rsqrt(jnp.mean(x32 * x32, axis=-1, keepdims=True) + EPS)
    return (y * g.astype(jnp.float32)).astype(x.dtype)

def modulate(h, shift, scale):
    return h * (1 + scale[..., None, :]) + shift[..., None, :]

def _ctx_stream_needed(layer):
    return any(j % N_MIXERS == 0 for j in range(layer + 1, DEPTH))

def mlstm_project(h, w_in, b_in):
    B, T, _ = h.shape
    hk, hv = M_HEADS * M_DK, M_HEADS * M_DV
    p = h @ w_in + b_in
    q, k, v, o, gates = jnp.split(p, [hk, 2 * hk, 2 * hk + hv, 2 * hk + 2 * hv], axis=-1)

    def heads(t, d):
        return t.reshape(B, T, M_HEADS, d).transpose(0, 2, 1, 3).astype(jnp.float32)

    q = heads(q, M_DK)
    k = heads(k, M_DK) * (M_DK ** -0.5)
    v = heads(v, M_DV)
    g = gates.astype(jnp.float32).reshape(B, T, 4, M_HEADS).transpose(2, 0, 3, 1)
    fwd = (g[0], jax.nn.log_sigmoid(g[1]))
    bwd = (g[2], jax.nn.log_sigmoid(g[3]))
    return q, k, v, o, fwd, bwd

def mlstm_zero_state(B):
    return (jnp.zeros((B, M_HEADS, M_DK, M_DV), jnp.float32),
            jnp.zeros((B, M_HEADS, M_DK), jnp.float32),
            jnp.zeros((B, M_HEADS), jnp.float32))

def mlstm_chunk_scan(q, k, v, logi, logf, state0, with_outputs):
    B, H, T, _ = q.shape
    L = M_CHUNK
    nc = T // L

    def chunks(t):
        return jnp.moveaxis(t.reshape((B, H, nc, L) + t.shape[3:]), 2, 0)

    tri = jnp.tril(jnp.ones((L, L), dtype=bool))

    def step(carry, inp):
        C, n, m = carry
        qc, kc, vc, li, lf = inp
        b = jnp.cumsum(lf, axis=-1)
        bL = b[..., -1]
        g_s = bL[..., None] - b + li
        m_new = jnp.maximum(bL + m, jnp.max(g_s, axis=-1))
        a = jnp.exp(bL + m - m_new)
        ws = jnp.exp(g_s - m_new[..., None])
        C_new = a[..., None, None] * C + jnp.einsum('bhs,bhsd,bhse->bhde', ws, kc, vc)
        n_new = a[..., None] * n + jnp.einsum('bhs,bhsd->bhd', ws, kc)
        if not with_outputs:
            return (C_new, n_new, m_new), None
        dmat = jnp.where(tri, b[..., :, None] - b[..., None, :] + li[..., None, :], -jnp.inf)
        inter = b + m[..., None]
        m_t = jnp.maximum(inter, jnp.max(dmat, axis=-1))
        w_inter = jnp.exp(inter - m_t)
        s = jnp.einsum('bhtd,bhsd->bhts', qc, kc) * jnp.exp(dmat - m_t[..., None])
        num = w_inter[..., None] * jnp.einsum('bhtd,bhde->bhte', qc, C) + jnp.einsum('bhts,bhse->bhte', s, vc)
        den = w_inter * jnp.einsum('bhtd,bhd->bht', qc, n) + jnp.sum(s, axis=-1)
        h = num / jnp.maximum(jnp.abs(den), jnp.exp(-m_t))[..., None]
        return (C_new, n_new, m_new), h

    state, hs = lax.scan(step, state0, (chunks(q), chunks(k), chunks(v), chunks(logi), chunks(logf)))
    if with_outputs:
        hs = jnp.moveaxis(hs, 0, 2).reshape(B, H, T, M_DV)
    return hs, state

def mlstm_direction(q, k, v, gates, state0, reverse, with_outputs):
    logi, logf = gates
    if reverse:
        q, k, v = q[:, :, ::-1], k[:, :, ::-1], v[:, :, ::-1]
        logi, logf = logi[..., ::-1], logf[..., ::-1]
    h, state = mlstm_chunk_scan(q, k, v, logi, logf, state0, with_outputs)
    if reverse and with_outputs:
        h = h[:, :, ::-1]
    return h, state

def mlstm_readout(h, o, norm_g, w_out):
    B, H, T, _ = h.shape
    hn = h * lax.rsqrt(jnp.mean(h * h, axis=-1, keepdims=True) + EPS)
    hn = hn * norm_g.astype(jnp.float32).reshape(H, 1, M_DV)
    hn = hn.transpose(0, 2, 1, 3).reshape(B, T, H * M_DV)
    y = (hn * jax.nn.sigmoid(o.astype(jnp.float32))).astype(o.dtype)
    return y @ w_out

def mlstm_mixer(hx, hc, w_in, b_in, norm_g, w_out, ctx_outputs):
    B = hx.shape[0]
    s0 = mlstm_zero_state(B)
    qc, kc, vc, oc, gfc, gbc = mlstm_project(hc, w_in, b_in)
    hcf, st_f = mlstm_direction(qc, kc, vc, gfc, s0, False, ctx_outputs)
    hcb, st_b = mlstm_direction(qc, kc, vc, gbc, s0, True, ctx_outputs)
    qx, kx, vx, ox, gfx, gbx = mlstm_project(hx, w_in, b_in)
    hxf, _ = mlstm_direction(qx, kx, vx, gfx, st_f, False, True)
    hxb, _ = mlstm_direction(qx, kx, vx, gbx, st_b, True, True)
    yx = mlstm_readout(hxf + hxb, ox, norm_g, w_out)
    yc = mlstm_readout(hcf + hcb, oc, norm_g, w_out) if ctx_outputs else None
    return yx, yc

def fourier_mixer(h, w_out, b_out):
    B, T, D = h.shape
    hg = h.astype(jnp.float32).reshape(B, T, F_GROUPS, F_GROUP_DIM)
    y = jnp.real(jnp.fft.fft2(hg, axes=(1, 3), norm="ortho")).reshape(B, T, D).astype(h.dtype)
    return y @ w_out + b_out

def dwconv3(g, w, b, axis):
    n = g.shape[axis]
    pad = [(0, 0)] * g.ndim
    pad[axis] = (1, 1)
    gp = jnp.pad(g, pad)
    return (lax.slice_in_dim(gp, 0, n, axis=axis) * w[0]
            + lax.slice_in_dim(gp, 1, n + 1, axis=axis) * w[1]
            + lax.slice_in_dim(gp, 2, n + 2, axis=axis) * w[2] + b)

def conv_ffn(h, up_w, conv_w, conv_b, down_w, on_grid):
    u, g = jnp.split(h @ up_w, 2, axis=-1)
    if on_grid:
        B, T, F = g.shape
        rows = T // GRID_W
        g = dwconv3(g.reshape(B, rows, GRID_W, F), conv_w, conv_b, axis=2).reshape(B, T, F)
    else:
        g = dwconv3(g, conv_w, conv_b, axis=1)
    return (jax.nn.silu(g) * u) @ down_w

def first_inputs(seed: int = 0) -> dict:
    key = jax.random.key(seed)
    ks = jax.random.split(key, 24)
    D, F = D_MODEL, FFN_DIM
    NA = (DEPTH + N_MIXERS - 1) // N_MIXERS
    NB = DEPTH // N_MIXERS
    nrm = jax.random.normal
    x = nrm(ks[0], (BATCH, SEQ, D), jnp.float32)
    c = nrm(ks[1], (BATCH, D), jnp.float32)
    ctx = nrm(ks[2], (BATCH, CTX_LEN, D), jnp.float32)
    c_ctx = nrm(ks[3], (D,), jnp.float32)
    ada_w = nrm(ks[4], (DEPTH, D, 6 * D), jnp.float32) * D ** -0.5
    ada_b = 0.02 * nrm(ks[5], (DEPTH, 6 * D), jnp.float32)
    pre_mix_g = 1.0 + 0.05 * nrm(ks[6], (DEPTH, D), jnp.float32)
    post_mix_g = 1.0 + 0.05 * nrm(ks[7], (DEPTH, D), jnp.float32)
    pre_ffn_g = 1.0 + 0.05 * nrm(ks[8], (DEPTH, D), jnp.float32)
    post_ffn_g = 1.0 + 0.05 * nrm(ks[9], (DEPTH, D), jnp.float32)
    ffn_up_w = nrm(ks[10], (DEPTH, D, 2 * F), jnp.float32) * D ** -0.5
    ffn_conv_w = nrm(ks[11], (DEPTH, CONV_W, F), jnp.float32) * CONV_W ** -0.5
    ffn_conv_b = 0.02 * nrm(ks[12], (DEPTH, F), jnp.float32)
    ffn_down_w = nrm(ks[13], (DEPTH, F, D), jnp.float32) * F ** -0.5
    m_in_w = nrm(ks[14], (NA, D, M_PROJ), jnp.float32) * D ** -0.5
    lin_b = 0.02 * nrm(ks[15], (NA, M_PROJ - 4 * M_HEADS), jnp.float32)
    f_base = jnp.linspace(3.0, 6.0, M_HEADS, dtype=jnp.float32)
    gn = 0.1 * nrm(ks[16], (NA, 4, M_HEADS), jnp.float32)
    gate_b = gn + jnp.stack([jnp.zeros_like(f_base), f_base, jnp.zeros_like(f_base), f_base])[None]
    m_in_b = jnp.concatenate([lin_b, gate_b.reshape(NA, 4 * M_HEADS)], axis=-1)
    m_norm_g = 1.0 + 0.05 * nrm(ks[17], (NA, M_HEADS * M_DV), jnp.float32)
    m_out_w = nrm(ks[18], (NA, M_HEADS * M_DV, D), jnp.float32) * (M_HEADS * M_DV) ** -0.5
    f_out_w = nrm(ks[19], (NB, D, D), jnp.float32) * D ** -0.5
    f_out_b = 0.02 * nrm(ks[20], (NB, D), jnp.float32)
    return {"x": x, "c": c, "ctx": ctx, "c_ctx": c_ctx,
            "ada_w": ada_w, "ada_b": ada_b,
            "pre_mix_g": pre_mix_g, "post_mix_g": post_mix_g,
            "pre_ffn_g": pre_ffn_g, "post_ffn_g": post_ffn_g,
            "ffn_up_w": ffn_up_w, "ffn_conv_w": ffn_conv_w, "ffn_conv_b": ffn_conv_b,
            "ffn_down_w": ffn_down_w,
            "m_in_w": m_in_w, "m_in_b": m_in_b, "m_norm_g": m_norm_g, "m_out_w": m_out_w,
            "f_out_w": f_out_w, "f_out_b": f_out_b}

def first_block(x, c, ctx, c_ctx, ada_w, ada_b, pre_mix_g, post_mix_g, pre_ffn_g, post_ffn_g,
              ffn_up_w, ffn_conv_w, ffn_conv_b, ffn_down_w,
              m_in_w, m_in_b, m_norm_g, m_out_w, f_out_w, f_out_b):
    cx = jax.nn.silu(c)
    cc = jax.nn.silu(c_ctx)
    h_ctx = ctx
    for i in range(DEPTH):
        is_mlstm = (i % N_MIXERS) == 0
        j = i // N_MIXERS
        ctx_out = _ctx_stream_needed(i)
        sh1, sc1, g1, sh2, sc2, g2 = jnp.split(cx @ ada_w[i] + ada_b[i], 6, axis=-1)
        if is_mlstm or ctx_out:
            csh1, csc1, cg1, csh2, csc2, cg2 = jnp.split(cc @ ada_w[i] + ada_b[i], 6, axis=-1)
        hx = modulate(rmsnorm(x, pre_mix_g[i]), sh1, sc1)
        if is_mlstm:
            hc = modulate(rmsnorm(h_ctx, pre_mix_g[i]), csh1, csc1)
            yx, yc = mlstm_mixer(hx, hc, m_in_w[j], m_in_b[j], m_norm_g[j], m_out_w[j], ctx_out)
        else:
            yx = fourier_mixer(hx, f_out_w[j], f_out_b[j])
            if ctx_out:
                hc = modulate(rmsnorm(h_ctx, pre_mix_g[i]), csh1, csc1)
                yc = fourier_mixer(hc, f_out_w[j], f_out_b[j])
        x = x + g1[..., None, :] * rmsnorm(yx, post_mix_g[i])
        if ctx_out:
            h_ctx = h_ctx + cg1[..., None, :] * rmsnorm(yc, post_mix_g[i])
        hx = modulate(rmsnorm(x, pre_ffn_g[i]), sh2, sc2)
        yx = conv_ffn(hx, ffn_up_w[i], ffn_conv_w[i], ffn_conv_b[i], ffn_down_w[i], True)
        x = x + g2[..., None, :] * rmsnorm(yx, post_ffn_g[i])
        if ctx_out:
            hc = modulate(rmsnorm(h_ctx, pre_ffn_g[i]), csh2, csc2)
            yc = conv_ffn(hc, ffn_up_w[i], ffn_conv_w[i], ffn_conv_b[i], ffn_down_w[i], False)
            h_ctx = h_ctx + cg2[..., None, :] * rmsnorm(yc, post_ffn_g[i])
    return x


PLE_DIM = 256
MIX_WIDTH = D_MODEL
GDN_WIDTH = D_MODEL // 2
GDN_HEAD_DIM = 128
GDN_HEADS = GDN_WIDTH // GDN_HEAD_DIM
FOX_WIDTH = MIX_WIDTH - GDN_WIDTH
FOX_HEAD_DIM = 64
FOX_HEADS = FOX_WIDTH // FOX_HEAD_DIM
CONV_WIDTH = 4
CHUNK = 64
Q_BLOCK = 128
D_FF = -(-8 * D_MODEL // (3 * 256)) * 256

IN_SIZES = [3 * GDN_WIDTH, GDN_WIDTH, GDN_HEADS, GDN_HEADS, 3 * FOX_WIDTH, FOX_HEADS]
D_IN = sum(IN_SIZES)
IN_SPLITS = [sum(IN_SIZES[:i + 1]) for i in range(len(IN_SIZES) - 1)]


def rmsnorm_2(x, w):
    xf = x.astype(jnp.float32)
    y = xf * lax.rsqrt(jnp.mean(xf * xf, axis=-1, keepdims=True) + EPS)
    return (y * w.astype(jnp.float32)).astype(x.dtype)

def l2norm(x):
    return x * lax.rsqrt(jnp.sum(x * x, axis=-1, keepdims=True) + EPS)

def causal_depthwise_conv(x, w):
    c = x.shape[-1]
    return lax.conv_general_dilated(
        x, w.astype(x.dtype)[:, None, :], window_strides=(1,),
        padding=[(CONV_WIDTH - 1, 0)], dimension_numbers=('NWC', 'WIO', 'NWC'),
        feature_group_count=c)

def gated_delta_rule(q, k, v, g, beta):
    b, s, h, dk = q.shape
    dv = v.shape[-1]
    n = s // CHUNK

    def chunk(t):
        return jnp.moveaxis(t.reshape((b, n, CHUNK, h) + t.shape[3:]), 3, 2)

    q = chunk(q * (dk ** -0.5))
    k, v, g, beta = chunk(k), chunk(v), chunk(g), chunk(beta)
    gc = jnp.cumsum(g, axis=-1)
    lower = jnp.tril(jnp.ones((CHUNK, CHUNK), bool))
    strict = jnp.tril(jnp.ones((CHUNK, CHUNK), bool), -1)
    diff = gc[..., :, None] - gc[..., None, :]
    decay = jnp.where(lower, jnp.exp(jnp.where(lower, diff, 0.0)), 0.0)
    kb = k * beta[..., None]
    vb = v * beta[..., None]
    kk = jnp.einsum('bnhid,bnhjd->bnhij', kb, k) * decay
    a_mat = jnp.where(strict, kk, 0.0) + jnp.eye(CHUNK, dtype=kk.dtype)
    rhs = jnp.concatenate([vb, kb * jnp.exp(gc)[..., None]], axis=-1)
    sol = lax.linalg.triangular_solve(a_mat, rhs, left_side=True, lower=True, unit_diagonal=True)
    u, w = sol[..., :dv], sol[..., dv:]
    qk = jnp.where(lower, jnp.einsum('bnhid,bnhjd->bnhij', q, k) * decay, 0.0)

    def step(state, xs):
        q_c, k_c, u_c, w_c, gc_c, qk_c = xs
        v_new = u_c - jnp.einsum('bhcd,bhde->bhce', w_c, state)
        o = (jnp.einsum('bhcd,bhde->bhce', q_c * jnp.exp(gc_c)[..., None], state)
             + jnp.einsum('bhij,bhje->bhie', qk_c, v_new))
        g_last = gc_c[..., -1]
        k_dec = k_c * jnp.exp(g_last[..., None] - gc_c)[..., None]
        state = state * jnp.exp(g_last)[..., None, None] + jnp.einsum('bhcd,bhce->bhde', k_dec, v_new)
        return state, o

    xs = tuple(jnp.moveaxis(t, 1, 0) for t in (q, k, u, w, gc, qk))
    state0 = jnp.zeros((b, h, dk, dv), jnp.float32)
    _, o = lax.scan(step, state0, xs)
    o = jnp.moveaxis(jnp.moveaxis(o, 0, 1), 2, 3)
    return o.reshape(b, s, h, dv)

def forgetting_attention(q, k, v, log_f):
    b, s, h, d = q.shape
    scale = d ** -0.5
    c = jnp.cumsum(log_f.astype(jnp.float32), axis=1).transpose(0, 2, 1)
    q, k, v = (t.transpose(0, 2, 1, 3) for t in (q, k, v))
    outs = []
    for blk in range(s // Q_BLOCK):
        q0, q1 = blk * Q_BLOCK, (blk + 1) * Q_BLOCK
        logits = jnp.einsum('bhqd,bhkd->bhqk', q[:, :, q0:q1], k[:, :, :q1],
                            preferred_element_type=jnp.float32) * scale
        logits = logits + c[:, :, q0:q1, None] - c[:, :, None, :q1]
        causal = jnp.arange(q0, q1)[:, None] >= jnp.arange(q1)[None, :]
        logits = jnp.where(causal, logits, -jnp.inf)
        prob = jax.nn.softmax(logits, axis=-1)
        outs.append(jnp.einsum('bhqk,bhkd->bhqd', prob.astype(v.dtype), v[:, :, :q1]))
    o = jnp.concatenate(outs, axis=2)
    return o.transpose(0, 2, 1, 3)

def second_inputs(seed: int = 0) -> dict:
    key = jax.random.key(seed)
    ks = jax.random.split(key, 20)
    f32 = jnp.float32
    nrm = lambda k, shape, s: jax.random.normal(k, shape, f32) * s
    gain = lambda k, shape: 1.0 + 0.1 * jax.random.normal(k, shape, f32)
    dt = jnp.exp(jax.random.uniform(ks[5], (DEPTH, GDN_HEADS), f32) * (np.log(0.1) - np.log(0.001)) + np.log(0.001))
    dt_bias = dt + jnp.log(-jnp.expm1(-dt))
    return {
        'x': nrm(ks[0], (BATCH, SEQ, D_MODEL), 1.0),
        'p': nrm(ks[1], (DEPTH, BATCH, SEQ, PLE_DIM), 1.0),
        'attn_norm_w': gain(ks[2], (DEPTH, D_MODEL)),
        'w_in': nrm(ks[3], (DEPTH, D_MODEL, D_IN), D_MODEL ** -0.5),
        'conv_w': nrm(ks[4], (DEPTH, CONV_WIDTH, 3 * GDN_WIDTH), CONV_WIDTH ** -0.5),
        'a_log': jnp.log(jax.random.uniform(ks[6], (DEPTH, GDN_HEADS), f32, 1.0, 16.0)),
        'dt_bias': dt_bias,
        'gdn_norm_w': gain(ks[7], (DEPTH, GDN_HEAD_DIM)),
        'fox_f_bias': 3.0 + 0.5 * jax.random.normal(ks[8], (DEPTH, FOX_HEADS), f32),
        'w_out': nrm(ks[9], (DEPTH, MIX_WIDTH, D_MODEL), MIX_WIDTH ** -0.5),
        'ffn_norm_w': gain(ks[10], (DEPTH, D_MODEL)),
        'w_gate_up': nrm(ks[11], (DEPTH, D_MODEL, 2 * D_FF), D_MODEL ** -0.5),
        'w_down': nrm(ks[12], (DEPTH, D_FF, D_MODEL), D_FF ** -0.5),
        'ple_norm_w': gain(ks[13], (DEPTH, D_MODEL)),
        'w_ple_gate': nrm(ks[14], (DEPTH, D_MODEL, D_MODEL), D_MODEL ** -0.5),
        'w_ple_proj': nrm(ks[15], (DEPTH, PLE_DIM, D_MODEL), PLE_DIM ** -0.5),
        'final_norm_w': gain(ks[16], (D_MODEL,)),
    }

def second_block(x, p, attn_norm_w, w_in, conv_w, a_log, dt_bias, gdn_norm_w, fox_f_bias, w_out,
              ffn_norm_w, w_gate_up, w_down, ple_norm_w, w_ple_gate, w_ple_proj, final_norm_w):
    b, s, _ = x.shape
    f32 = jnp.float32
    h = x
    for i in range(DEPTH):
        xn = rmsnorm_2(h, attn_norm_w[i])
        proj = xn @ w_in[i]
        g_qkv, g_z, g_a, g_b, f_qkv, f_f = jnp.split(proj, IN_SPLITS, axis=-1)

        g_qkv = jax.nn.silu(causal_depthwise_conv(g_qkv, conv_w[i])).astype(f32)
        gq, gk, gv = jnp.split(g_qkv.reshape(b, s, 3 * GDN_HEADS, GDN_HEAD_DIM), 3, axis=2)
        gq, gk = l2norm(gq), l2norm(gk)
        beta = jax.nn.sigmoid(g_b.astype(f32))
        g_decay = -jnp.exp(a_log[i].astype(f32)) * jax.nn.softplus(g_a.astype(f32) + dt_bias[i].astype(f32))
        o_g = gated_delta_rule(gq, gk, gv, g_decay, beta)
        o_g = o_g * lax.rsqrt(jnp.mean(o_g * o_g, axis=-1, keepdims=True) + EPS) * gdn_norm_w[i].astype(f32)
        o_g = o_g * jax.nn.silu(g_z.astype(f32)).reshape(b, s, GDN_HEADS, GDN_HEAD_DIM)
        o_g = o_g.reshape(b, s, GDN_WIDTH).astype(h.dtype)

        fq, fk, fv = jnp.split(f_qkv.reshape(b, s, 3 * FOX_HEADS, FOX_HEAD_DIM), 3, axis=2)
        log_f = jax.nn.log_sigmoid(f_f.astype(f32) + fox_f_bias[i].astype(f32))
        o_f = forgetting_attention(fq, fk, fv, log_f).reshape(b, s, FOX_WIDTH).astype(h.dtype)

        h = h + jnp.concatenate([o_g, o_f], axis=-1) @ w_out[i]

        hn = rmsnorm_2(h, ffn_norm_w[i])
        gate, up = jnp.split(hn @ w_gate_up[i], 2, axis=-1)
        h = h + (jax.nn.silu(gate) * up) @ w_down[i]

        ple_gate = jax.nn.sigmoid(rmsnorm_2(h, ple_norm_w[i]) @ w_ple_gate[i])
        h = h + ple_gate * (p[i] @ w_ple_proj[i])
    return rmsnorm_2(h, final_norm_w)


def setup_inputs(seed=0):
    out = dict(first_inputs(seed))
    for name, value in second_inputs(seed + 1).items():
        if name != "x":
            out[name + "_2"] = value
    return out


def reference(
    x, c, ctx, c_ctx, ada_w, ada_b, pre_mix_g, post_mix_g, pre_ffn_g, post_ffn_g, ffn_up_w,
    ffn_conv_w, ffn_conv_b, ffn_down_w, m_in_w, m_in_b, m_norm_g, m_out_w, f_out_w, f_out_b,
    p_2, attn_norm_w_2, w_in_2, conv_w_2, a_log_2, dt_bias_2, gdn_norm_w_2, fox_f_bias_2,
    w_out_2, ffn_norm_w_2, w_gate_up_2, w_down_2, ple_norm_w_2, w_ple_gate_2, w_ple_proj_2,
    final_norm_w_2,
):
    x = first_block(
        x, c, ctx, c_ctx, ada_w, ada_b, pre_mix_g, post_mix_g, pre_ffn_g, post_ffn_g, ffn_up_w,
        ffn_conv_w, ffn_conv_b, ffn_down_w, m_in_w, m_in_b, m_norm_g, m_out_w, f_out_w, f_out_b,
    )
    return second_block(
        x, p_2, attn_norm_w_2, w_in_2, conv_w_2, a_log_2, dt_bias_2, gdn_norm_w_2, fox_f_bias_2,
        w_out_2, ffn_norm_w_2, w_gate_up_2, w_down_2, ple_norm_w_2, w_ple_gate_2, w_ple_proj_2,
        final_norm_w_2,
    )


_drawn_inputs = setup_inputs


def setup_inputs(seed=0):
    import zlib

    import numpy as np

    out = dict(_drawn_inputs(seed))
    spreads = {}
    factors = {'ffn_conv_b': 6.832, 'ple_norm_w_2': 4.374}
    for name, (base, spread) in spreads.items():
        noise = np.random.default_rng([zlib.crc32(name.encode()), seed]).standard_normal(out[name].shape)
        drawn = base * np.exp(spread * noise) if base else spread * noise
        out[name] = __import__('jax').numpy.asarray(drawn.astype(out[name].dtype))
    for name, factor in factors.items():
        out[name] = (out[name] * factor).astype(out[name].dtype)
    return out
```

```python
from contextlib import ExitStack

import concourse.bass as bass
from concourse import mybir

F32 = mybir.dt.float32
F32R = mybir.dt.float32r
ALU = mybir.AluOpType
ACT = mybir.ActivationFunctionType
AX_X = mybir.AxisListType.X

P = 128
T = 256
TT = T // P
D = 1024
KD = D // P
NB = 512
EPS = 1e-6
RING = 3
GROUP = 2048

MH, DK, DV = 4, 128, 256
FF = 2816
KF = FF // P
PAIRS = KF // 2
GRID_W = 64
GH, GD = 4, 128
FH, FD = 8, 64
PLE = 256
LEVELS = (2, 4, 8, 16, 32, 64)
NEG = -1.0e30


def plan_groups(I):
    groups, split, at = [], [], {}

    def add(w, k0, nk, c0, ncol, consumer="split"):
        if consumer == "split":
            split.append(len(groups))
        groups.append((w[k0 * P:(k0 + nk) * P, c0:c0 + ncol].rearrange("(k p) n -> p k n", p=P), nk, ncol, consumer))

    def block(name, w, c0, nk=KD):
        at.setdefault(name, []).append(len(split))
        for k0 in range(0, nk, 4):
            add(w, k0, min(4, nk - k0), c0, NB)

    def tiles(name, w, c0):
        at.setdefault(name, []).append(len(split))
        add(w, 0, KD, c0, 2 * P)

    def ada(v, consumer):
        for n in range(D // NB):
            for k0 in (0, 4):
                add(I["ada_w"][0], k0, 4, v * D + n * NB, NB, consumer)

    m_in, w_in = I["m_in_w"][0], I["w_in_2"][0]
    v0, o0 = 2 * MH * DK, 2 * MH * DK + MH * DV
    fox0 = 4 * GH * GD + 2 * GH
    ada(0, "ada1")
    ada(1, "ada1")
    block("k", m_in, MH * DK)
    block("q", m_in, 0)
    ada(2, "ada2")
    block("v", m_in, v0)
    ada(3, "ada2")
    block("v", m_in, v0 + NB)
    ada(4, "ada2")
    block("o", m_in, o0)
    ada(5, "ada2")
    block("o", m_in, o0 + NB)
    for n in range(2):
        block("mix_out", I["m_out_w"][0], n * NB)
    for j in range(PAIRS):
        tiles("up", I["ffn_up_w"][0], FF + 2 * j * P)
        tiles("up", I["ffn_up_w"][0], 2 * j * P)
    for n in range(2):
        block("down", I["ffn_down_w"][0], n * NB, KF)
    for j in range(6):
        tiles("gdn", w_in, 2 * j * P)
    for j in range(4):
        tiles("fox", w_in, fox0 + 2 * j * P)
    block("fox_v", w_in, fox0 + 2 * FH * FD)
    block("z", w_in, 3 * GH * GD)
    for n in range(2):
        block("att_out", I["w_out_2"][0], n * NB)
    for j in range(PAIRS):
        tiles("gate_up", I["w_gate_up_2"][0], 2 * j * P)
        tiles("gate_up", I["w_gate_up_2"][0], FF + 2 * j * P)
    for n in range(2):
        block("down2", I["w_down_2"][0], n * NB, KF)
    at["ple_p"] = [len(split)]
    add(I["w_ple_proj_2"][0], 0, 2, 0, D)
    for n in range(2):
        block("ple_g", I["w_ple_gate_2"][0], n * NB)
    return groups, split, at


def two_blocks(nc, I, out, STOP=None):
    groups, split, at = plan_groups(I)
    ada1 = [g for g, x in enumerate(groups) if x[3] == "ada1"]
    ada2 = [g for g, x in enumerate(groups) if x[3] == "ada2"]
    n_split = len(split)
    last_group = {"A": split[at["o"][1] + 1], "B": split[at["mix_out"][1] + 1], "D": split[at["down"][1] + 5],
                  "E": split[at["att_out"][1] + 1], None: len(groups) - 1}[STOP]
    n_split = sum(1 for g in split if g <= last_group)

    with ExitStack() as ctx:
        sems = {}

        def S(name):
            if name not in sems:
                sems[name] = ctx.enter_context(nc.semaphore(name))
            return sems[name]

        FAMILY = {
            "ss": (("norm1", 4), ("head", 8), ("post1", 4), ("norm2", 2), ("post2", 4), ("norm3", 2), ("gdn", 8),
                   ("norm4", 2), ("norm5", 2), ("final", 2)),
            "rstd": (("norm1", 1), ("head", 4), ("post1", 1), ("norm2", 1), ("post2", 1), ("norm3", 1), ("gdn", 2),
                     ("norm4", 1), ("norm5", 1), ("final", 1)),
            "diag": (("norm2", 2), ("norm3", 2), ("norm4", 2), ("norm5", 2)),
        }
        for kind, n in (("tr", 8), ("full", 8), ("hi", 4), ("hT", 4)):
            FAMILY[kind] = tuple((name, n) for name in ("y1", "norm2", "norm3", "mix", "norm4", "norm5"))

        def base(kind, name):
            before = 0
            for stage, n in FAMILY[kind]:
                if stage == name:
                    return before
                before += n

        def sb(scope, name, shape, dt=F32):
            return scope.enter_context(nc.sbuf_tensor(name, shape, dt))

        ps = ctx.enter_context(nc.psum_tensor("ps", [P, 8, NB], F32))
        raw = sb(ctx, "raw", [P, RING, GROUP])
        w_hi = sb(ctx, "w_hi", [P, RING, GROUP], F32R)
        w_lo = sb(ctx, "w_lo", [P, RING, GROUP], F32R)
        x = sb(ctx, "x", [P, TT, D])
        full = sb(ctx, "full", [P, KD, T])
        h_hi = sb(ctx, "h_hi", [P, KD, T], F32R)
        h_lo = sb(ctx, "h_lo", [P, KD, T], F32R)
        ident = sb(ctx, "ident", [P, P])
        s_le_t = sb(ctx, "s_le_t", [P, P])
        s_ge_t = sb(ctx, "s_ge_t", [P, P])
        s_lt_t = sb(ctx, "s_lt_t", [P, P])
        s_gt_t = sb(ctx, "s_gt_t", [P, P])
        ones = sb(ctx, "ones", [P, P])
        diag = sb(ctx, "diag", [P, 2 * TT, P])
        VEC = (("c", I["c"][0]), ("c_ctx", I["c_ctx"]), ("ada_b", I["ada_b"][0]), ("pre_mix", I["pre_mix_g"][0]),
               ("pre_ffn", I["pre_ffn_g"][0]), ("attn_norm", I["attn_norm_w_2"][0]), ("ffn_norm", I["ffn_norm_w_2"][0]),
               ("ple_norm", I["ple_norm_w_2"][0]), ("m_norm", I["m_norm_g"][0]), ("gdn_norm", I["gdn_norm_w_2"][0]))
        col, n_vec = {}, 0
        for name, src in VEC:
            col[name] = n_vec
            n_vec += src.shape[0] // P
        col["conv_w"], col["conv_b"], col["conv2"] = n_vec, n_vec + 3 * KF, n_vec + 4 * KF
        n_col = n_vec + 4 * KF + 48
        cols = sb(ctx, "cols", [P, n_col])

        def pcol(name, k):
            return cols[:, col[name] + k:col[name] + k + 1]

        cpad = sb(ctx, "cpad", [P, KD, 32])
        row_of = sb(ctx, "row_of", [P, 2])
        mod = sb(ctx, "mod", [P, 2 * KD, 2])
        mod2 = sb(ctx, "mod2", [P, 2 * KD])
        mhalf = sb(ctx, "mhalf", [P, 16])
        ss = sb(ctx, "ss", [P, 64])
        rstd = sb(ctx, "rstd", [P, 64])
        junk = sb(ctx, "junk", [P, D])
        junk_pool = sb(ctx, "junk_pool", [P, 1])
        tmp = sb(ctx, "tmp", [P, 2, NB])

        with ExitStack() as b1:
            gp1 = sb(b1, "gp1", [P, D])
            gp2 = sb(b1, "gp2", [P, D])
            acc2 = sb(b1, "acc2", [P, 2, D])
            acc1 = full[:].rearrange("p k t -> p (k t)").rearrange("p (a n) -> p a n", a=2)
            ada_acc = (acc1[:, 0], acc1[:, 1], acc2[:, 0], acc2[:, 1])
            with ExitStack() as mx:
                with ExitStack() as early:
                    c_hi = sb(early, "c_hi", [P, KD, T], F32R)
                    c_lo = sb(early, "c_lo", [P, KD, T], F32R)
                late = sb(mx, "late", [P, MH * 2 * (DV + 1) + TT * D])
                state = late[:, 0:MH * 2 * (DV + 1)].rearrange("p (h d e) -> p h d e", h=MH, d=2)
                hsum = late[:, MH * 2 * (DV + 1):].rearrange("p (t n) -> p t n", t=TT)
                r2 = sb(mx, "r2", [P, TT * D])
                cfull = r2[:].rearrange("p (k t) -> p k t", k=KD)
                qk_tok = r2[:].rearrange("p (a t n) -> p a t n", a=2, t=TT)
                so = r2[:].rearrange("p (t n) -> p t n", t=TT)
                r3 = sb(mx, "r3", [P, 2 * TT * MH * (DV + 1)])
                vaug = r3[:].rearrange("p (t h e) -> p t h e", t=2 * TT, h=MH)
                u_row = r3[0:MH, 2048:2048 + 2 * T].rearrange("p (d t) -> p d t", d=2)
                ws_row = r3[0:MH, 2560:2560 + 2 * T].rearrange("p (d t) -> p d t", d=2)
                ada_rows = r3[:, 0:4 * NB].rearrange("p (n c) -> p n c", n=4)
                vec_rows = (r3[0:n_vec, 2048:2048 + P], r3[0:4 * KF, 2048 + P:2048 + 2 * P],
                            r3[0:48, 2048 + 2 * P:2048 + 3 * P])
                qkT = sb(mx, "qkT", [P, MH, 2, T])
                prob = sb(mx, "prob", [P, MH, 2, 3 * P])
                prob_flat = prob[:].rearrange("p h d n -> p (h d n)")
                ctx_tok = prob_flat[:, 0:TT * D].rearrange("p (t n) -> p t n", t=TT)
                ymix = ctx_tok
                qTw = sb(mx, "qTw", [P, MH, 2, T])
                r4 = sb(mx, "r4", [P, 2 * TT * 2 * P])
                kw = r4[:].rearrange("p (b t d n) -> p b t d n", b=2, t=TT, d=2)
                m_row = r4[0:MH, 0:2 * T].rearrange("p (d t) -> p d t", d=2)
                w_row = r4[0:MH, 2 * T:4 * T].rearrange("p (d t) -> p d t", d=2)
                k_ctx = sb(mx, "k_ctx", [P, TT, NB])
                bias = sb(mx, "bias", [P, 2, NB])
                wg = sb(mx, "wg", [P, KD, 16])
                bg = sb(mx, "bg", [P, 16])
                gate = sb(mx, "gate", [P, 2 * TT, 16])
                gate_v = gate[:].rearrange("p t (d x h) -> p (t d) x h", d=2, x=2)
                lf = sb(mx, "lf", [P, 2 * TT * 2, MH])
                sp1 = sb(mx, "sp1", [P, 2 * TT * 2, MH])
                b_col = sb(mx, "b_col", [P, TT * 2, MH])
                u_col = sb(mx, "u_col", [P, TT * 2, MH])
                gs_col = sb(mx, "gs_col", [P, TT * 2, MH])
                ws_col = sb(mx, "ws_col", [P, TT * 2, MH])
                emt = sb(mx, "emt", [P, TT * 2, MH])
                b_ctx = sb(mx, "b_ctx", [MH, 2])
                m_ctx = sb(mx, "m_ctx", [MH, 4])
                sel = sb(mx, "sel", [MH, MH, P])
                den = sb(mx, "den", [P, 2, 4])
            with ExitStack() as fs:
                act_hi = sb(fs, "act_hi", [P, KF, T], F32R)
                act_lo = sb(fs, "act_lo", [P, KF, T], F32R)
                cv = sb(fs, "cv", [P, 2, 2, T])
                actf = sb(fs, "actf", [P, 2, 2, T])
        with ExitStack() as b2:
            r5 = sb(b2, "r5", [P, 12, T])
            r5f = r5[:].rearrange("p f t -> p (f t)")
            inv = r5f[:, 0:1024].rearrange("p (a i) -> p a i", i=P)
            invT = r5f[:, 1024:2048].rearrange("p (a i) -> p a i", i=P)
            xs = r5f[:, 2048:3072].rearrange("p (a i) -> p a i", i=P)
            qk_n = sb(b2, "qk_n", [P, 2, TT, NB])
            mix = qk_n[:].rearrange("p a t n -> p (a t n)").rearrange("p (t n) -> p t n", t=TT)
            vb = sb(b2, "vb", [P, TT, NB])
            k_beta = sb(b2, "k_beta", [P, NB])
            k_dec = sb(b2, "k_dec", [P, NB])
            q_exp = sb(b2, "q_exp", [P, NB])
            q_expT = sb(b2, "q_expT", [P, GH, P])
            gT = sb(b2, "gT", [P, GH, 2, T])
            gTf = gT[:].rearrange("p h a t -> p (h a t)")
            st1 = gTf[:, 0:NB]
            wT = gTf[:, NB:2 * NB]
            v_new = gTf[:, 2 * NB:3 * NB]
            decT = sb(b2, "decT", [P, TT * GH, P])
            u_tok = decT[:].rearrange("p (t h) i -> p t (h i)", t=TT)
            cT = sb(b2, "cT", [P, TT * GH, P])
            cTl = sb(b2, "cTl", [P, 2, TT * GH, P])
            c_mat = cTl[:, 1]
            qkT2 = sb(b2, "qkT2", [P, TT * GH, P])
            neg_c = sb(b2, "neg_c", [P, FH, T])
            foxT = sb(b2, "foxT", [P, 8, T])
            fox_v = sb(b2, "fox_v", [P, TT, NB])
            zs = sb(b2, "zs", [P, TT, NB])
            r6 = sb(b2, "r6", [P, 4, 3 * P])
            logit = r6[:, 0:2]
            prT = r6[:, 2:4]
            sq = r6[:].rearrange("p a n -> p (a n)")[:, 0:2 * NB].rearrange("p (t n) -> p t n", t=TT)
            level = sb(b2, "level", [P, 7, P])
            wsm = sb(b2, "wsm", [P, KD, 16])
            sm = sb(b2, "sm", [P, TT, 16])
            gprm = sb(b2, "gprm", [P, 16])
            g_dec = sb(b2, "g_dec", [P, TT, GH])
            beta = sb(b2, "beta", [P, TT, GH])
            lf2 = sb(b2, "lf2", [P, TT, FH])
            sp2 = sb(b2, "sp2", [P, TT, 16])
            gc = sb(b2, "gc", [P, 3, GH])
            egc = sb(b2, "egc", [P, 3, GH])
            fsum = sb(b2, "fsum", [P, 2, 4])
            og = sb(b2, "og", [P, TT, NB])
        with ExitStack() as b3:
            act2_hi = sb(b3, "act2_hi", [P, KF, T], F32R)
            act2_lo = sb(b3, "act2_lo", [P, KF, T], F32R)
            sil = sb(b3, "sil", [P, 2, 2, T])
            actf2 = sb(b3, "actf2", [P, 2, 2, T])
            p_tok = sb(b3, "p_tok", [P, TT, PLE])
            pT = sb(b3, "pT", [P, 2, T])
            p_hi = sb(b3, "p_hi", [P, 2, T], F32R)
            p_lo = sb(b3, "p_lo", [P, 2, T], F32R)
            gp3 = sb(b3, "gp3", [P, D])
            pgate = sb(b3, "pgate", [P, TT, D])

        raw_in = [S(f"raw_in{i}") for i in range(RING)]
        hi_ready, lo_ready, group_used = S("hi_ready"), S("lo_ready"), S("group_used")
        ada1_used, ada2_used = S("ada1_used"), S("ada2_used")

        def raw_view(g):
            _, nk, ncol, _ = groups[g]
            return raw[:, g % RING, :nk * ncol].rearrange("p (k n) -> p k n", k=nk)

        def part_view(part, s):
            _, nk, ncol, _ = groups[split[s]]
            return part[:, s % RING, :nk * ncol].rearrange("p (k n) -> p k n", k=nk)

        def raw_arrived(eng, g):
            eng.wait_ge(raw_in[g % RING], 16 * (g // RING + 1))

        def chained(eng, name):
            count = [0]

            def link(ins):
                count[0] += 1
                ins.then_inc(S(name), 1)
                eng.wait_ge(S(name), count[0])

            return link

        block = ctx.enter_context(nc.Block())


        @block.sync
        def _(sp):
            for g in range(last_group + 1):
                if g >= RING:
                    old = g - RING
                    consumer = groups[old][3]
                    if consumer == "ada1":
                        sp.wait_ge(ada1_used, ada1.index(old) + 1)
                    elif consumer == "ada2":
                        sp.wait_ge(ada2_used, ada2.index(old) + 1)
                    else:
                        sp.wait_ge(lo_ready, split.index(old) + 1)
                sp.dma_start(raw_view(g), groups[g][0]).then_inc(raw_in[g % RING], 16)
            for t in range(TT):
                if STOP:
                    if STOP != "A":
                        sp.wait_ge(S("x_upd"), {"B": 4, "D": 8, "E": 12}[STOP])
                    sp.dma_start(out[0, t * P:(t + 1) * P, :], x[:, t, :]).then_inc(S("out_done"), 16)
                else:
                    sp.wait_ge(S("result"), t + 1)
                    sp.dma_start(out[0, t * P:(t + 1) * P, :], pgate[:, t, :]).then_inc(S("out_done"), 16)
            sp.wait_ge(S("out_done"), 16 * TT)

        @block.gpsimd
        def _(pool):
            link = chained(pool, "pool_chain")

            def rms_scale(name, c0, n, width, halves=False):
                s = ss[:, c0:c0 + n]
                if halves:
                    link(pool.tensor_tensor(s, s, ss[:, c0 + n:c0 + 2 * n], ALU.add))
                link(pool.tensor_scalar(s, s, 1.0 / width, EPS, ALU.mult, ALU.add))
                pool.tensor_tensor(rstd[:, c0:c0 + n], s, mhalf[:, 0:n], ALU.pow).then_inc(S("rstd"), 1)

            def keep(a, op, pattern, channel, fill=0.0, base=0):
                return pool.affine_select(out=a, in_=a, compare_op=op, fill=fill, base=base, pattern=pattern,
                                          channel_multiplier=channel)

            for m in (ident, cpad, row_of):
                link(pool.memset(m[:], 0.0))
            for m in (s_le_t, s_ge_t, s_lt_t, s_gt_t, ones, sel):
                link(pool.memset(m[:], 1.0))
            link(pool.memset(mhalf[:], -0.5))
            link(keep(ident[:], ALU.not_equal, [[-1, P]], 1, fill=1.0))
            link(keep(s_le_t[:], ALU.is_ge, [[1, P]], -1))
            link(keep(s_ge_t[:], ALU.is_ge, [[-1, P]], 1))
            link(keep(s_lt_t[:], ALU.is_gt, [[1, P]], -1))
            link(keep(s_gt_t[:], ALU.is_gt, [[-1, P]], 1))
            for j in range(4):
                link(keep(row_of[:], ALU.not_equal, [[-1, 2]], 1, fill=1.0, base=-32 * j))
            keep(sel[:], ALU.is_equal, [[-1, MH], [0, P]], 1).then_inc(S("const_ready"), 1)

            pool.wait_ge(S("ss"), base("ss", "norm1") + 2 * TT)
            rms_scale("norm1", 0, 2 * TT, D)

            pool.wait_ge(S("gate_mm"), 1)
            pool.wait_ge(S("hT1"), 4)
            pool.memset(full[:], 0.0).then_inc(S("acc_zero"), 1)
            pool.memset(acc2[:], 0.0).then_inc(S("acc_zero"), 1)

            def causal(h):
                for d in range(2):
                    pool.wait_ge(S("prob_full"), 2 * h + d + 1)
                    sign = 1 - 2 * d
                    pr = prob[:, h, d, :]
                    link(keep(pr[:, d * P:(d + 1) * P], ALU.is_ge, [[sign, P]], -sign))
                    keep(pr[:, 2 * P:], ALU.is_ge, [[sign, P]], -sign).then_inc(S("prob_ready"), 1)

            def weighted_keys(h):
                if h >= 2:
                    pool.wait_ge(S("state_mm"), 2 * (h - 1))
                for t in range(TT):
                    for d in range(2):
                        ins = pool.tensor_scalar(kw[:, h % 2, t, d, :], k_ctx[:, t, h * DK:(h + 1) * DK],
                                                 ws_col[:, 2 * t + d, h:h + 1], None, ALU.mult)
                        if t == 0 or d == 0:
                            link(ins)
                ins.then_inc(S("kw_ready"), 1)

            causal(0)
            causal(1)
            causal(2)
            pool.wait_ge(S("ws_out"), 1)
            pool.wait_ge(S("k_done"), 4)
            pool.wait_ge(S("m_bcast"), 2 * MH)
            weighted_keys(0)
            weighted_keys(1)
            causal(3)
            if STOP == "A":
                return
            weighted_keys(2)
            weighted_keys(3)
            for h in range(MH):
                pool.wait_ge(S("ss"), base("ss", "head") + TT * (h + 1))
                rms_scale("head", 4 + TT * h, TT, DV)
            pool.wait_ge(S("ss"), base("ss", "post1") + 4)
            rms_scale("post1", 12, TT, D, halves=True)
            if STOP == "B":
                return
            pool.wait_ge(S("ss"), base("ss", "norm2") + TT)
            rms_scale("norm2", 16, TT, D)
            pool.wait_ge(S("ss"), base("ss", "post2") + 4)
            rms_scale("post2", 18, TT, D, halves=True)
            if STOP == "D":
                return

            pool.wait_ge(S("ss"), base("ss", "norm3") + TT)
            rms_scale("norm3", 22, TT, D)
            pool.wait_ge(S("x_upd"), 8)
            link(pool.memset(level[:], 1.0))
            for i in range(6):
                b = 2 << i
                view = level[:, i, :].rearrange("p (n b) -> p n b", b=b)
                link(keep(view, ALU.is_ge, [[-b, P // b], [0, b]], 1))
                link(keep(view, ALU.is_ge, [[b, P // b], [0, b]], -1, base=b - 1))
            for i in range(6, 0, -1):
                link(pool.tensor_tensor(level[:, i, :], level[:, i, :], level[:, i - 1, :], ALU.subtract))
            pool.memset(junk_pool[:], 0.0).then_inc(S("level_ready"), 1)

            for i in range(4):
                pool.wait_ge(S("ss_l2"), i + 1)
                s = ss[:, 24 + GH * i:24 + GH * (i + 1)]
                link(pool.tensor_scalar(s, s, EPS, float(GD) if i < 2 else 1.0, ALU.add, ALU.mult))
                pool.tensor_tensor(rstd[:, 24 + GH * i:24 + GH * (i + 1)], s, mhalf[:, 0:GH], ALU.pow)\
                    .then_inc(S("rstd_l2"), 1)
                if i < 2:
                    pool.wait_ge(S("dec_exp"), i + 1)
                    keep(decT[:, GH * i:GH * (i + 1), :], ALU.is_ge, [[0, GH], [1, P]], -1).then_inc(S("dec_ready"), 1)

            def by_head(out_, in_, scale, want):
                pool.tensor_tensor(out_.rearrange("p (h n) -> p h n", h=GH), in_.rearrange("p (h n) -> p h n", h=GH),
                                   scale.unsqueeze(2).to_broadcast([P, GH, GD]), ALU.mult).then_inc(S(want), 1)

            pool.wait_ge(S("tok_out"), 4)
            pool.wait_ge(S("egc_ready"), 1)
            by_head(q_exp[:], qk_n[:, 0, 1, :], egc[:, 0, :], "q_exp_ready")
            for t in range(TT):
                pool.wait_ge(S("cT_full"), t + 1)
                c = cT[:, GH * t:GH * (t + 1), :]
                ins = keep(c, ALU.is_gt, [[0, GH], [1, P]], -1)
                if t == 0:
                    link(ins)
            ins.then_inc(S("cT_ready"), 1)
            pool.wait_ge(S("cT_ready"), 1)

            def level_of(i):
                if i == 1:
                    pool.wait_ge(S("inv_ready"), TT)
                elif i >= 2:
                    pool.wait_ge(S("xs_mm"), TT * (i - 1))
                pool.tensor_tensor(cTl[:, i % 2], cT[:], level[:, i + 1, :].unsqueeze(1).to_broadcast([P, TT * GH, P]),
                                   ALU.mult).then_inc(S("cTl_ready"), 1)

            def fox_mask(h):
                pool.wait_ge(S("logit_ready"), TT * (h + 1))
                for c in (0, 2 * P):
                    keep(logit[:, h % 2, c:c + P], ALU.is_ge, [[-1, P]], 1, fill=NEG).then_inc(S("logit_masked"), 1)

            level_of(0)
            by_head(k_beta[:], qk_n[:, 1, 1, :], egc[:, 1, :], "k_beta_ready")
            by_head(k_dec[:], qk_n[:, 1, 0, :], egc[:, 2, :], "k_dec_ready")
            fox_mask(0)
            for i in range(1, len(LEVELS)):
                level_of(i)
                fox_mask(i)
            for h in range(len(LEVELS), FH):
                fox_mask(h)
            for t in range(TT):
                pool.wait_ge(S("ss"), base("ss", "gdn") + GH * (t + 1))
                rms_scale("gdn", 40 + GH * t, GH, GD)
            if STOP == "E":
                return
            for name, c0 in (("norm4", 48), ("norm5", 50), ("final", 52)):
                pool.wait_ge(S("ss"), base("ss", name) + TT)
                rms_scale(name, c0, TT, D)


        @block.scalar
        def _(act):
            s_next = [0]

            def hi_until(n):
                while s_next[0] < min(n, n_split):
                    s = s_next[0]
                    raw_arrived(act, split[s])
                    if s >= RING:
                        act.wait_ge(group_used, s - RING + 1)
                    act.copy(part_view(w_hi, s), raw_view(split[s])).then_inc(hi_ready, 1)
                    s_next[0] += 1

            def load(dst, src, sem_name):
                act.dma_start(dst, src).then_inc(S(sem_name), 16)

            n_sums = [0]

            def sum_sq(src, c):
                n_sums[0] += 1
                act.activation(junk[:, 0:src.shape[-1]], src, ACT.Square, accum_out=ss[:, c:c + 1]).then_inc(S("ss"), 1)
                act.wait_ge(S("ss"), n_sums[0])

            def norm(name, c0, arrived):
                for t in range(TT):
                    act.wait_ge(S("x_upd"), arrived[t])
                    sum_sq(x[:, t, :], c0 + t)

            def post(name, c0, g0):
                for n in range(2):
                    hi_until(at[g0][n] + n_groups(g0) + 2)
                    act.wait_ge(group_used, at[g0][n] + n_groups(g0))
                    for t in range(TT):
                        sum_sq(ps[:, 4 + 2 * n + t, :], c0 + TT * n + t)

            def n_groups(name):
                return at[name][1] - at[name][0]

            def hi_T(name):
                for i in range(KD // 2):
                    act.wait_ge(S("full"), base("full", name) + 2 * i + 2)
                    act.copy(h_hi[:, 2 * i:2 * i + 2, :], full[:, 2 * i:2 * i + 2, :]).then_inc(S("hi"), 1)

            for i, (name, src) in enumerate(VEC):
                n = src.shape[0] // P
                load(vec_rows[0][col[name]:col[name] + n, :], src.rearrange("(k p) -> k p", p=P), "vec_in")
            load(vec_rows[1][0:3 * KF, :], I["ffn_conv_w"][0].rearrange("w (a b) -> (w a) b", b=P), "vec_in")
            load(vec_rows[1][3 * KF:4 * KF, :], I["ffn_conv_b"][0].rearrange("(a b) -> a b", b=P), "vec_in")
            load(vec_rows[2], I["conv_w_2"][0].rearrange("w (a b) -> (w a) b", b=P), "vec_in")
            load(x[:], I["x"][0].rearrange("(t p) n -> p t n", p=P), "x_in")
            load(ctx_tok, I["ctx"][0].rearrange("(t p) n -> p t n", p=P), "ctx_in")
            gate0 = 2 * MH * DK + 2 * MH * DV
            load(wg[:], I["m_in_w"][0][:, gate0:gate0 + 16].rearrange("(k p) n -> p k n", p=P), "wg_in")
            load(bg[:], I["m_in_b"][0][gate0:gate0 + 16].partition_broadcast(P), "wg_in")
            bias_cols = (MH * DK, 0, 2 * MH * DK, 2 * MH * DK + NB, 2 * MH * DK + MH * DV, 2 * MH * DK + MH * DV + NB)

            def load_bias(i):
                load(bias[:, i % 2, :], I["m_in_b"][0][bias_cols[i]:bias_cols[i] + NB].partition_broadcast(P),
                     f"bias_in{i % 2}")

            load_bias(0)
            load_bias(1)
            load(gp1[:], I["post_mix_g"][0].partition_broadcast(P), "gp_in")
            load(gp2[:], I["post_ffn_g"][0].partition_broadcast(P), "gp_in")

            act.wait_ge(S("cols_ready"), 1)
            act.activation(cpad[:, :, 0:2], cols[:, 0:2 * KD].rearrange("p (c k) -> p k c", c=2), ACT.Silu)\
                .then_inc(S("c_ready"), 1)
            act.wait_ge(S("x_in"), 16)
            for t in range(TT):
                sum_sq(x[:, t, :], t)
            act.wait_ge(S("ctx_in"), 16)
            for t in range(TT):
                sum_sq(ctx_tok[:, t, :], TT + t)
            for n in (2, 3):
                act.wait_ge(ada1_used, 2 * n + 2)
                act.copy(ada_rows[:, n, :], ps[:, n, :]).then_inc(S("ada_rows_act"), 1)
            for i in range(KD // 2):
                act.wait_ge(S("full1"), 2 * i + 2)
                pair = slice(2 * i, 2 * i + 2)
                act.copy(h_hi[:, pair, :], full[:, pair, :]).then_inc(S("h1_hi"), 1)
                act.copy(c_hi[:, pair, :], cfull[:, pair, :]).then_inc(S("h1_hi"), 1)
            hi_until(3)
            act.wait_ge(S("gate_abs"), 1)
            act.activation(sp1[:], sp1[:], ACT.Exp, scale=-1.0).then_inc(S("gate_exp"), 1)
            act.wait_ge(S("gate_exp"), 1)
            act.activation(sp1[:], sp1[:], ACT.Ln, bias=ones[:, 0:1]).then_inc(S("gate_ln"), 1)
            act.wait_ge(S("acc_zero"), 2)
            for v in range(4):
                load(ada_acc[v][0:1, :], I["ada_b"][:, (2 + v) * D:(3 + v) * D], "ada_b_in")
            hi_until(4)
            act.wait_ge(S("k_done"), 4)
            load_bias(2)
            hi_until(5)
            act.wait_ge(S("mrow_ready"), 2)
            for d in range(2):
                act.activation(ws_row[:, d, :], ps[0:MH, 4, d * T:(d + 1) * T], ACT.Exp, bias=m_ctx[:, 2 + d:3 + d])\
                    .then_inc(S("ws_row"), 1)
            for d in range(2):
                act.activation(w_row[:, d, :], m_row[:, d, :], ACT.Exp, bias=m_ctx[:, d:d + 1], scale=-1.0)\
                    .then_inc(S("w_row"), 1)
            act.wait_ge(S("q_done"), 2)
            load_bias(3)
            hi_until(6)
            act.wait_ge(S("mt_ready"), 1)
            act.activation(emt[:], emt[:], ACT.Exp, scale=-1.0).then_inc(S("emt_ready"), 1)

            def decay(h):
                for d in range(2):
                    act.wait_ge(S("z_ready"), 2 * (2 * h + d) + 2)
                    act.activation(prob[:, h, d, :], prob[:, h, d, :], ACT.Exp, scale=-1.0).then_inc(S("decay_ready"), 1)

            decay(0)
            hi_until(7)
            decay(1)
            hi_until(8)
            act.wait_ge(S("v_done"), 4)
            load_bias(4)
            decay(2)
            hi_until(10)
            decay(3)
            hi_until(11)
            if STOP == "A":
                return
            act.wait_ge(S("v_done"), 8)
            load_bias(5)
            hi_until(12)

            def gate_o(n):
                for t in range(TT):
                    act.wait_ge(S("o_done"), TT * n + t + 1)
                    o = so[:, t, n * NB:(n + 1) * NB]
                    act.activation(o, o, ACT.Sigmoid).then_inc(S("so_ready"), 1)

            def head_squares(h):
                for t in range(TT):
                    act.wait_ge(S("h_sum"), TT * h + t + 1)
                    sum_sq(hsum[:, t, h * DV:(h + 1) * DV], 4 + TT * h + t)

            gate_o(0)
            hi_until(13)
            head_squares(0)
            hi_until(14)
            head_squares(1)
            gate_o(1)
            hi_until(15)
            head_squares(2)
            head_squares(3)
            hi_T("y1")
            post("post1", 12, "mix_out")
            if STOP == "B":
                return
            norm("norm2", 16, (2, 4))
            hi_T("norm2")

            for j in range(PAIRS):
                g = at["up"][2 * j]
                hi_until(g + 3)
                act.wait_ge(group_used, g + 1)
                if j >= 2:
                    act.wait_ge(S("act_full"), j - 1)
                for f in range(2):
                    k = 2 * j + f
                    act.activation(cv[:, j % 2, f, :], ps[:, 4 * (j % 2) + f, 0:T], ACT.Identity,
                                   bias=pcol("conv_b", k), scale=pcol("conv_w", KF + k)).then_inc(S("conv_mid"), 1)
                hi_until(g + 4)
                act.wait_ge(S("conv_done"), 2 * j + 2)
                act.activation(cv[:, j % 2], cv[:, j % 2], ACT.Silu).then_inc(S("silu_ready"), 1)
                hi_until(g + 5)
                act.wait_ge(S("act_full"), j + 1)
                act.copy(act_hi[:, 2 * j:2 * j + 2, :], actf[:, j % 2]).then_inc(S("act_hi_ready"), 1)
            post("post2", 18, "down")
            if STOP == "D":
                return

            norm("norm3", 22, (6, 8))
            load(wsm[:, :, 0:8], I["w_in_2"][0][:, 4 * GH * GD:4 * GH * GD + 2 * GH].rearrange("(k p) n -> p k n", p=P),
                 "small_in")
            f0 = 4 * GH * GD + 2 * GH + 3 * FH * FD
            load(wsm[:, :, 8:16], I["w_in_2"][0][:, f0:f0 + FH].rearrange("(k p) n -> p k n", p=P), "small_in")
            load(gprm[:, 0:4], I["dt_bias_2"][0].partition_broadcast(P), "small_in")
            load(gprm[:, 4:8], I["a_log_2"][0].partition_broadcast(P), "small_in")
            load(gprm[:, 8:16], I["fox_f_bias_2"][0].partition_broadcast(P), "small_in")
            hi_T("norm3")
            G0 = at["gdn"][0]
            hi_until(G0 + 3)
            act.wait_ge(S("gate_abs"), 2)
            act.activation(sp2[:], sp2[:], ACT.Exp, scale=-1.0).then_inc(S("gate_exp"), 1)
            act.activation(gprm[:, 4:8], gprm[:, 4:8], ACT.Exp).then_inc(S("gate_exp"), 1)
            act.wait_ge(S("gate_exp"), 3)
            act.wait_ge(S("beta_ready"), 1)
            act.activation(sp2[:], sp2[:], ACT.Ln, bias=ones[:, 0:1]).then_inc(S("gate_ln"), 1)

            def conv2_mid(f):
                act.activation(r5[:, f, :], ps[:, f % 4, 0:T], ACT.Copy, scale=pcol("conv2", 36 + f))\
                    .then_inc(S("conv2_mid"), 1)

            def conv2_silu(f):
                act.wait_ge(S("conv2_done"), f + 1)
                act.activation(r5[:, f, :], r5[:, f, :], ACT.Silu).then_inc(S("conv2_silu"), 1)

            def gdn(j):
                hi_until(G0 + j + 3)
                act.wait_ge(group_used, G0 + j + 1)
                conv2_mid(2 * j)
                conv2_mid(2 * j + 1)

            def fsum_out(i):
                act.wait_ge(S("fsum_mm"), i + 1)
                act.activation(neg_c[:, 2 * i:2 * i + 2, :], ps[:, 7, :].rearrange("p (b t) -> p b t", b=2), ACT.Copy,
                               scale=-1.0).then_inc(S("neg_c_out"), 1)

            def token_squares(i):
                act.wait_ge(S("tok_T"), i + 1)
                if i >= 2:
                    act.wait_ge(S("ss_l2"), i - 1)
                act.activation(sq[:, i % 2, :], ps[:, (4, 5, 6, 4)[i], :], ACT.Square).then_inc(S("sq_ready"), 1)

            def fox_evac(j):
                hi_until(at["fox"][j] + 3)
                act.wait_ge(group_used, at["fox"][j] + 1)
                for f in range(2):
                    act.copy(foxT[:, 2 * j + f, :], ps[:, 2 * (j % 2) + f, 0:T]).then_inc(S("fox_T"), 1)

            gdn(0)
            conv2_silu(0)
            conv2_silu(1)
            gdn(1)
            conv2_silu(2)
            conv2_silu(3)
            for t in range(TT):
                act.wait_ge(S("dec_z"), t + 1)
                d = decT[:, GH * t:GH * (t + 1), :]
                act.activation(d, d, ACT.Exp).then_inc(S("dec_exp"), 1)
            act.wait_ge(S("egc_diff"), 2)
            for i in (0, 2):
                act.activation(egc[:, i, :], egc[:, i, :], ACT.Exp).then_inc(S("egc_exp"), 1)
            gdn(2)
            conv2_silu(4)
            conv2_silu(5)
            fsum_out(0)
            hi_until(G0 + 6)
            token_squares(0)
            token_squares(1)
            gdn(3)
            conv2_silu(6)
            conv2_silu(7)
            fsum_out(1)
            gdn(4)
            conv2_silu(8)
            conv2_silu(9)
            fsum_out(2)
            hi_until(G0 + 8)
            token_squares(2)
            token_squares(3)
            gdn(5)
            conv2_silu(10)
            conv2_silu(11)
            fsum_out(3)
            for j in range(3):
                fox_evac(j)
            hi_until(at["fox"][3] + 3)
            for h in range(GH):
                act.wait_ge(S("gT_mm"), h + 1)
                act.copy(gT[:, h].rearrange("p a t -> p (a t)"), ps[:, 4 + h, :]).then_inc(S("gT_ready"), 1)
            fox_evac(3)

            def bank_out(dst, bank, want, func=None):
                if func is None:
                    act.copy(dst, ps[:, bank, :]).then_inc(S(want), 1)
                else:
                    act.activation(dst, ps[:, bank, :], func).then_inc(S(want), 1)

            hi_until(at["fox_v"][0] + 4)
            act.wait_ge(group_used, at["fox_v"][0] + 2)
            for t in range(TT):
                bank_out(fox_v[:, t, :], t, "fox_v_out")
            hi_until(at["z"][0] + 4)
            act.wait_ge(group_used, at["z"][0] + 2)
            for t in range(TT):
                bank_out(zs[:, t, :], 6 + t, "z_out", ACT.Silu)
            act.wait_ge(S("q_expT_mm"), 1)
            bank_out(q_expT[:].rearrange("p h t -> p (h t)"), 0, "q_expT_ready")
            for t in range(TT):
                act.wait_ge(S("c_T"), t + 1)
                bank_out(c_mat[:, GH * t:GH * (t + 1), :].rearrange("p h t -> p (h t)"), 4 + t, "c_out")

            def fox_exp(h):
                act.wait_ge(S("fox_max"), h + 1)
                act.wait_ge(S("logit_masked"), 2 * h + 2)
                for t, part in ((0, slice(0, P)), (1, slice(P, 3 * P))):
                    row = logit[:, h % 2, part]
                    act.activation(row, row, ACT.Exp, bias=fsum[:, h % 2, t:t + 1],
                                   accum_out=fsum[:, h % 2, 2 + t:3 + t]).then_inc(S("prob2_ready"), 1)

            def prT_out(h):
                act.wait_ge(S("prT_mm"), h + 1)
                if h >= 2:
                    act.wait_ge(S("fox_mm"), h - 1)
                act.copy(prT[:, h % 2, :], ps[:, 2, 0:3 * P]).then_inc(S("prT_ready"), 1)

            for i in range(len(LEVELS)):
                for t in range(TT):
                    act.wait_ge(S("xs_mm"), TT * i + t + 1)
                    if i:
                        act.wait_ge(S("y_mm"), TT * (i - 1) + t + 1)
                    bank_out(xs[:, GH * t:GH * (t + 1), :].rearrange("p h t -> p (h t)"), 4 + t, "xs_ready")
                fox_exp(i)
                if i:
                    prT_out(i - 1)
            prT_out(len(LEVELS) - 1)
            fox_exp(len(LEVELS))
            fox_exp(len(LEVELS) + 1)
            act.wait_ge(S("u_mm"), 1)
            bank_out(u_tok[:, 0, :], 4, "u_out")
            act.wait_ge(S("u_mm"), 2)
            bank_out(u_tok[:, 1, :], 5, "u_out")
            act.wait_ge(S("w_mm"), 1)
            bank_out(wT, 6, "wT_ready")
            act.wait_ge(S("st_mm"), 1)
            bank_out(st1, 7, "st_ready")
            prT_out(len(LEVELS))
            prT_out(len(LEVELS) + 1)
            for t in range(TT):
                act.wait_ge(S("o_mm"), t + 1)
                for h in range(GH):
                    sum_sq(ps[:, t, h * GD:(h + 1) * GD], 40 + GH * t + h)
            hi_T("mix")
            hi_until(at["att_out"][1] + 4)
            if STOP == "E":
                return
            norm("norm4", 48, (11, 12))
            load(p_tok[:], I["p_2"][0, 0].rearrange("(t p) n -> p t n", p=P), "p_in")
            load(gp3[:], I["final_norm_w_2"].partition_broadcast(P), "gp3_in")
            hi_T("norm4")
            for j in range(PAIRS):
                g = at["gate_up"][2 * j]
                hi_until(g + 3)
                act.wait_ge(group_used, g + 1)
                if j >= 2:
                    act.wait_ge(S("act_full"), PAIRS + j - 1)
                act.activation(sil[:, j % 2], ps[:, 4 * (j % 2):4 * (j % 2) + 2, 0:T], ACT.Silu).then_inc(S("silu_ready"), 1)
                hi_until(g + 5)
                act.wait_ge(S("act_full"), PAIRS + j + 1)
                act.copy(act2_hi[:, 2 * j:2 * j + 2, :], actf2[:, j % 2]).then_inc(S("act_hi_ready"), 1)
            hi_until(at["down2"][1] + 6 + 2)
            act.wait_ge(S("pT_ready"), 1)
            act.copy(p_hi[:], pT[:]).then_inc(S("p_hi"), 1)
            hi_until(at["ple_p"][0] + 3)
            act.wait_ge(group_used, at["ple_p"][0] + 1)
            for n in range(2):
                for t in range(TT):
                    bank_out(pgate[:, t, n * NB:(n + 1) * NB], 2 * n + t, "p_out")
            norm("norm5", 50, (15, 16))
            hi_T("norm5")
            for n in range(2):
                hi_until(at["ple_g"][n] + 4)
                act.wait_ge(group_used, at["ple_g"][n] + 2)
                for t in range(TT):
                    i = TT * n + t
                    if i >= 2:
                        act.wait_ge(S("x_upd"), 16 + i - 1)
                    bank_out(tmp[:, i % 2, :], 4 + i, "sig_ready", ACT.Sigmoid)
            norm("final", 52, (19, 20))


        @block.vector
        def _(dve):
            link = chained(dve, "dve_chain")
            s_next = [0]

            def lo_until(n):
                while s_next[0] < min(n, n_split):
                    s = s_next[0]
                    dve.wait_ge(hi_ready, s + 1)
                    dve.tensor_tensor(part_view(w_lo, s), raw_view(split[s]), part_view(w_hi, s).bitcast(F32),
                                      ALU.subtract).then_inc(lo_ready, 1)
                    s_next[0] += 1

            def lo_part(lo, src, hi, want):
                dve.tensor_tensor(lo, src, hi.bitcast(F32), ALU.subtract).then_inc(S(want), 1)

            def transposed(name, scale=None, shift=None):
                def lo_pair(i):
                    dve.wait_ge(S("hi"), base("hi", name) + i + 1)
                    pair = slice(2 * i, 2 * i + 2)
                    lo_part(h_lo[:, pair, :], full[:, pair, :], h_hi[:, pair, :], "hT")

                for k in range(KD):
                    dve.wait_ge(S("tr"), base("tr", name) + k + 1)
                    src = ps[:, k % 4, 0:T]
                    a = scale(k) if scale else None
                    if a is None:
                        ins = dve.tensor_copy(full[:, k, :], src)
                    elif shift is None:
                        ins = dve.tensor_scalar(full[:, k, :], src, a, None, ALU.mult)
                    else:
                        ins = dve.tensor_scalar(full[:, k, :], src, a, shift(k), ALU.mult, ALU.add)
                    ins.then_inc(S("full"), 1)
                    if k >= 3 and k % 2:
                        lo_pair(k // 2 - 1)
                lo_pair(KD // 2 - 1)

            def diagonal(name, c0):
                dve.wait_ge(S("rstd"), base("rstd", name) + 1)
                for t in range(TT):
                    dve.tensor_scalar(diag[:, t, :], ident[:], rstd[:, c0 + t:c0 + t + 1], None, ALU.mult)\
                        .then_inc(S("diag"), 1)

            def post_residual(name, c0, gain):
                dve.wait_ge(S("rstd"), base("rstd", name) + 1)
                for t in range(TT):
                    for n in range(2):
                        c = slice(n * NB, (n + 1) * NB)
                        link(dve.scalar_tensor_tensor(tmp[:, n, :], ps[:, 4 + 2 * n + t, :], rstd[:, c0 + t:c0 + t + 1],
                                                      gain[:, c], ALU.mult, ALU.mult))
                        dve.tensor_tensor(x[:, t, c], x[:, t, c], tmp[:, n, :], ALU.add).then_inc(S("x_upd"), 1)

            def residual(name, nk=2):
                for n in range(2):
                    lo_until(at[name][n] + nk + 2)
                    dve.wait_ge(group_used, at[name][n] + nk)
                    c = slice(n * NB, (n + 1) * NB)
                    for t in range(TT):
                        dve.tensor_tensor(x[:, t, c], x[:, t, c], ps[:, 4 + 2 * n + t, :], ALU.add).then_inc(S("x_upd"), 1)

            def ada_vector(v):
                if v == 0:
                    dve.wait_ge(S("ada_b_in"), 64)
                for n in range(2):
                    a = ada_acc[v][:, n * NB:(n + 1) * NB]
                    for half in range(2):
                        i = 4 * v + 2 * n + half
                        raw_arrived(dve, ada2[i])
                        for k in range(4):
                            ins = dve.scalar_tensor_tensor(a, raw_view(ada2[i])[:, k, :], cpad[:, 4 * half + k, 0:1], a,
                                                           ALU.mult, ALU.add)
                            if k < 3:
                                link(ins)
                        ins.then_inc(ada2_used, 1)
                        dve.wait_ge(ada2_used, i + 1)

            dve.wait_ge(S("vec_T"), 3)
            dve.tensor_copy(cols[:], ps[:, 7, 0:n_col]).then_inc(S("cols_ready"), 1)
            dve.wait_ge(S("rstd"), base("rstd", "norm1") + 1)
            for t in range(2 * TT):
                dve.tensor_scalar(diag[:, t, :], ident[:], rstd[:, t:t + 1], None, ALU.mult).then_inc(S("diag1"), 1)
            for n in range(2):
                dve.wait_ge(ada1_used, 2 * n + 2)
                dve.tensor_copy(ada_rows[:, n, :], ps[:, n, :]).then_inc(S("ada_rows_dve"), 1)
            dve.wait_ge(S("ada_T"), 1)
            link(dve.tensor_tensor(mod[:], ps[:, 4, 0:4 * KD].rearrange("p (j c) -> p j c", c=2),
                                   cols[:, col["ada_b"]:col["ada_b"] + 2 * KD].unsqueeze(2).to_broadcast([P, 2 * KD, 2]),
                                   ALU.add))
            gain = cols[:, col["pre_mix"]:col["pre_mix"] + KD].unsqueeze(2).to_broadcast([P, KD, 2])
            link(dve.scalar_tensor_tensor(mod[:, KD:], mod[:, KD:], 1.0, gain, ALU.add, ALU.mult))

            def lo_first(i):
                dve.wait_ge(S("h1_hi"), 2 * i + 2)
                pair = slice(2 * i, 2 * i + 2)
                link(dve.tensor_tensor(h_lo[:, pair, :], full[:, pair, :], h_hi[:, pair, :].bitcast(F32), ALU.subtract))
                lo_part(c_lo[:, pair, :], cfull[:, pair, :], c_hi[:, pair, :], "hT1")

            for k in range(KD):
                dve.wait_ge(S("tr1"), k + 1)
                for i, dst in ((0, full), (1, cfull)):
                    ins = dve.tensor_scalar(dst[:, k, :], ps[:, 5 + k % 3, i * T:(i + 1) * T], mod[:, KD + k, i:i + 1],
                                            mod[:, k, i:i + 1], ALU.mult, ALU.add)
                    if i == 0:
                        link(ins)
                ins.then_inc(S("full1"), 1)
                if k >= 3 and k % 2:
                    lo_first(k // 2 - 1)
            lo_first(KD // 2 - 1)
            lo_until(2)

            dve.wait_ge(S("gate_mm"), 1)
            dve.wait_ge(S("wg_in"), 32)
            link(dve.tensor_tensor(gate[:], ps[:, 4, 0:2 * TT * 16].rearrange("p (t g) -> p t g", t=2 * TT),
                                   bg[:].unsqueeze(1).to_broadcast([P, 2 * TT, 16]), ALU.add))
            dve.scalar_tensor_tensor(sp1[:], gate_v[:, :, 1, :], -1.0, gate_v[:, :, 1, :], ALU.mult, ALU.max).then_inc(S("gate_abs"), 1)
            lo_until(3)
            dve.wait_ge(S("gate_ln"), 1)
            dve.scalar_tensor_tensor(lf[:], gate_v[:, :, 1, :], 0.0, sp1[:], ALU.min, ALU.subtract).then_inc(S("lf_ready"), 1)
            lo_until(4)
            ada_vector(0)

            def bias_of(i):
                dve.wait_ge(S(f"bias_in{i % 2}"), 16 * (i // 2 + 1))
                return bias[:, i % 2, :]

            dve.wait_ge(group_used, at["k"][0] + 2)
            for i, dst in enumerate((qk_tok[:, 1, 0, :], qk_tok[:, 1, 1, :], k_ctx[:, 0, :], k_ctx[:, 1, :])):
                dve.tensor_tensor(dst, ps[:, i, :], bias_of(0), ALU.add).then_inc(S("k_done"), 1)
            lo_until(5)
            dve.wait_ge(S("cum_mm"), 1)
            n_td = TT * 2
            link(dve.tensor_copy(b_col[:], ps[:, 4, 0:16].rearrange("p (a h) -> p a h", h=MH)))
            dve.tensor_tensor(u_col[:], gate_v[:, 0:n_td, 0, :], b_col[:], ALU.subtract).then_inc(S("u_ready"), 1)
            dve.tensor_tensor(gs_col[:], ps[:, 4, 16:32].rearrange("p (a h) -> p a h", h=MH), gate_v[:, n_td:, 0, :],
                              ALU.add).then_inc(S("u_ready"), 1)
            dve.tensor_copy(b_ctx[:], ps[0:MH, 4, 32:34]).then_inc(S("u_ready"), 1)
            dve.wait_ge(group_used, at["q"][0] + 2)
            for t in range(TT):
                dve.tensor_tensor(qk_tok[:, 0, t, :], ps[:, 5 + t, :], bias_of(1), ALU.add).then_inc(S("q_done"), 1)
            dve.wait_ge(S("u_rows"), 1)
            link(dve.tensor_copy(u_row, ps[0:MH, 7, :].rearrange("p (d t) -> p d t", d=2)))
            link(dve.tensor_reduce(m_ctx[:, 0:2], ps[0:MH, 4, :].rearrange("p (d t) -> p d t", d=2), AX_X, ALU.max))
            link(dve.tensor_tensor(m_ctx[:, 0:2], m_ctx[:, 0:2], b_ctx[:], ALU.max))
            link(dve.tensor_scalar(m_ctx[:, 2:4], m_ctx[:, 0:2], -1.0, None, ALU.mult))
            dve.tensor_tensor_scan(m_row[:, 0, :], u_row[:, 0, :], u_row[:, 0, :], m_ctx[:, 0:1], ALU.max, ALU.max)\
                .then_inc(S("mrow_ready"), 1)
            dve.tensor_tensor_scan(m_row[:, 1, ::-1], u_row[:, 1, ::-1], u_row[:, 1, ::-1], m_ctx[:, 1:2], ALU.max, ALU.max)\
                .then_inc(S("mrow_ready"), 1)
            for h in range(MH):
                dve.wait_ge(S("qk_T"), h + 1)
                dve.tensor_scalar(qkT[:, h, 0, :], ps[:, h, 0:T], DK ** -0.5, None, ALU.mult).then_inc(S("qkT_ready"), 1)
                dve.tensor_copy(qkT[:, h, 1, :], ps[:, h, T:2 * T]).then_inc(S("qkT_ready"), 1)
            lo_until(6)
            dve.wait_ge(S("m_cols"), 1)
            dve.tensor_tensor(emt[:], ps[:, 7, 0:16].rearrange("p (a h) -> p a h", h=MH), b_col[:], ALU.add)\
                .then_inc(S("mt_ready"), 1)
            dve.tensor_copy(ws_col[:], ps[:, 7, 16:32].rearrange("p (a h) -> p a h", h=MH)).then_inc(S("ws_out"), 1)
            link(dve.memset(vaug[:, :, :, DV:DV + 1], 1.0))

            def exponents(h):
                for d in range(2):
                    dve.wait_ge(S("m_bcast"), 2 * h + d + 1)
                    pr = prob[:, h, d, :]
                    one = slice(P, T) if d == 0 else slice(0, P)
                    for part, tt, tok in ((slice(0, T), d, slice(0, T)), (slice(T, 3 * P), 1 - d, one)):
                        dve.tensor_scalar(pr[:, part], ps[:, 5 + d, tok], u_col[:, 2 * tt + d, h:h + 1], 0.0,
                                          ALU.subtract, ALU.max).then_inc(S("z_ready"), 1)
                    dve.tensor_tensor(qTw[:, h, d, :], qkT[:, h, 0, :], ps[:, 5 + d, T:2 * T], ALU.mult)\
                        .then_inc(S("qTw_ready"), 1)

            def weigh_scores(h):
                dve.wait_ge(S("score_mm"), h + 1)
                for d in range(2):
                    dve.wait_ge(S("decay_ready"), 2 * h + d + 1)
                    pr = prob[:, h, d, :]
                    link(dve.tensor_tensor(pr[:, 0:T], pr[:, 0:T], ps[:, 4, d * T:(d + 1) * T], ALU.mult))
                    one = (1 - d) * T + (1 - d) * P
                    dve.tensor_tensor(pr[:, T:], pr[:, T:], ps[:, 4, one:one + P], ALU.mult).then_inc(S("prob_full"), 1)

            def v_evac(n):
                dve.wait_ge(group_used, at["v"][n] + 2)
                for i in range(2 * TT):
                    dve.tensor_tensor(vaug[:, i, 2 * n:2 * n + 2, 0:DV], ps[:, i, :].rearrange("p (h e) -> p h e", h=2),
                                      bias_of(2 + n).rearrange("p (h e) -> p h e", h=2), ALU.add).then_inc(S("v_done"), 1)

            exponents(0)
            ada_vector(1)
            lo_until(7)
            weigh_scores(0)
            exponents(1)
            lo_until(8)
            v_evac(0)
            weigh_scores(1)
            exponents(2)
            ada_vector(2)
            lo_until(9)
            weigh_scores(2)
            lo_until(10)
            exponents(3)
            ada_vector(3)
            lo_until(11)
            weigh_scores(3)
            v_evac(1)
            if STOP == "A":
                return

            def state_evac(h):
                for d in range(2):
                    dve.wait_ge(S("state_mm"), 2 * h + d + 1)
                    dve.tensor_copy(state[:, h, d, :], ps[:, 4 + 2 * (h % 2) + d, 0:DV + 1]).then_inc(S("state_out"), 1)

            def o_evac(n):
                dve.wait_ge(group_used, at["o"][n] + 2)
                for t in range(TT):
                    dve.tensor_tensor(so[:, t, n * NB:(n + 1) * NB], ps[:, 2 * n + t, :], bias_of(4 + n), ALU.add)\
                        .then_inc(S("o_done"), 1)

            def head_out(h):
                if h == 0:
                    dve.wait_ge(S("emt_ready"), 1)
                dve.wait_ge(S("out_mm"), h + 1)
                num_den = ps[:, 4:8, DV].rearrange("p (d t) -> p d t", d=2)
                by_d = den[:, 0, :].rearrange("p (d t) -> p d t", d=2)
                floor = emt[:].rearrange("p (t d) h -> p d t h", d=2)[:, :, :, h]
                link(dve.scalar_tensor_tensor(by_d, num_den, -1.0, floor, ALU.mult, ALU.max))
                link(dve.tensor_tensor(by_d, by_d, num_den, ALU.max))
                link(dve.reciprocal(den[:, 1, :], den[:, 0, :]))
                for t in range(TT):
                    hs = hsum[:, t, h * DV:(h + 1) * DV]
                    link(dve.tensor_scalar(hs, ps[:, 4 + t, 0:DV], den[:, 1, t:t + 1], None, ALU.mult))
                    dve.scalar_tensor_tensor(hs, ps[:, 6 + t, 0:DV], den[:, 1, TT + t:TT + t + 1], hs, ALU.mult, ALU.add)\
                        .then_inc(S("h_sum"), 1)

            def times_gate(bank, gp):
                for n in range(2):
                    c = slice(n * NB, (n + 1) * NB)
                    dve.tensor_tensor(gp[:, c], gp[:, c], ps[:, bank + n, :], ALU.mult).then_inc(S("mods_out"), 1)

            state_evac(0)
            state_evac(1)
            lo_until(12)
            state_evac(2)
            state_evac(3)
            o_evac(0)
            lo_until(13)
            head_out(0)
            lo_until(14)
            head_out(1)
            o_evac(1)
            lo_until(15)
            dve.wait_ge(S("gp_in"), 32)
            dve.wait_ge(S("ada_sum"), 1)
            times_gate(0, gp1)
            dve.wait_ge(S("ada_sum"), 2)
            link(dve.tensor_copy(mod2[:, 0:KD], ps[:, 2, 0:KD]))
            dve.scalar_tensor_tensor(mod2[:, KD:], ps[:, 2, KD:2 * KD], 1.0, cols[:, col["pre_ffn"]:col["pre_ffn"] + KD],
                                     ALU.add, ALU.mult).then_inc(S("mods_out"), 1)
            head_out(2)
            dve.wait_ge(S("ada_sum"), 3)
            times_gate(0, gp2)
            head_out(3)
            dve.wait_ge(S("so_ready"), 4)
            for h in range(MH):
                dve.wait_ge(S("rstd"), base("rstd", "head") + h + 1)
                for t in range(TT):
                    c = slice(h * DV, (h + 1) * DV)
                    r = 4 + TT * h + t
                    dve.scalar_tensor_tensor(ymix[:, t, c], hsum[:, t, c], rstd[:, r:r + 1], so[:, t, c], ALU.mult, ALU.mult)\
                        .then_inc(S("y1_ready"), 1)
            transposed("y1", lambda k: pcol("m_norm", k))
            lo_until(at["mix_out"][1] + 4)
            post_residual("post1", 12, gp1)
            if STOP == "B":
                return
            diagonal("norm2", 16)
            transposed("norm2", lambda k: mod2[:, KD + k:KD + k + 1], lambda k: mod2[:, k:k + 1])

            for j in range(PAIRS):
                g = at["up"][2 * j]
                lo_until(g + 3)
                for f in range(2):
                    k = 2 * j + f
                    dve.wait_ge(S("conv_mid"), k + 1)
                    rows = cv[:, j % 2, f, :].rearrange("p (r w) -> p r w", w=GRID_W)
                    src = ps[:, 4 * (j % 2) + f, 0:T].rearrange("p (r w) -> p r w", w=GRID_W)
                    link(dve.scalar_tensor_tensor(rows[:, :, 1:], src[:, :, :-1], pcol("conv_w", k), rows[:, :, 1:],
                                                  ALU.mult, ALU.add))
                    dve.scalar_tensor_tensor(rows[:, :, :-1], src[:, :, 1:], pcol("conv_w", 2 * KF + k), rows[:, :, :-1],
                                             ALU.mult, ALU.add).then_inc(S("conv_done"), 1)
                lo_until(g + 4)
                dve.wait_ge(S("silu_ready"), j + 1)
                dve.wait_ge(group_used, g + 2)
                dve.tensor_tensor(actf[:, j % 2], cv[:, j % 2], ps[:, 4 * (j % 2) + 2:4 * (j % 2) + 4, 0:T], ALU.mult)\
                    .then_inc(S("act_full"), 1)
                lo_until(g + 5)
                dve.wait_ge(S("act_hi_ready"), j + 1)
                pair = slice(2 * j, 2 * j + 2)
                lo_part(act_lo[:, pair, :], actf[:, j % 2], act_hi[:, pair, :], "act_lo")
            lo_until(at["down"][1] + 6 + 2)
            post_residual("post2", 18, gp2)
            if STOP == "D":
                return

            diagonal("norm3", 22)
            transposed("norm3", lambda k: pcol("attn_norm", k))
            G0 = at["gdn"][0]
            lo_until(G0 + 3)
            dve.wait_ge(S("sgate_mm"), 1)
            pre = ps[:, 4, 0:TT * 16].rearrange("p (t g) -> p t g", t=TT)
            for c in (slice(0, GH), slice(2 * GH, 16)):
                link(dve.tensor_tensor(sm[:, :, c], pre[:, :, c],
                                       gprm[:, c].unsqueeze(1).to_broadcast([P, TT, c.stop - c.start]), ALU.add))
                link(dve.scalar_tensor_tensor(sp2[:, :, c], sm[:, :, c], -1.0, sm[:, :, c], ALU.mult, ALU.max))
            dve.tensor_copy(sp2[:, :, GH:2 * GH], pre[:, :, GH:2 * GH]).then_inc(S("gate_abs"), 1)
            dve.wait_ge(S("gate_exp"), 3)
            link(dve.tensor_scalar(beta[:], sp2[:, :, GH:2 * GH], 1.0, None, ALU.add))
            dve.reciprocal(beta[:], beta[:]).then_inc(S("beta_ready"), 1)
            dve.wait_ge(S("gate_ln"), 2)
            link(dve.scalar_tensor_tensor(g_dec[:], sm[:, :, 0:GH], 0.0, sp2[:, :, 0:GH], ALU.max, ALU.add))
            dve.scalar_tensor_tensor(g_dec[:], g_dec[:], -1.0, gprm[:, GH:2 * GH].unsqueeze(1).to_broadcast([P, TT, GH]),
                                     ALU.mult, ALU.mult).then_inc(S("sgate_ready"), 1)
            dve.scalar_tensor_tensor(lf2[:], sm[:, :, 2 * GH:], 0.0, sp2[:, :, 2 * GH:], ALU.min, ALU.subtract)\
                .then_inc(S("sgate_ready"), 1)

            def gdn(j):
                lo_until(G0 + j + 3)
                for f in (2 * j, 2 * j + 1):
                    dve.wait_ge(S("conv2_mid"), f + 1)
                    for back in (1, 2, 3):
                        ins = dve.scalar_tensor_tensor(r5[:, f, back:], ps[:, f % 4, 0:T - back],
                                                       pcol("conv2", 12 * (3 - back) + f), r5[:, f, back:], ALU.mult, ALU.add)
                        if back < 3:
                            link(ins)
                    ins.then_inc(S("conv2_done"), 1)

            def heads(a):
                return a.rearrange("p (h n) -> p h n", h=GH)

            def per_head(a):
                return a.unsqueeze(2).to_broadcast([P, GH, GD])

            def token_norm(i):
                a, t = i // 2, i % 2
                c = 24 + GH * i
                dve.wait_ge(S("sq_ready"), i + 1)
                dve.tensor_reduce(ss[:, c:c + GH], heads(sq[:, i % 2, :]), AX_X, ALU.add).then_inc(S("ss_l2"), 1)
                dve.wait_ge(S("rstd_l2"), i + 1)
                dve.tensor_tensor(heads(qk_n[:, a, t, :]), heads(ps[:, (4, 5, 6, 4)[i], :]), per_head(rstd[:, c:c + GH]),
                                  ALU.mult).then_inc(S("tok_out"), 1)

            gdn(0)
            gdn(1)
            dve.wait_ge(S("gc_mm"), 1)
            link(dve.tensor_copy(gc[:], ps[:, 4, 0:3 * GH].rearrange("p (a h) -> p a h", h=GH)))
            dve.tensor_copy(egc[:, 0, :], gc[:, 1, :]).then_inc(S("egc_diff"), 1)
            dve.tensor_tensor(egc[:, 2, :], gc[:, 2, :], gc[:, 0, :], ALU.subtract).then_inc(S("egc_diff"), 1)
            for t in range(TT):
                dve.wait_ge(S("gcb_mm"), t + 1)
                for h in range(GH):
                    ins = dve.tensor_scalar(decT[:, GH * t + h, :], ps[:, 5 + t, h * P:(h + 1) * P], gc[:, t, h:h + 1], 0.0,
                                            ALU.subtract, ALU.min)
                    if h < GH - 1:
                        link(ins)
                ins.then_inc(S("dec_z"), 1)
            dve.wait_ge(S("egc_exp"), 2)
            dve.tensor_tensor(egc[:, 1, :], egc[:, 0, :], beta[:, 1, :], ALU.mult).then_inc(S("egc_ready"), 1)
            gdn(2)
            lo_until(G0 + 6)
            token_norm(0)
            token_norm(1)
            gdn(3)
            gdn(4)
            lo_until(G0 + 8)
            token_norm(2)
            token_norm(3)
            gdn(5)
            F0 = at["fox"][0]
            lo_until(F0 + 3)
            for t in range(TT):
                dve.wait_ge(S("tok_T"), 4 + t + 1)
                dve.tensor_tensor(heads(vb[:, t, :]), heads(ps[:, 5 + t, :]), per_head(beta[:, t, :]), ALU.mult)\
                    .then_inc(S("tok_out"), 1)
            lo_until(F0 + 7)

            def all_heads(a, t):
                return a[:, GH * t:GH * (t + 1), :]

            def bank(b):
                return heads(ps[:, b, :])

            dve.wait_ge(S("dec_ready"), TT)
            for t in range(TT):
                dve.wait_ge(S("kk_mm"), t + 1)
                link(dve.tensor_tensor(all_heads(cT, t), bank(4 + t), all_heads(decT, t), ALU.mult))
            for t in range(TT):
                dve.wait_ge(S("kk_mm"), TT + t + 1)
                dve.tensor_tensor(all_heads(qkT2, t), bank(6 + t), all_heads(decT, t), ALU.mult)\
                    .then_inc(S("qkT2_ready"), 1)
            lo_until(at["fox_v"][0] + 4)
            for t in range(TT):
                dve.wait_ge(S("beta_mm"), t + 1)
                dve.tensor_tensor(all_heads(cT, t), all_heads(cT, t), bank(2 + t), ALU.mult).then_inc(S("cT_full"), 1)
            lo_until(at["z"][0] + 4)

            def fox_logits(h):
                dve.wait_ge(S("logit_mm"), h + 1)
                if h >= 2:
                    dve.wait_ge(S("prT_mm"), h - 1)
                for t, part in ((0, slice(0, P)), (1, slice(P, 3 * P))):
                    dve.scalar_tensor_tensor(logit[:, h % 2, part], ps[:, h % 2, part], FD ** -0.5,
                                             neg_c[:, h, 0:(t + 1) * P], ALU.mult, ALU.add).then_inc(S("logit_ready"), 1)

            def fox_max(h):
                dve.wait_ge(S("logit_masked"), 2 * h + 2)
                for t, part in ((0, slice(0, P)), (1, slice(P, 3 * P))):
                    link(dve.tensor_reduce(fsum[:, h % 2, t:t + 1], logit[:, h % 2, part], AX_X, ALU.max))
                dve.tensor_scalar(fsum[:, h % 2, 0:2], fsum[:, h % 2, 0:2], -1.0, None, ALU.mult).then_inc(S("fox_max"), 1)

            def fox_done(h):
                dve.wait_ge(S("fox_mm"), h + 1)
                link(dve.reciprocal(fsum[:, h % 2, 2:4], fsum[:, h % 2, 2:4]))
                for t in range(TT):
                    c = GH * GD + FD * h
                    dve.tensor_scalar(mix[:, t, c:c + FD], ps[:, 3, t * FD:(t + 1) * FD], fsum[:, h % 2, 2 + t:3 + t], None,
                                      ALU.mult).then_inc(S("fox_done"), 1)

            dve.wait_ge(S("level_ready"), 1)
            dve.wait_ge(S("cT_ready"), 1)
            for t in range(TT):
                dve.wait_ge(S("c_out"), t + 1)
                for dst, src in ((inv, c_mat), (invT, cT)):
                    d = all_heads(dst, t)
                    link(dve.tensor_tensor(d, all_heads(src, t), level[:, 0, :].unsqueeze(1).to_broadcast([P, GH, P]), ALU.mult))
                    ins = dve.tensor_tensor(d, ident[:].unsqueeze(1).to_broadcast([P, GH, P]), d, ALU.subtract)
                    if dst is inv:
                        link(ins)
                ins.then_inc(S("inv_ready"), 1)
            fox_logits(0)
            for i in range(len(LEVELS)):
                fox_max(i)
                fox_logits(i + 1)
                if i == 1:
                    dve.wait_ge(S("q_exp_ready"), 1)
                    dve.wait_ge(S("k_beta_ready"), 1)
                    dve.wait_ge(S("k_dec_ready"), 1)
                    dve.wait_ge(S("gT_mm"), GH)
                if i:
                    fox_done(i - 1)
                for t in range(TT):
                    dve.wait_ge(S("y_mm"), TT * i + t + 1)
                    if i < len(LEVELS) - 1:
                        link(dve.tensor_tensor(all_heads(inv, t), all_heads(inv, t), bank(6 + t), ALU.subtract))
                    dve.tensor_tensor(all_heads(invT, t), all_heads(invT, t), bank(4 + t), ALU.subtract)\
                        .then_inc(S("inv_ready"), 1)
            h = len(LEVELS)
            fox_max(h)
            fox_logits(h + 1)
            fox_done(h - 1)
            fox_max(h + 1)
            fox_done(h)
            fox_done(h + 1)
            dve.wait_ge(S("u_out"), 2)
            dve.wait_ge(S("ws_mm"), 1)
            dve.tensor_tensor(v_new, u_tok[:, 1, :], ps[:, 6, :], ALU.subtract).then_inc(S("v_new_ready"), 1)
            dve.wait_ge(S("z_out"), TT)
            for t in range(TT):
                dve.wait_ge(S("rstd"), base("rstd", "gdn") + t + 1)
                c = 40 + GH * t
                link(dve.tensor_tensor(heads(og[:, t, :]), bank(t), per_head(rstd[:, c:c + GH]), ALU.mult))
                dve.tensor_tensor(mix[:, t, 0:GH * GD], og[:, t, :], zs[:, t, :], ALU.mult).then_inc(S("mix_ready"), 1)
            transposed("mix", lambda k: pcol("gdn_norm", 0) if k < GH else None)
            residual("att_out")
            if STOP == "E":
                return
            diagonal("norm4", 48)
            transposed("norm4", lambda k: pcol("ffn_norm", k))
            for j in range(PAIRS):
                g = at["gate_up"][2 * j]
                lo_until(g + 4)
                dve.wait_ge(S("silu_ready"), PAIRS + j + 1)
                dve.wait_ge(group_used, g + 2)
                dve.tensor_tensor(actf2[:, j % 2], sil[:, j % 2], ps[:, 4 * (j % 2) + 2:4 * (j % 2) + 4, 0:T], ALU.mult)\
                    .then_inc(S("act_full"), 1)
                lo_until(g + 5)
                dve.wait_ge(S("act_hi_ready"), PAIRS + j + 1)
                pair = slice(2 * j, 2 * j + 2)
                lo_part(act2_lo[:, pair, :], actf2[:, j % 2], act2_hi[:, pair, :], "act_lo")
            residual("down2", 6)
            dve.wait_ge(S("p_T"), 1)
            dve.tensor_copy(pT[:].rearrange("p k t -> p (k t)"), ps[:, 0, :]).then_inc(S("pT_ready"), 1)
            dve.wait_ge(S("p_hi"), 1)
            lo_part(p_lo[:], pT[:], p_hi[:], "p_lo")
            lo_until(at["ple_p"][0] + 3)
            diagonal("norm5", 50)
            transposed("norm5", lambda k: pcol("ple_norm", k))
            lo_until(n_split)
            dve.wait_ge(S("p_out"), 4)
            for n in range(2):
                for t in range(TT):
                    i = TT * n + t
                    c = slice(n * NB, (n + 1) * NB)
                    dve.wait_ge(S("sig_ready"), i + 1)
                    link(dve.tensor_tensor(pgate[:, t, c], pgate[:, t, c], tmp[:, i % 2, :], ALU.mult))
                    dve.tensor_tensor(x[:, t, c], x[:, t, c], pgate[:, t, c], ALU.add).then_inc(S("x_upd"), 1)
            dve.wait_ge(S("rstd"), base("rstd", "final") + 1)
            dve.wait_ge(S("gp3_in"), 16)
            for t in range(TT):
                dve.scalar_tensor_tensor(pgate[:, t, :], x[:, t, :], rstd[:, 52 + t:53 + t], gp3[:], ALU.mult, ALU.mult)\
                    .then_inc(S("result"), 1)

        @block.tensor
        def _(pe):
            def mm3(dst, left, right, first, last):
                (l_hi, l_lo), (r_hi, r_lo) = left, right
                pe.matmul(dst, l_hi, r_hi, start=first, stop=False)
                pe.matmul(dst, l_hi, r_lo, start=False, stop=False)
                return pe.matmul(dst, l_lo, r_hi, start=False, stop=last)

            def weights(s):
                pe.wait_ge(lo_ready, s + 1)
                return part_view(w_hi, s), part_view(w_lo, s)

            def token_block(s0, sources, nk=KD, before=None, arrived=None):
                for s in range(s0, s0 + (nk + 3) // 4):
                    hi, lo = weights(s)
                    k0 = 4 * (s - s0)
                    if arrived is not None:
                        arrived(k0, min(k0 + 4, nk))
                    for a_hi, a_lo, t, bank in sources:
                        for k in range(k0, min(k0 + 4, nk)):
                            tok = slice(t * P, (t + 1) * P)
                            ins = mm3(ps[:, bank, :], (a_hi[:, k, tok], a_lo[:, k, tok]),
                                      (hi[:, k - k0, :], lo[:, k - k0, :]), k == 0, k == nk - 1)
                    ins.then_inc(group_used, 1)
                    if before is not None and s == s0:
                        before()

            def feature_tiles(s, banks):
                hi, lo = weights(s)
                for f, bank in enumerate(banks):
                    fs_ = slice(f * P, (f + 1) * P)
                    for k in range(KD):
                        ins = mm3(ps[:, bank, 0:T], (hi[:, k, fs_], lo[:, k, fs_]), (h_hi[:, k, :], h_lo[:, k, :]),
                                  k == 0, k == KD - 1)
                ins.then_inc(group_used, 1)

            def transposed(name, src, by_diag):
                for k in range(KD):
                    if k >= 4:
                        pe.wait_ge(S("full"), base("full", name) + k - 3)
                    for t in range(TT):
                        if by_diag and k == 0:
                            pe.wait_ge(S("diag"), base("diag", name) + t + 1)
                        dst = ps[:, k % 4, t * P:(t + 1) * P]
                        if by_diag:
                            ins = pe.matmul(dst, src[:, t, k * P:(k + 1) * P], diag[:, t, :], start=True, stop=True)
                        else:
                            ins = pe.transpose(dst, src[:, t, k * P:(k + 1) * P], ident[:])
                    ins.then_inc(S("tr"), 1)

            def hT(name):
                return lambda k0, k1: pe.wait_ge(S("hT"), base("hT", name) + k1 // 2)

            def flip(dst, src):
                n = src.shape[0]
                return pe.transpose(dst, src, ident[0:n, 0:n])

            X0, X1 = (h_hi, h_lo, 0), (h_hi, h_lo, 1)
            C0, C1 = (c_hi, c_lo, 0), (c_hi, c_lo, 1)

            pe.wait_ge(S("const_ready"), 1)
            pe.wait_ge(S("vec_in"), 16 * (len(VEC) + 3))
            at_col = 0
            for rows in vec_rows:
                n = rows.shape[0]
                flip(ps[:, 7, at_col:at_col + n], rows).then_inc(S("vec_T"), 1)
                at_col += n

            pe.wait_ge(S("c_ready"), 1)
            for i, g in enumerate(ada1):
                raw_arrived(pe, g)
                n, half = i // 2, i % 2
                for kk in range(4):
                    ins = pe.matmul(ps[32 * kk:32 * kk + 32, n, :], cpad[:, 4 * half + kk, :], raw_view(g)[:, kk, :],
                                    start=half == 0, stop=half == 1)
                ins.then_inc(ada1_used, 1)
            pe.wait_ge(S("ada_rows_dve"), 2)
            pe.wait_ge(S("ada_rows_act"), 2)
            for j in range(2 * KD):
                ins = pe.matmul(ps[:, 4, 2 * j:2 * j + 2], ada_rows[:, j // 4, (j % 4) * P:(j % 4 + 1) * P], row_of[:],
                                start=True, stop=True)
            ins.then_inc(S("ada_T"), 1)

            pe.wait_ge(S("diag1"), 4)
            pe.wait_ge(S("cols_ready"), 1)
            for k in range(KD):
                if k >= 3:
                    pe.wait_ge(S("full1"), k - 2)
                for t in range(2 * TT):
                    src = x[:, t, :] if t < TT else ctx_tok[:, t - TT, :]
                    ins = pe.matmul(ps[:, 5 + k % 3, t * P:(t + 1) * P], src[:, k * P:(k + 1) * P], diag[:, t, :],
                                    start=True, stop=True)
                ins.then_inc(S("tr1"), 1)

            pe.wait_ge(S("full1"), KD)
            pe.wait_ge(S("wg_in"), 32)
            for t in range(2 * TT):
                src = full if t < TT else cfull
                for k in range(KD):
                    ins = pe.matmul(ps[:, 4, 16 * t:16 * t + 16], src[:, k, (t % TT) * P:(t % TT + 1) * P], wg[:, k, :],
                                    start=k == 0, stop=k == KD - 1)
            ins.then_inc(S("gate_mm"), 1)

            def hT1(k0, k1):
                pe.wait_ge(S("hT1"), k1 // 2)

            token_block(at["k"][0], [(*X0, 0), (*X1, 1), (*C0, 2), (*C1, 3)], arrived=hT1)

            pe.wait_ge(S("lf_ready"), 1)

            def lf_of(tile, d):
                return lf[:, 2 * tile + d, :]

            for a in range(2):
                for t in range(TT):
                    for d in range(2):
                        dst = ps[:, 4, 16 * a + 8 * t + 4 * d:16 * a + 8 * t + 4 * d + 4]
                        tri = ((s_le_t, s_ge_t), (s_gt_t, s_lt_t))[a][d]
                        other = t != (a + d) % 2
                        pe.matmul(dst, tri[:], lf_of(TT * a + t, d), start=True, stop=not other)
                        if other:
                            pe.matmul(dst, ones[:], lf_of(TT * a + 1 - t, d), start=False, stop=True)
            for d in range(2):
                for t in range(TT):
                    ins = pe.matmul(ps[0:MH, 4, 32 + d:33 + d], lf_of(TT + t, d), ones[:, 0:1], start=t == 0, stop=t == 1)
            ins.then_inc(S("cum_mm"), 1)

            token_block(at["q"][0], [(*X0, 5), (*X1, 6)])

            pe.wait_ge(S("u_ready"), 3)
            for bank, src in ((7, u_col), (4, gs_col)):
                for t in range(TT):
                    for d in range(2):
                        ins = flip(ps[0:MH, bank, d * T + t * P:d * T + (t + 1) * P], src[:, 2 * t + d, :])
            ins.then_inc(S("u_rows"), 1)

            pe.wait_ge(S("k_done"), 4)
            pe.wait_ge(S("q_done"), 2)
            for h in range(MH):
                for a in range(2):
                    for t in range(TT):
                        ins = flip(ps[:, h, a * T + t * P:a * T + (t + 1) * P], qk_tok[:, a, t, h * DK:(h + 1) * DK])
                ins.then_inc(S("qk_T"), 1)

            def maxima_in_columns():
                pe.wait_ge(S("mrow_ready"), 2)
                pe.wait_ge(S("ws_row"), 2)
                for i, src in enumerate((m_row, ws_row)):
                    for t in range(TT):
                        for d in range(2):
                            c = 16 * i + 8 * t + 4 * d
                            ins = flip(ps[:, 7, c:c + 4], src[:, d, t * P:(t + 1) * P])
                ins.then_inc(S("m_cols"), 1)

            def scores(h):
                pe.wait_ge(S("w_row"), 2)
                pe.wait_ge(S("qkT_ready"), 2 * h + 2)
                if h:
                    pe.wait_ge(S("prob_full"), 2 * h)
                for t in range(TT):
                    ins = pe.matmul(ps[:, 4, t * T:(t + 1) * T], qkT[:, h, 1, t * P:(t + 1) * P], qkT[:, h, 0, :],
                                    start=True, stop=True)
                ins.then_inc(S("score_mm"), 1)
                for d in range(2):
                    if h:
                        pe.wait_ge(S("qTw_ready"), 2 * (h - 1) + d + 1)
                    pe.matmul(ps[:, 5 + d, 0:T], sel[:, h, :], m_row[:, d, :], start=True, stop=True)
                    pe.matmul(ps[:, 5 + d, T:2 * T], sel[:, h, :], w_row[:, d, :], start=True, stop=True)\
                        .then_inc(S("m_bcast"), 1)

            vtiles = [(*X0, 0), (*X1, 1), (*C0, 2), (*C1, 3)]
            pe.wait_ge(S("qkT_ready"), 2 * MH)
            token_block(at["v"][0], vtiles, before=lambda: (maxima_in_columns(), scores(0)))
            scores(1)
            pe.wait_ge(S("v_done"), 4)
            token_block(at["v"][1], vtiles, before=lambda: scores(2))
            scores(3)
            if STOP == "A":
                return

            def ctx_state(h):
                pe.wait_ge(S("kw_ready"), h + 1)
                pe.wait_ge(S("v_done"), 8)
                if h >= 2:
                    pe.wait_ge(S("state_out"), 2 * (h - 1))
                for d in range(2):
                    for t in range(TT):
                        ins = pe.matmul(ps[:, 4 + 2 * (h % 2) + d, 0:DV + 1], kw[:, h % 2, t, d, :], vaug[:, TT + t, h, :],
                                        start=t == 0, stop=t == 1)
                    ins.then_inc(S("state_mm"), 1)

            def outputs(h):
                pe.wait_ge(S("prob_ready"), 2 * h + 2)
                pe.wait_ge(S("state_out"), 2 * MH)
                if h:
                    pe.wait_ge(S("h_sum"), 2 * h)
                for d in range(2):
                    pr = prob[:, h, d, :]
                    for t in range(TT):
                        dst = ps[:, 4 + 2 * d + t, 0:DV + 1]
                        pe.matmul(dst, qTw[:, h, d, t * P:(t + 1) * P], state[:, h, d, :], start=True, stop=False)
                        if t != d:
                            pe.matmul(dst, pr[:, T:T + P], vaug[:, 1 - d, h, :], start=False, stop=False)
                        ins = pe.matmul(dst, pr[:, t * P:(t + 1) * P], vaug[:, d, h, :], start=False, stop=True)
                ins.then_inc(S("out_mm"), 1)

            def gate_vector(v, bank):
                for n in range(2):
                    ins = pe.matmul(ps[:, bank + n, :], ones[:], ada_acc[v][:, n * NB:(n + 1) * NB], start=True, stop=True)
                ins.then_inc(S("ada_sum"), 1)

            ctx_state(0)
            ctx_state(1)
            token_block(at["o"][0], [(*X0, 0), (*X1, 1)], before=lambda: (ctx_state(2), ctx_state(3)))
            outputs(0)
            token_block(at["o"][1], [(*X0, 2), (*X1, 3)], before=lambda: outputs(1))
            pe.wait_ge(S("o_done"), 4)
            pe.wait_ge(ada2_used, len(ada2))
            gate_vector(0, 0)
            for j in range(2 * KD):
                ins = pe.matmul(ps[:, 2, j:j + 1], ada_acc[1 + j // KD][:, (j % KD) * P:(j % KD + 1) * P], ones[:, 0:1],
                                start=True, stop=True)
            ins.then_inc(S("ada_sum"), 1)
            outputs(2)
            pe.wait_ge(S("mods_out"), 2)
            gate_vector(3, 0)
            outputs(3)
            pe.wait_ge(S("mods_out"), 5)
            pe.wait_ge(S("y1_ready"), MH * TT)
            transposed("y1", ymix, False)
            pe.wait_ge(S("h_sum"), 2 * MH)
            for n in range(2):
                token_block(at["mix_out"][n], [(*X0, 4 + 2 * n), (*X1, 5 + 2 * n)], arrived=hT("y1") if n == 0 else None)
            if STOP == "B":
                return

            done = {"up": 0, "gate_up": PAIRS}

            def ffn(name, norm):
                for j in range(PAIRS):
                    b = 4 * (j % 2)
                    if j == 0:
                        pe.wait_ge(S("hT"), base("hT", norm) + 4)
                    if j >= 2:
                        pe.wait_ge(S("act_full"), done[name] + j - 1)
                    feature_tiles(at[name][2 * j], (b, b + 1))
                    feature_tiles(at[name][2 * j + 1], (b + 2, b + 3))

            def act_arrived(name):
                return lambda k0, k1: pe.wait_ge(S("act_lo"), done[name] + k1 // 2)

            def second(name, first, hi, lo):
                pe.wait_ge(S("act_full"), done[first] + PAIRS - 1)
                for n in range(2):
                    token_block(at[name][n], [(hi, lo, 0, 4 + 2 * n), (hi, lo, 1, 5 + 2 * n)], nk=KF,
                                arrived=act_arrived(first) if n == 0 else None)

            transposed("norm2", x, True)
            ffn("up", "norm2")
            second("down", "up", act_hi, act_lo)
            if STOP == "D":
                return

            transposed("norm3", x, True)
            pe.wait_ge(S("full"), base("full", "norm3") + KD)
            pe.wait_ge(S("small_in"), 16 * 5)
            pe.wait_ge(S("x_upd"), 8)
            for t in range(TT):
                for k in range(KD):
                    ins = pe.matmul(ps[:, 4, 16 * t:16 * t + 16], full[:, k, t * P:(t + 1) * P], wsm[:, k, :],
                                    start=k == 0, stop=k == KD - 1)
            ins.then_inc(S("sgate_mm"), 1)

            def gdn_tiles(j):
                if j >= 2:
                    pe.wait_ge(S("conv2_done"), 2 * j - 2)
                feature_tiles(at["gdn"][j], (2 * (j % 2), 2 * (j % 2) + 1))

            def to_tokens(i, banks):
                pe.wait_ge(S("conv2_silu"), 4 * i + 4)
                for t in range(TT):
                    for h in range(GH):
                        ins = flip(ps[:, banks[t], h * GD:(h + 1) * GD], r5[:, 4 * i + h, t * P:(t + 1) * P])
                    ins.then_inc(S("tok_T"), 1)

            def decay_sums():
                pe.wait_ge(S("sgate_ready"), 1)
                for t in range(TT):
                    pe.matmul(ps[:, 4, 4 * t:4 * t + 4], s_le_t[:], g_dec[:, t, :], start=True, stop=True)
                pe.matmul(ps[:, 4, 8:12], ones[:], g_dec[:, 0, :], start=True, stop=True).then_inc(S("gc_mm"), 1)
                for t in range(TT):
                    for h in range(GH):
                        ins = pe.matmul(ps[:, 5 + t, h * P:(h + 1) * P], g_dec[:, t, h:h + 1].to_broadcast([P, P]),
                                        s_le_t[:], start=True, stop=True)
                    ins.then_inc(S("gcb_mm"), 1)

            def forget_sums(i):
                if i == 0:
                    pe.wait_ge(S("sgate_ready"), 2)
                else:
                    pe.wait_ge(S("neg_c_out"), i)
                for b in range(2):
                    f0, f1 = (lf2[:, t, 2 * i + b:2 * i + b + 1].to_broadcast([P, P]) for t in range(TT))
                    c = b * T
                    pe.matmul(ps[:, 7, c:c + P], f0, s_le_t[:], start=True, stop=True)
                    pe.matmul(ps[:, 7, c + P:c + T], f0, ones[:], start=True, stop=False)
                    ins = pe.matmul(ps[:, 7, c + P:c + T], f1, s_le_t[:], start=False, stop=True)
                ins.then_inc(S("fsum_mm"), 1)

            pe.wait_ge(S("hT"), base("hT", "norm3") + 4)
            gdn_tiles(0)
            gdn_tiles(1)
            decay_sums()
            gdn_tiles(2)
            forget_sums(0)
            pe.wait_ge(S("dec_z"), TT)
            to_tokens(0, (4, 5))
            gdn_tiles(3)
            forget_sums(1)
            gdn_tiles(4)
            forget_sums(2)
            pe.wait_ge(S("tok_out"), 1)
            to_tokens(1, (6, 4))
            gdn_tiles(5)
            forget_sums(3)

            def fox_tiles(j):
                if j < 2:
                    pe.wait_ge(S("conv2_done"), 8 + 2 * j + 2)
                else:
                    pe.wait_ge(S("fox_T"), 2 * j - 2)
                feature_tiles(at["fox"][j], (2 * (j % 2), 2 * (j % 2) + 1))

            fox_tiles(0)
            pe.wait_ge(S("tok_out"), 3)
            to_tokens(2, (5, 6))
            fox_tiles(1)
            fox_tiles(2)

            pe.wait_ge(S("tok_out"), 6)
            pe.wait_ge(S("neg_c_out"), 4)
            for h in range(GH):
                for a in range(2):
                    for t in range(TT):
                        ins = flip(ps[:, 4 + h, a * T + t * P:a * T + (t + 1) * P], qk_n[:, a, t, h * GD:(h + 1) * GD])
                ins.then_inc(S("gT_mm"), 1)
            fox_tiles(3)
            pe.wait_ge(S("gT_ready"), GH)
            for a, bank in ((1, 4), (0, 6)):
                for t in range(TT):
                    tok = slice(t * P, (t + 1) * P)
                    for h in range(GH):
                        ins = pe.matmul(ps[:, bank + t, h * P:(h + 1) * P], gT[:, h, 1, tok], gT[:, h, a, tok],
                                        start=True, stop=True)
                    ins.then_inc(S("kk_mm"), 1)
            pe.wait_ge(S("fox_T"), 8)
            token_block(at["fox_v"][0], [(*X0, 0), (*X1, 1)])
            for t in range(TT):
                for h in range(GH):
                    ins = pe.matmul(ps[:, 2 + t, h * P:(h + 1) * P], beta[:, t, h:h + 1].to_broadcast([P, P]), ident[:],
                                    start=True, stop=True)
                ins.then_inc(S("beta_mm"), 1)
            pe.wait_ge(S("qkT2_ready"), TT)
            token_block(at["z"][0], [(*X0, 6), (*X1, 7)])
            pe.wait_ge(S("q_exp_ready"), 1)
            pe.wait_ge(S("fox_v_out"), 2)
            for h in range(GH):
                ins = flip(ps[:, 0, h * P:(h + 1) * P], q_exp[:, h * GD:(h + 1) * GD])
            ins.then_inc(S("q_expT_mm"), 1)
            pe.wait_ge(S("cT_ready"), 1)
            for t in range(TT):
                for h in range(GH):
                    ins = flip(ps[:, 4 + t, h * P:(h + 1) * P], cT[:, GH * t + h, :])
                ins.then_inc(S("c_T"), 1)

            def fox_logits(h):
                if h == 0:
                    pe.wait_ge(S("q_expT_ready"), 1)
                    pe.wait_ge(S("cT_ready"), 1)
                if h >= 2:
                    pe.wait_ge(S("logit_ready"), 2 * (h - 1))
                row = slice(FD * (h % 2), FD * (h % 2) + FD)
                q, k = foxT[row, h // 2, :], foxT[row, FH // 2 + h // 2, :]
                pe.matmul(ps[:, h % 2, 0:P], q[:, 0:P], k[:, 0:P], start=True, stop=True)
                pe.matmul(ps[:, h % 2, P:3 * P], q[:, P:T], k, start=True, stop=True).then_inc(S("logit_mm"), 1)

            def fox_transpose(h):
                pe.wait_ge(S("prob2_ready"), 2 * h + 2)
                if h:
                    pe.wait_ge(S("prT_ready"), h)
                for i in range(3):
                    ins = flip(ps[:, 2, i * P:(i + 1) * P], logit[:, h % 2, i * P:(i + 1) * P])
                ins.then_inc(S("prT_mm"), 1)

            def fox_out(h):
                pe.wait_ge(S("prT_ready"), h + 1)
                if h:
                    pe.wait_ge(S("fox_done"), 2 * h)
                v = fox_v[:, :, h * FD:(h + 1) * FD]
                pe.matmul(ps[:, 3, 0:FD], prT[:, h % 2, 0:P], v[:, 0], start=True, stop=True)
                pe.matmul(ps[:, 3, FD:2 * FD], prT[:, h % 2, P:2 * P], v[:, 0], start=True, stop=False)
                pe.matmul(ps[:, 3, FD:2 * FD], prT[:, h % 2, 2 * P:], v[:, 1], start=False, stop=True)                    .then_inc(S("fox_mm"), 1)

            def fox_step(i):
                if i < FH:
                    fox_logits(i)
                if 1 <= i <= FH:
                    fox_transpose(i - 1)
                if 2 <= i <= FH + 1:
                    fox_out(i - 2)

            fox_step(0)
            for i in range(len(LEVELS)):
                last = i == len(LEVELS) - 1
                pe.wait_ge(S("cTl_ready"), i + 1)
                for t in range(TT):
                    pe.wait_ge(S("inv_ready"), TT * i + t + 1)
                    if i == 0:
                        pe.wait_ge(S("c_out"), TT)
                    for h in range(GH):
                        a = GH * t + h
                        ins = pe.matmul(ps[:, 4 + t, h * P:(h + 1) * P], cTl[:, i % 2, a, :], inv[:, a, :],
                                        start=True, stop=True)
                    ins.then_inc(S("xs_mm"), 1)
                fox_step(i + 1)
                for t in range(TT):
                    pe.wait_ge(S("xs_ready"), TT * i + t + 1)
                    if i == 0 and t == 0:
                        pe.wait_ge(S("z_out"), 2)
                    if not last:
                        for h in range(GH):
                            a = GH * t + h
                            pe.matmul(ps[:, 6 + t, h * P:(h + 1) * P], invT[:, a, :], xs[:, a, :], start=True, stop=True)
                    for h in range(GH):
                        a = GH * t + h
                        ins = pe.matmul(ps[:, 4 + t, h * P:(h + 1) * P], xs[:, a, :], invT[:, a, :], start=True, stop=True)
                    ins.then_inc(S("y_mm"), 1)
            fox_step(len(LEVELS) + 1)
            for t in range(TT):
                pe.wait_ge(S("inv_ready"), TT * len(LEVELS) + t + 1)
                pe.wait_ge(S("inv_ready"), TT * (len(LEVELS) + 1))
                for h in range(GH):
                    ins = pe.matmul(ps[:, 4 + t, h * P:(h + 1) * P], invT[:, GH * t + h, :], vb[:, t, h * GD:(h + 1) * GD],
                                    start=True, stop=True)
                ins.then_inc(S("u_mm"), 1)
            pe.wait_ge(S("k_beta_ready"), 1)
            for h in range(GH):
                ins = pe.matmul(ps[:, 6, h * P:(h + 1) * P], k_beta[:, h * GD:(h + 1) * GD], invT[:, GH + h, :],
                                start=True, stop=True)
            ins.then_inc(S("w_mm"), 1)
            pe.wait_ge(S("k_dec_ready"), 1)
            pe.wait_ge(S("u_out"), 1)
            for h in range(GH):
                hs = slice(h * GD, (h + 1) * GD)
                ins = pe.matmul(ps[:, 7, hs], k_dec[:, hs], u_tok[:, 0, hs], start=True, stop=True)
            ins.then_inc(S("st_mm"), 1)
            fox_step(len(LEVELS) + 2)
            fox_step(len(LEVELS) + 3)
            pe.wait_ge(S("logit_ready"), 2 * FH)
            for h in range(GH):
                hs = slice(h * GD, (h + 1) * GD)
                ins = pe.matmul(ps[:, 0, hs], qkT2[:, h, :], u_tok[:, 0, hs], start=True, stop=True)
            ins.then_inc(S("o_mm"), 1)
            pe.wait_ge(S("st_ready"), 1)
            pe.wait_ge(S("wT_ready"), 1)
            for h in range(GH):
                hs = slice(h * GD, (h + 1) * GD)
                ins = pe.matmul(ps[:, 6, hs], wT[:, hs], st1[:, hs], start=True, stop=True)
            ins.then_inc(S("ws_mm"), 1)
            pe.wait_ge(S("v_new_ready"), 1)
            for h in range(GH):
                hs = slice(h * GD, (h + 1) * GD)
                pe.matmul(ps[:, 1, hs], q_expT[:, h, :], st1[:, hs], start=True, stop=False)
                ins = pe.matmul(ps[:, 1, hs], qkT2[:, GH + h, :], v_new[:, hs], start=False, stop=True)
            ins.then_inc(S("o_mm"), 1)
            pe.wait_ge(S("mix_ready"), 2)
            pe.wait_ge(S("fox_done"), 2 * FH)
            transposed("mix", mix, False)
            pe.wait_ge(S("u_out"), 2)
            for n in range(2):
                token_block(at["att_out"][n], [(*X0, 4 + 2 * n), (*X1, 5 + 2 * n)], arrived=hT("mix") if n == 0 else None)
            if STOP == "E":
                return
            pe.wait_ge(S("x_upd"), 12)
            transposed("norm4", x, True)
            ffn("gate_up", "norm4")
            second("down2", "gate_up", act2_hi, act2_lo)
            pe.wait_ge(S("p_in"), 16)
            for k in range(2):
                for t in range(TT):
                    ins = flip(ps[:, 0, k * T + t * P:k * T + (t + 1) * P], p_tok[:, t, k * P:(k + 1) * P])
            ins.then_inc(S("p_T"), 1)
            pe.wait_ge(S("p_lo"), 1)
            s = at["ple_p"][0]
            hi, lo = weights(s)
            for n in range(2):
                for t in range(TT):
                    for k in range(2):
                        tok, c = slice(t * P, (t + 1) * P), slice(n * NB, (n + 1) * NB)
                        ins = mm3(ps[:, 2 * n + t, :], (p_hi[:, k, tok], p_lo[:, k, tok]), (hi[:, k, c], lo[:, k, c]),
                                  k == 0, k == 1)
            ins.then_inc(group_used, 1)
            pe.wait_ge(S("p_out"), 4)
            pe.wait_ge(S("x_upd"), 16)
            transposed("norm5", x, True)
            for n in range(2):
                token_block(at["ple_g"][n], [(*X0, 4 + 2 * n), (*X1, 5 + 2 * n)], arrived=hT("norm5") if n == 0 else None)


_INS = ['x', 'c', 'ctx', 'c_ctx', 'ada_w', 'ada_b', 'pre_mix_g', 'post_mix_g', 'pre_ffn_g', 'post_ffn_g', 'ffn_up_w',
        'ffn_conv_w', 'ffn_conv_b', 'ffn_down_w', 'm_in_w', 'm_in_b', 'm_norm_g', 'm_out_w', 'p_2', 'attn_norm_w_2',
        'w_in_2', 'conv_w_2', 'a_log_2', 'dt_bias_2', 'gdn_norm_w_2', 'fox_f_bias_2', 'w_out_2', 'ffn_norm_w_2',
        'w_gate_up_2', 'w_down_2', 'ple_norm_w_2', 'w_ple_gate_2', 'w_ple_proj_2', 'final_norm_w_2']


def kernel(**inputs):
    import numpy as _np
    import concourse.bacc as _bacc
    from concourse import mybir as _mybir
    from concourse.bass_utils import run_bass_kernel_spmd as _run

    nc = _bacc.Bacc("TRN2", target_bir_lowering=False, num_devices=1, dynamic_dma_scratch_size=1024)
    arrays, tensors = {}, {}
    for name in _INS:
        a = _np.ascontiguousarray(inputs[name])
        arrays[f"in_{name}"] = a
        tensors[name] = nc.dram_tensor(f"in_{name}", a.shape, _mybir.dt.from_np(a.dtype), kind="ExternalInput").ap()
    out = nc.dram_tensor("out", (1, T, D), F32, kind="ExternalOutput").ap()
    two_blocks(nc, tensors, out)
    r = _run(nc, [arrays], core_ids=[0])
    return r.results[0]["out"]
```

```python
from contextlib import ExitStack

import concourse.bass as bass
from concourse import mybir

F32 = mybir.dt.float32
F32R = mybir.dt.float32r
ALU = mybir.AluOpType
ACT = mybir.ActivationFunctionType
AX_X = mybir.AxisListType.X

P = 128
T = 256
TT = T // P
D = 1024
KD = D // P
NB = 512
EPS = 1e-6
RING = 3
GROUP = 2048

MH, DK, DV = 4, 128, 256
FF = 2816
KF = FF // P
PAIRS = KF // 2
GRID_W = 64
GH, GD = 4, 128
FOX_ORDER = (0, 2, 1, 3)
FH, FD = 8, 64
PLE = 256
LEVELS = (2, 4, 8, 16, 32, 64)
NEG = -1.0e30


def plan_groups(I):
    groups, split, at = [], [], {}

    def add(w, k0, nk, c0, ncol, consumer="split"):
        if consumer == "split":
            split.append(len(groups))
        groups.append((w[k0 * P:(k0 + nk) * P, c0:c0 + ncol].rearrange("(k p) n -> p k n", p=P), nk, ncol, consumer))

    def block(name, w, c0, nk=KD, ada_after=(), first=0):
        at.setdefault(name, []).append(len(split))
        for i, k0 in enumerate(range(0, nk, 4)):
            k0 = (k0 + first) % nk if first else k0
            add(w, k0, min(4, nk - k0), c0, NB)
            if i < len(ada_after):
                (ada1 if name == "k" else ada2)(ada_after[i])

    def tiles(name, w, c0):
        at.setdefault(name, []).append(len(split))
        add(w, 0, KD, c0, 2 * P)

    def ada_groups(v0, n_vec):
        return iter([(k0, v * D + n * NB) for v in range(v0, v0 + n_vec) for n in range(D // NB) for k0 in (0, 4)])

    ada_early, ada_late = ada_groups(0, 2), ada_groups(2, 4)

    def ada1(count):
        for _ in range(count):
            k0, c0 = next(ada_early)
            add(I["ada_w"][0], k0, 4, c0, NB, "ada1")

    def ada2(count):
        for _ in range(count):
            k0, c0 = next(ada_late)
            add(I["ada_w"][0], k0, 4, c0, NB, "ada2")

    m_in, w_in = I["m_in_w"][0], I["w_in_2"][0]
    v0, o0 = 2 * MH * DK, 2 * MH * DK + MH * DV
    fox0 = 4 * GH * GD + 2 * GH
    ada1(7)
    block("k", m_in, MH * DK, ada_after=(1,))
    block("q", m_in, 0, ada_after=(1, 2))
    block("v", m_in, v0, ada_after=(1, 2))
    block("v", m_in, v0 + NB, ada_after=(1, 2))
    block("o", m_in, o0, ada_after=(1, 2))
    block("o", m_in, o0 + NB)
    for n in range(2):
        block("mix_out", I["m_out_w"][0], n * NB)
    for j in range(PAIRS):
        tiles("up", I["ffn_up_w"][0], FF + 2 * j * P)
        tiles("up", I["ffn_up_w"][0], 2 * j * P)
    for n in range(2):
        block("down", I["ffn_down_w"][0], n * NB, KF, ada_after=(0, 1, 1, 1, 1) if n == 0 else ())
    for j in range(6):
        tiles("gdn", w_in, 2 * j * P)
    for j in FOX_ORDER[:2]:
        tiles("fox", w_in, fox0 + 2 * j * P)
    block("fox_v", w_in, fox0 + 2 * FH * FD)
    for j in FOX_ORDER[2:]:
        tiles("fox", w_in, fox0 + 2 * j * P)
    block("z", w_in, 3 * GH * GD)
    for n in range(2):
        block("att_out", I["w_out_2"][0], n * NB, first=KD // 2)
    for j in range(PAIRS):
        tiles("gate_up", I["w_gate_up_2"][0], 2 * j * P)
        tiles("gate_up", I["w_gate_up_2"][0], FF + 2 * j * P)
    for n in range(2):
        block("down2", I["w_down_2"][0], n * NB, KF)
    at["ple_p"] = [len(split)]
    add(I["w_ple_proj_2"][0], 0, 2, 0, D)
    for n in range(2):
        block("ple_g", I["w_ple_gate_2"][0], n * NB)
    return groups, split, at


def two_blocks(nc, I, out, STOP=None):
    groups, split, at = plan_groups(I)
    ada1 = [g for g, x in enumerate(groups) if x[3] == "ada1"]
    ada2 = [g for g, x in enumerate(groups) if x[3] == "ada2"]
    n_split = len(split)
    last_group = {"A": split[at["o"][1] + 1], "B": split[at["mix_out"][1] + 1], "D": split[at["down"][1] + 5],
                  "E": split[at["att_out"][1] + 1], None: len(groups) - 1}[STOP]
    n_split = sum(1 for g in split if g <= last_group)

    with ExitStack() as ctx:
        sems = {}

        def S(name):
            if name not in sems:
                sems[name] = ctx.enter_context(nc.semaphore(name))
            return sems[name]

        FAMILY = {
            "ss": (("norm1", 4), ("head", 8), ("post1", 4), ("norm2", 4), ("post2", 4), ("norm3", 4), ("gdn", 8),
                   ("norm4", 4), ("norm5", 4), ("final", 4)),
            "rstd": (("norm1", 2), ("head", 4), ("post1", 1), ("norm2", 1), ("post2", 1), ("norm3", 1), ("gdn", 2),
                     ("norm4", 1), ("norm5", 1), ("final", 2)),
            "diag": (("norm1", 4), ("norm2", 2), ("norm3", 2), ("norm4", 2), ("norm5", 2)),
        }
        for kind in ("tr", "hi", "hT"):
            FAMILY[kind] = tuple((name, KD) for name in ("norm1", "y1", "norm2", "norm3", "mix", "norm4", "norm5"))
        SS = {"norm1": 0, "head": 4, "post1": 12, "norm2": 16, "post2": 20, "norm3": 24, "l2": 28, "gdn": 44,
              "norm4": 52, "norm5": 56, "final": 60}

        def base(kind, name):
            before = 0
            for stage, n in FAMILY[kind]:
                if stage == name:
                    return before
                before += n

        def sb(scope, name, shape, dt=F32):
            return scope.enter_context(nc.sbuf_tensor(name, shape, dt))

        ps = ctx.enter_context(nc.psum_tensor("ps", [P, 8, NB], F32))
        raw = sb(ctx, "raw", [P, RING, GROUP])
        w_hi = sb(ctx, "w_hi", [P, RING, GROUP], F32R)
        w_lo = sb(ctx, "w_lo", [P, RING, GROUP], F32R)
        x = sb(ctx, "x", [P, TT, D])
        full = sb(ctx, "full", [P, KD, T])
        yg = full[:].rearrange("p k t -> p (k t)").rearrange("p (t n) -> p t n", t=TT)
        h_hi = sb(ctx, "h_hi", [P, KD, T], F32R)
        h_lo = sb(ctx, "h_lo", [P, KD, T], F32R)
        ident = sb(ctx, "ident", [P, P])
        s_le_t = sb(ctx, "s_le_t", [P, P])
        s_ge_t = sb(ctx, "s_ge_t", [P, P])
        s_lt_t = sb(ctx, "s_lt_t", [P, P])
        s_gt_t = sb(ctx, "s_gt_t", [P, P])
        ones = sb(ctx, "ones", [P, P])
        diag = sb(ctx, "diag", [P, 2 * TT, P])
        VEC = (("ada_b", I["ada_b"][0]), ("pre_mix", I["pre_mix_g"][0]),
               ("pre_ffn", I["pre_ffn_g"][0]), ("attn_norm", I["attn_norm_w_2"][0]), ("ffn_norm", I["ffn_norm_w_2"][0]),
               ("ple_norm", I["ple_norm_w_2"][0]), ("m_norm", I["m_norm_g"][0]), ("gdn_norm", I["gdn_norm_w_2"][0]))
        col, n_vec = {}, 0
        for name, src in VEC:
            col[name] = n_vec
            n_vec += src.shape[0] // P
        col["conv_w"], col["conv_b"], col["conv2"] = n_vec, n_vec + 3 * KF, n_vec + 4 * KF
        n_col = n_vec + 4 * KF + 48
        cols = sb(ctx, "cols", [P, n_col])

        def pcol(name, k):
            return cols[:, col[name] + k:col[name] + k + 1]

        c_rows = sb(ctx, "c_rows", [2 * KD, P])
        cpad = sb(ctx, "cpad", [P, KD, 32])
        row_of = sb(ctx, "row_of", [P, 2])
        mod = sb(ctx, "mod", [P, 2 * KD, 2])
        mod2 = sb(ctx, "mod2", [P, 2 * KD])
        mhalf = sb(ctx, "mhalf", [P, 16])
        ss = sb(ctx, "ss", [P, 64])
        rstd = sb(ctx, "rstd", [P, 64])
        junk = sb(ctx, "junk", [P, D])
        tmp = sb(ctx, "tmp", [P, 2, NB])

        with ExitStack() as b1:
            gp1 = sb(b1, "gp1", [P, D])
            gp2 = sb(b1, "gp2", [P, D])
            acc2 = sb(b1, "acc2", [P, 2, D])
            acc1 = full[:].rearrange("p k t -> p (k t)").rearrange("p (a n) -> p a n", a=2)
            ada_acc = (acc1[:, 0], acc1[:, 1], acc2[:, 0], acc2[:, 1])
            with ExitStack() as mx:
                with ExitStack() as early:
                    c_hi = sb(early, "c_hi", [P, KD, T], F32R)
                    c_lo = sb(early, "c_lo", [P, KD, T], F32R)
                late = sb(mx, "late", [P, MH * 2 * (DV + 1) + TT * D])
                state = late[:, 0:MH * 2 * (DV + 1)].rearrange("p (h d e) -> p h d e", h=MH, d=2)
                hsum = late[:, MH * 2 * (DV + 1):].rearrange("p (t n) -> p t n", t=TT)
                r2 = sb(mx, "r2", [P, TT * D])
                cfull = r2[:].rearrange("p (k t) -> p k t", k=KD)
                qk_tok = r2[:].rearrange("p (a t n) -> p a t n", a=2, t=TT)
                so = r2[:].rearrange("p (t n) -> p t n", t=TT)
                r3 = sb(mx, "r3", [P, 2 * TT * MH * (DV + 1)])
                vaug = r3[:].rearrange("p (t h e) -> p t h e", t=2 * TT, h=MH)
                u_row = r3[0:MH, 2048:2048 + 2 * T].rearrange("p (d t) -> p d t", d=2)
                ws_row = r3[0:MH, 2560:2560 + 2 * T].rearrange("p (d t) -> p d t", d=2)
                ada_rows = r3[:, 0:4 * NB].rearrange("p (n c) -> p n c", n=4)
                vec_rows = (r3[0:n_vec, 2048:2048 + P], r3[0:4 * KF, 2048 + P:2048 + 2 * P],
                            r3[0:48, 2048 + 2 * P:2048 + 3 * P])
                qkT = sb(mx, "qkT", [P, MH, 2, T])
                prob = sb(mx, "prob", [P, MH, 2, 3 * P])
                prob_flat = prob[:].rearrange("p h d n -> p (h d n)")
                ctx_tok = prob_flat[:, 0:TT * D].rearrange("p (t n) -> p t n", t=TT)
                ymix = ctx_tok
                qTw = sb(mx, "qTw", [P, MH, 2, T])
                r4 = sb(mx, "r4", [P, 2 * TT * 2 * P])
                kw = r4[:].rearrange("p (b t d n) -> p b t d n", b=2, t=TT, d=2)
                m_row = junk[0:MH, 0:2 * T].rearrange("p (d t) -> p d t", d=2)
                w_row = junk[0:MH, 2 * T:4 * T].rearrange("p (d t) -> p d t", d=2)
                k_ctx = sb(mx, "k_ctx", [P, TT, NB])
                bias = sb(mx, "bias", [P, 2, NB])
                wg = sb(mx, "wg", [P, KD, 16])
                bg = sb(mx, "bg", [P, 16])
                gate = sb(mx, "gate", [P, 2 * TT, 16])
                gate_v = gate[:].rearrange("p t (d x h) -> p (t d) x h", d=2, x=2)
                lf = sb(mx, "lf", [P, 2 * TT * 2, MH])
                sp1 = sb(mx, "sp1", [P, 2 * TT * 2, MH])
                b_col = sb(mx, "b_col", [P, TT * 2, MH])
                u_col = sb(mx, "u_col", [P, TT * 2, MH])
                gs_col = sb(mx, "gs_col", [P, TT * 2, MH])
                ws_col = sb(mx, "ws_col", [P, TT * 2, MH])
                emt = sb(mx, "emt", [P, TT * 2, MH])
                b_ctx = sb(mx, "b_ctx", [MH, 2])
                m_ctx = sb(mx, "m_ctx", [MH, 4])
                sel = sb(mx, "sel", [MH, MH, P])
                den = sb(mx, "den", [P, 2, 4])
            with ExitStack() as fs:
                act_hi = sb(fs, "act_hi", [P, KF, T], F32R)
                act_lo = sb(fs, "act_lo", [P, KF, T], F32R)
                cv = sb(fs, "cv", [P, 2, 2, T])
                actf = sb(fs, "actf", [P, 2, 2, T])
        with ExitStack() as b2:
            r5 = sb(b2, "r5", [P, 12, T])
            r5f = r5[:].rearrange("p f t -> p (f t)")
            inv = r5f[:, 0:1024].rearrange("p (a i) -> p a i", i=P)
            invT = r5f[:, 1024:2048].rearrange("p (a i) -> p a i", i=P)
            qk_n = sb(b2, "qk_n", [P, 2, TT, NB])
            mix = qk_n[:].rearrange("p a t n -> p (a t n)").rearrange("p (t n) -> p t n", t=TT)
            vb = sb(b2, "vb", [P, TT, NB])
            k_beta = sb(b2, "k_beta", [P, NB])
            k_dec = sb(b2, "k_dec", [P, NB])
            q_exp = sb(b2, "q_exp", [P, NB])
            q_expT = sb(b2, "q_expT", [P, GH, P])
            gT = sb(b2, "gT", [P, GH, 2, T])
            gTf = gT[:].rearrange("p h a t -> p (h a t)")
            st1 = gTf[:, 0:NB]
            wT = gTf[:, NB:2 * NB]
            v_new = gTf[:, 2 * NB:3 * NB]
            decT = sb(b2, "decT", [P, TT * GH, P])
            u_tok = decT[:].rearrange("p (t h) i -> p t (h i)", t=TT)
            cT = sb(b2, "cT", [P, TT * GH, P])
            cTl = sb(b2, "cTl", [P, 2, TT * GH, P])
            qkT2 = sb(b2, "qkT2", [P, TT * GH, P])
            neg_c = sb(b2, "neg_c", [P, FH, T])
            foxT = sb(b2, "foxT", [P, 8, T])
            fox_v = sb(b2, "fox_v", [P, TT, NB])
            zs = sb(b2, "zs", [P, TT, NB])
            r6 = sb(b2, "r6", [P, 4, 3 * P])
            logit = r6[:, 0:2]
            prT = r6[:, 2:4]
            sq = r6[:].rearrange("p a n -> p (a n)")[:, 0:2 * NB].rearrange("p (t n) -> p t n", t=TT)
            level = sb(b2, "level", [P, 7, P])
            wsm = sb(b2, "wsm", [P, KD, 16])
            sm = sb(b2, "sm", [P, TT, 16])
            gprm = sb(b2, "gprm", [P, 16])
            g_dec = sb(b2, "g_dec", [P, TT, GH])
            beta = sb(b2, "beta", [P, TT, GH])
            lf2 = sb(b2, "lf2", [P, TT, FH])
            sp2 = sb(b2, "sp2", [P, TT, 16])
            gc = sb(b2, "gc", [P, 3, GH])
            egc = sb(b2, "egc", [P, 3, GH])
            fsum = sb(b2, "fsum", [P, 2, 4])
            og = sb(b2, "og", [P, TT, NB])
            xs = og[:].rearrange("p t (h i) -> p (t h) i", i=P)
        with ExitStack() as b3:
            act2_hi = sb(b3, "act2_hi", [P, KF, T], F32R)
            act2_lo = sb(b3, "act2_lo", [P, KF, T], F32R)
            sil = sb(b3, "sil", [P, 2, 2, T])
            actf2 = sb(b3, "actf2", [P, 2, 2, T])
            p_tok = sb(b3, "p_tok", [P, TT, PLE])
            pT = sb(b3, "pT", [P, 2, T])
            p_hi = sb(b3, "p_hi", [P, 2, T], F32R)
            p_lo = sb(b3, "p_lo", [P, 2, T], F32R)
            gp3 = sb(b3, "gp3", [P, D])
            pgate = sb(b3, "pgate", [P, TT, D])

        raw_in = [S(f"raw_in{i}") for i in range(RING)]
        hi_ready, lo_ready, group_used = S("hi_ready"), S("lo_ready"), S("group_used")
        ada1_used, ada2_used = S("ada1_used"), S("ada2_used")

        def raw_view(g):
            _, nk, ncol, _ = groups[g]
            return raw[:, g % RING, :nk * ncol].rearrange("p (k n) -> p k n", k=nk)

        def part_view(part, s):
            _, nk, ncol, _ = groups[split[s]]
            return part[:, s % RING, :nk * ncol].rearrange("p (k n) -> p k n", k=nk)

        def raw_arrived(eng, g):
            eng.wait_ge(raw_in[g % RING], 16 * (g // RING + 1))

        def chained(eng, name):
            count = [0]

            def link(ins):
                count[0] += 1
                ins.then_inc(S(name), 1)
                eng.wait_ge(S(name), count[0])

            return link

        def first_pairs(x_part, c_part):
            for two in (0, 2):
                for part, whole in ((x_part, full), (c_part, cfull)):
                    for i in (two, two + 1):
                        yield part, whole, slice(2 * i, 2 * i + 2)

        block = ctx.enter_context(nc.Block())


        @block.sync
        def _(sp):
            sp.dma_start(c_rows[0:KD, :], I["c"][0].rearrange("(k p) -> k p", p=P)).then_inc(S("c_in"), 16)
            for g in range(last_group + 1):
                if g >= RING:
                    old = g - RING
                    consumer = groups[old][3]
                    if consumer == "ada1":
                        sp.wait_ge(ada1_used, ada1.index(old) + 1)
                    elif consumer == "ada2":
                        sp.wait_ge(ada2_used, ada2.index(old) + 1)
                    else:
                        sp.wait_ge(lo_ready, split.index(old) + 1)
                sp.dma_start(raw_view(g), groups[g][0]).then_inc(raw_in[g % RING], 16)
            for t in range(TT):
                if STOP:
                    if STOP != "A":
                        sp.wait_ge(S("x_upd"), {"B": 4, "D": 8, "E": 12}[STOP])
                    sp.dma_start(out[0, t * P:(t + 1) * P, :], x[:, t, :]).then_inc(S("out_done"), 16)
                else:
                    sp.wait_ge(S("result"), t + 1)
                    sp.dma_start(out[0, t * P:(t + 1) * P, :], pgate[:, t, :]).then_inc(S("out_done"), 16)
            sp.wait_ge(S("out_done"), 16 * TT)

        @block.gpsimd
        def _(pool):
            link = chained(pool, "pool_chain")

            def rms_scale(name, c0, n, width, halves=False, apart=TT):
                s = ss[:, c0:c0 + n]
                if halves:
                    link(pool.tensor_tensor(s, s, ss[:, c0 + apart:c0 + apart + n], ALU.add))
                link(pool.tensor_scalar(s, s, 1.0 / width, EPS, ALU.mult, ALU.add))
                pool.tensor_tensor(rstd[:, c0:c0 + n], s, mhalf[:, 0:n], ALU.pow).then_inc(S("rstd"), 1)

            def keep(a, op, pattern, channel, fill=0.0, base=0):
                return pool.affine_select(out=a, in_=a, compare_op=op, fill=fill, base=base, pattern=pattern,
                                          channel_multiplier=channel)

            link(pool.memset(ident[:], 0.0))
            link(pool.memset(cpad[:], 0.0))
            keep(ident[:], ALU.not_equal, [[-1, P]], 1, fill=1.0).then_inc(S("const_ready"), 1)
            link(pool.memset(row_of[:], 0.0))
            for m in (s_le_t, s_ge_t, s_lt_t, s_gt_t, ones, sel):
                link(pool.memset(m[:], 1.0))
            link(pool.memset(mhalf[:], -0.5))
            for j in range(4):
                link(keep(row_of[:], ALU.not_equal, [[-1, 2]], 1, fill=1.0, base=-32 * j))
            link(keep(s_le_t[:], ALU.is_ge, [[1, P]], -1))
            link(keep(s_ge_t[:], ALU.is_ge, [[-1, P]], 1))
            link(keep(s_lt_t[:], ALU.is_gt, [[1, P]], -1))
            link(keep(s_gt_t[:], ALU.is_gt, [[-1, P]], 1))
            keep(sel[:], ALU.is_equal, [[-1, MH], [0, P]], 1).then_inc(S("const_ready"), 1)

            for i in range(2):
                pool.wait_ge(S("ss"), TT * (i + 1))
                rms_scale("norm1", SS["norm1"] + TT * i, TT, D)

            pool.wait_ge(S("mod_ready"), 1)
            for k in range(KD):
                ins = pool.tensor_scalar(cfull[:, k, :], cfull[:, k, :], mod[:, KD + k, 1:2], mod[:, k, 1:2], ALU.mult, ALU.add)
                if k % 2:
                    ins.then_inc(S("full_c"), 1)
                else:
                    link(ins)

            def causal(h):
                for d in range(2):
                    pool.wait_ge(S("prob_full"), 2 * h + d + 1)
                    sign = 1 - 2 * d
                    pr = prob[:, h, d, :]
                    link(keep(pr[:, d * P:(d + 1) * P], ALU.is_ge, [[sign, P]], -sign))
                    keep(pr[:, 2 * P:], ALU.is_ge, [[sign, P]], -sign).then_inc(S("prob_ready"), 1)

            def weighted_keys(h):
                if h >= 2:
                    pool.wait_ge(S("state_mm"), 2 * (h - 1))
                for t in range(TT):
                    for d in range(2):
                        ins = pool.tensor_scalar(kw[:, h % 2, t, d, :], k_ctx[:, t, h * DK:(h + 1) * DK],
                                                 ws_col[:, 2 * t + d, h:h + 1], None, ALU.mult)
                        if t == 0 or d == 0:
                            link(ins)
                ins.then_inc(S("kw_ready"), 1)

            pool.wait_ge(S("ws_out"), 1)
            pool.wait_ge(S("k_done"), 4)
            weighted_keys(0)
            weighted_keys(1)
            for h in range(MH):
                causal(h)
            weighted_keys(2)
            weighted_keys(3)
            for h in range(MH):
                pool.wait_ge(S("ss"), base("ss", "head") + TT * (h + 1))
                rms_scale("head", SS["head"] + TT * h, TT, DV)
            pool.wait_ge(S("ss"), base("ss", "post1") + 4)
            rms_scale("post1", SS["post1"], TT, D, halves=True)
            if STOP == "B":
                return
            pool.wait_ge(S("ss"), base("ss", "norm2") + 4)
            rms_scale("norm2", SS["norm2"], TT, D, halves=True)
            pool.wait_ge(S("ss"), base("ss", "post2") + 4)
            rms_scale("post2", SS["post2"], TT, D, halves=True)
            if STOP == "D":
                return

            pool.wait_ge(S("ss"), base("ss", "norm3") + 4)
            rms_scale("norm3", SS["norm3"], TT, D, halves=True)
            for i in range(4):
                pair = slice(2 * i, 2 * i + 2)
                pool.wait_ge(S("hT"), base("hT", "norm3") + 2 * i + 2)
                pool.tensor_tensor(full[:, pair, :], h_hi[:, pair, :].bitcast(F32), h_lo[:, pair, :].bitcast(F32), ALU.add)\
                    .then_inc(S("full_ready"), 1)
            pool.wait_ge(S("x_upd"), 8)
            link(pool.memset(level[:], 1.0))
            for i in range(6):
                b = 2 << i
                view = level[:, i, :].rearrange("p (n b) -> p n b", b=b)
                link(keep(view, ALU.is_ge, [[-b, P // b], [0, b]], 1))
                link(keep(view, ALU.is_ge, [[b, P // b], [0, b]], -1, base=b - 1))
            for i in range(6, 0, -1):
                link(pool.tensor_tensor(level[:, i, :], level[:, i, :], level[:, i - 1, :], ALU.subtract))
            pool.tensor_tensor(level[:, 0, :], level[:, 0, :], ident[:], ALU.subtract).then_inc(S("level_ready"), 1)

            for i in range(4):
                pool.wait_ge(S("ss_l2"), i + 1)
                c = slice(SS["l2"] + GH * i, SS["l2"] + GH * (i + 1))
                s = ss[:, c]
                link(pool.tensor_scalar(s, s, EPS, float(GD) if i < 2 else 1.0, ALU.add, ALU.mult))
                pool.tensor_tensor(rstd[:, c], s, mhalf[:, 0:GH], ALU.pow).then_inc(S("rstd_l2"), 1)
                if i < 2:
                    pool.wait_ge(S("dec_exp"), i + 1)
                    keep(decT[:, GH * i:GH * (i + 1), :], ALU.is_ge, [[0, GH], [1, P]], -1).then_inc(S("dec_ready"), 1)

            def by_head(out_, in_, scale, want):
                pool.tensor_tensor(out_.rearrange("p (h n) -> p h n", h=GH), in_.rearrange("p (h n) -> p h n", h=GH),
                                   scale.unsqueeze(2).to_broadcast([P, GH, GD]), ALU.mult).then_inc(S(want), 1)

            pool.wait_ge(S("tok_out"), 4)
            pool.wait_ge(S("egc_ready"), 1)
            by_head(q_exp[:], qk_n[:, 0, 1, :], egc[:, 0, :], "q_exp_ready")
            def level_of(i):
                if i >= 2:
                    pool.wait_ge(S("xs_mm"), TT * (i - 1))
                pool.tensor_tensor(cTl[:, i % 2], cT[:], level[:, i + 1, :].unsqueeze(1).to_broadcast([P, TT * GH, P]),
                                   ALU.mult).then_inc(S("cTl_ready"), 1)

            def fox_mask(h):
                pool.wait_ge(S("logit_ready"), TT * (h + 1))
                for c in (0, 2 * P):
                    keep(logit[:, h % 2, c:c + P], ALU.is_ge, [[-1, P]], 1, fill=NEG).then_inc(S("logit_masked"), 1)

            pool.wait_ge(S("cT_full"), TT)
            pool.wait_ge(S("level_ready"), 1)
            level_of(0)
            fox_mask(0)
            level_of(1)
            by_head(k_beta[:], qk_n[:, 1, 1, :], egc[:, 1, :], "k_beta_ready")
            by_head(k_dec[:], qk_n[:, 1, 0, :], egc[:, 2, :], "k_dec_ready")
            for i in range(1, FH):
                fox_mask(i)
                if i + 1 < len(LEVELS):
                    level_of(i + 1)
            for t in range(TT):
                pool.wait_ge(S("ss"), base("ss", "gdn") + GH * (t + 1))
                rms_scale("gdn", SS["gdn"] + GH * t, GH, GD)
            if STOP == "E":
                return
            for name in ("norm4", "norm5"):
                pool.wait_ge(S("ss"), base("ss", name) + 4)
                rms_scale(name, SS[name], TT, D, halves=True)
            for t in range(TT):
                pool.wait_ge(S("ss"), base("ss", "final") + TT + t + 1)
                rms_scale("final", SS["final"] + t, 1, D, halves=True)


        @block.scalar
        def _(act):
            s_next = [0]

            def hi_until(n):
                while s_next[0] < min(n, n_split):
                    s = s_next[0]
                    raw_arrived(act, split[s])
                    if s >= RING:
                        act.wait_ge(group_used, s - RING + 1)
                    act.copy(part_view(w_hi, s), raw_view(split[s])).then_inc(hi_ready, 1)
                    s_next[0] += 1

            def load(dst, src, sem_name):
                act.dma_start(dst, src).then_inc(S(sem_name), 16)

            n_sums = [0]

            def sum_sq(src, c):
                n_sums[0] += 1
                act.activation(junk[:, 0:src.shape[-1]], src, ACT.Square, accum_out=ss[:, c:c + 1]).then_inc(S("ss"), 1)
                act.wait_ge(S("ss"), n_sums[0])

            def norm(name, updates, by_token):
                for i in range(4):
                    t, n = (i // 2, i % 2) if by_token else (i % 2, i // 2)
                    act.wait_ge(S("x_upd"), updates + i + 1)
                    sum_sq(x[:, t, n * NB:(n + 1) * NB], SS[name] + TT * n + t)

            def post(name, product):
                for n in range(2):
                    done = at[product][n] + at[product][1] - at[product][0]
                    hi_until(done + 2)
                    act.wait_ge(group_used, done)
                    for t in range(TT):
                        sum_sq(ps[:, 4 + 2 * n + t, :], SS[name] + TT * n + t)

            def hi_T(name, bank0=0, scale=None, shift=None, order=range(KD)):
                for i, k in enumerate(order):
                    act.wait_ge(S("tr"), base("tr", name) + i + 1)
                    src = ps[:, bank0 + i % 4, 0:T]
                    a = scale(k) if scale else None
                    if a is None:
                        ins = act.copy(h_hi[:, k, :], src)
                    elif shift is None:
                        ins = act.activation(h_hi[:, k, :], src, ACT.Copy, scale=a)
                    else:
                        ins = act.activation(h_hi[:, k, :], src, ACT.Identity, scale=a, bias=shift(k))
                    ins.then_inc(S("hi"), 1)

            load(c_rows[KD:, :], I["c_ctx"].rearrange("(k p) -> k p", p=P), "c_in")
            load(x[:], I["x"][0].rearrange("(t p) n -> p t n", p=P), "x_in")
            act.wait_ge(S("const_ready"), 1)
            act.wait_ge(S("vec_T"), 1)
            act.activation(cpad[:, :, 0:2], ps[:, 7, 0:2 * KD].rearrange("p (c k) -> p k c", c=2), ACT.Silu)\
                .then_inc(S("c_ready"), 1)
            load(ctx_tok, I["ctx"][0].rearrange("(t p) n -> p t n", p=P), "ctx_in")
            for name, src in VEC:
                n = src.shape[0] // P
                load(vec_rows[0][col[name]:col[name] + n, :], src.rearrange("(k p) -> k p", p=P), "vec_in")
            load(vec_rows[1][0:3 * KF, :], I["ffn_conv_w"][0].rearrange("w (a b) -> (w a) b", b=P), "vec_in")
            load(vec_rows[1][3 * KF:4 * KF, :], I["ffn_conv_b"][0].rearrange("(a b) -> a b", b=P), "vec_in")
            load(vec_rows[2], I["conv_w_2"][0].rearrange("w (a b) -> (w a) b", b=P), "vec_in")
            act.wait_ge(S("x_in"), 16)
            for t in range(TT):
                sum_sq(x[:, t, :], SS["norm1"] + t)
            for i in range(4):
                act.wait_ge(S("tr"), i + 1)
                act.copy(full[:, 2 * i:2 * i + 2, :], ps[:, 2 + i, :].rearrange("p (k t) -> p k t", k=2)).then_inc(S("x_out"), 1)
            act.wait_ge(S("ctx_in"), 16)
            for t in range(TT):
                sum_sq(ctx_tok[:, t, :], SS["norm1"] + TT + t)
            hi_until(1)
            gate0 = 2 * MH * DK + 2 * MH * DV
            act.wait_ge(ada1_used, len(ada1))
            load(wg[:], I["m_in_w"][0][:, gate0:gate0 + 16].rearrange("(k p) n -> p k n", p=P), "wg_in")
            load(bg[:], I["m_in_b"][0][gate0:gate0 + 16].partition_broadcast(P), "wg_in")
            bias_cols = (MH * DK, 0, 2 * MH * DK, 2 * MH * DK + NB, 2 * MH * DK + MH * DV, 2 * MH * DK + MH * DV + NB)

            def load_bias(i):
                load(bias[:, i % 2, :], I["m_in_b"][0][bias_cols[i]:bias_cols[i] + NB].partition_broadcast(P),
                     f"bias_in{i % 2}")

            for i, (hi, src, pair) in enumerate(first_pairs(h_hi, c_hi)):
                act.wait_ge(S("full_x" if src is full else "full_c"), 2 * (i // 4) + i % 2 + 1)
                act.copy(hi[:, pair, :], src[:, pair, :]).then_inc(S("hi"), 1)
                if i == 3:
                    hi_until(2)
            act.wait_ge(S("hi"), KD)
            load_bias(0)
            load_bias(1)
            act.wait_ge(hi_ready, 2)
            load(gp1[:], I["post_mix_g"][0].partition_broadcast(P), "small_in")
            load(gp2[:], I["post_ffn_g"][0].partition_broadcast(P), "small_in")
            hi_until(3)
            act.wait_ge(S("gate_abs"), 1)
            act.activation(sp1[:], sp1[:], ACT.Exp, scale=-1.0).then_inc(S("gate_exp"), 1)
            act.wait_ge(S("gate_exp"), 1)
            act.activation(sp1[:], sp1[:], ACT.Ln, bias=ones[:, 0:1]).then_inc(S("gate_ln"), 1)
            hi_until(4)
            act.wait_ge(S("k_done"), 4)
            load_bias(2)
            hi_until(5)
            act.wait_ge(S("mrow_ready"), 2)
            for d in range(2):
                act.activation(ws_row[:, d, :], ps[0:MH, 4, d * T:(d + 1) * T], ACT.Exp, bias=m_ctx[:, 2 + d:3 + d])\
                    .then_inc(S("ws_row"), 1)
            for d in range(2):
                act.activation(w_row[:, d, :], m_row[:, d, :], ACT.Exp, bias=m_ctx[:, d:d + 1], scale=-1.0)\
                    .then_inc(S("w_row"), 1)
            act.wait_ge(S("q_done"), 2)
            load_bias(3)
            hi_until(6)
            for h in range(MH):
                act.wait_ge(S("qk_T"), h + 1)
                bank = ps[:, 5 + h % 2, :]
                act.activation(qkT[:, h, 0, :], bank[:, 0:T], ACT.Copy, scale=DK ** -0.5).then_inc(S("qkT_ready"), 1)
                act.copy(qkT[:, h, 1, :], bank[:, T:2 * T]).then_inc(S("qkT_ready"), 1)
            act.wait_ge(S("mt_ready"), 1)
            act.activation(emt[:], emt[:], ACT.Exp, scale=-1.0).then_inc(S("emt_ready"), 1)
            hi_until(7)

            def decay(h):
                for d in range(2):
                    act.wait_ge(S("z_ready"), 2 * (2 * h + d) + 2)
                    act.activation(prob[:, h, d, :], prob[:, h, d, :], ACT.Exp, scale=-1.0).then_inc(S("decay_ready"), 1)

            def state_out(h):
                for d in range(2):
                    act.wait_ge(S("state_mm"), 2 * h + d + 1)
                    act.copy(state[:, h, d, :], ps[:, 4 + 2 * (h % 2) + d, 0:DV + 1]).then_inc(S("state_out"), 1)

            decay(0)
            hi_until(8)
            act.wait_ge(S("v_done"), 4)
            load_bias(4)
            hi_until(9)
            decay(1)
            hi_until(10)
            decay(2)
            hi_until(11)
            act.wait_ge(S("v_done"), 8)
            load_bias(5)
            decay(3)
            hi_until(12)
            state_out(0)
            state_out(1)
            hi_until(13)

            def gate_o(n):
                for t in range(TT):
                    act.wait_ge(S("o_done"), TT * n + t + 1)
                    o = so[:, t, n * NB:(n + 1) * NB]
                    act.activation(o, o, ACT.Sigmoid).then_inc(S("so_ready"), 1)

            def head_squares(h):
                for t in range(TT):
                    act.wait_ge(S("h_sum"), TT * h + t + 1)
                    sum_sq(hsum[:, t, h * DV:(h + 1) * DV], SS["head"] + TT * h + t)

            state_out(2)
            state_out(3)
            hi_until(14)
            gate_o(0)
            gate_o(1)
            hi_until(15)
            for h in range(MH):
                head_squares(h)
            hi_T("y1", scale=lambda k: pcol("m_norm", k))
            post("post1", "mix_out")
            if STOP == "B":
                return
            norm("norm2", 0, True)
            hi_T("norm2", scale=lambda k: mod2[:, KD + k:KD + k + 1], shift=lambda k: mod2[:, k:k + 1])

            for j in range(PAIRS):
                g = at["up"][2 * j]
                hi_until(g + 3)
                act.wait_ge(group_used, g + 1)
                if j >= 2:
                    act.wait_ge(S("act_full"), j - 1)
                for f in range(2):
                    k = 2 * j + f
                    act.activation(cv[:, j % 2, f, :], ps[:, 2 * (j % 3), f * T:(f + 1) * T], ACT.Identity,
                                   bias=pcol("conv_b", k), scale=pcol("conv_w", KF + k)).then_inc(S("conv_mid"), 1)
                hi_until(g + 4)
                act.wait_ge(S("conv_done"), 2 * j + 2)
                act.activation(cv[:, j % 2], cv[:, j % 2], ACT.Silu).then_inc(S("silu_ready"), 1)
                hi_until(g + 5)
                act.wait_ge(S("act_full"), j + 1)
                act.copy(act_hi[:, 2 * j:2 * j + 2, :], actf[:, j % 2]).then_inc(S("act_hi_ready"), 1)
            post("post2", "down")
            if STOP == "D":
                return

            norm("norm3", 4, True)
            load(wsm[:, :, 0:8], I["w_in_2"][0][:, 4 * GH * GD:4 * GH * GD + 2 * GH].rearrange("(k p) n -> p k n", p=P),
                 "small_in")
            f0 = 4 * GH * GD + 2 * GH + 3 * FH * FD
            load(wsm[:, :, 8:16], I["w_in_2"][0][:, f0:f0 + FH].rearrange("(k p) n -> p k n", p=P), "small_in")
            load(gprm[:, 0:4], I["dt_bias_2"][0].partition_broadcast(P), "small_in")
            load(gprm[:, 4:8], I["a_log_2"][0].partition_broadcast(P), "small_in")
            load(gprm[:, 8:16], I["fox_f_bias_2"][0].partition_broadcast(P), "small_in")
            hi_T("norm3", scale=lambda k: pcol("attn_norm", k))
            G0 = at["gdn"][0]
            hi_until(G0 + 3)

            def gdn_mid(j):
                s = at["gdn"][j]
                hi_until(s + 3)
                act.wait_ge(group_used, s + 1)
                for f in range(2):
                    act.activation(r5[:, 2 * j + f, :], ps[:, j % 2, f * T:(f + 1) * T], ACT.Copy,
                                   scale=pcol("conv2", 36 + 2 * j + f)).then_inc(S("conv2_mid"), 1)

            def gdn_silu(j):
                for f in (2 * j, 2 * j + 1):
                    act.wait_ge(S("conv2_done"), f + 1)
                    act.activation(r5[:, f, :], r5[:, f, :], ACT.Silu).then_inc(S("conv2_silu"), 1)

            gdn_mid(0)
            act.wait_ge(S("gate_abs"), 2)
            act.activation(sp2[:], sp2[:], ACT.Exp, scale=-1.0).then_inc(S("gate_exp"), 1)
            act.activation(gprm[:, 4:8], gprm[:, 4:8], ACT.Exp).then_inc(S("gate_exp"), 1)
            act.wait_ge(S("gate_exp"), 3)
            act.wait_ge(S("beta_ready"), 1)
            act.activation(sp2[:], sp2[:], ACT.Ln, bias=ones[:, 0:1]).then_inc(S("gate_ln"), 1)

            def fsum_out(i):
                act.wait_ge(S("fsum_mm"), i + 1)
                act.activation(neg_c[:, 2 * i:2 * i + 2, :], ps[:, 7, :].rearrange("p (b t) -> p b t", b=2), ACT.Copy,
                               scale=-1.0).then_inc(S("neg_c_out"), 1)

            def token_squares(i):
                act.wait_ge(S("tok_T"), i + 1)
                if i >= 2:
                    act.wait_ge(S("ss_l2"), i - 1)
                act.activation(sq[:, i % 2, :], ps[:, (4, 5, 6, 4)[i], :], ACT.Square).then_inc(S("sq_ready"), 1)

            def fox_evac(m):
                s, j = at["fox"][m], FOX_ORDER[m]
                hi_until(s + 3)
                act.wait_ge(group_used, s + 1)
                act.copy(foxT[:, 2 * j:2 * j + 2, :], ps[:, m if m < 2 else 3, :].rearrange("p (f t) -> p f t", f=2))\
                    .then_inc(S("fox_T"), 2)

            def bank_out(dst, bank, want, func=None):
                if func is None:
                    act.copy(dst, ps[:, bank, :]).then_inc(S(want), 1)
                else:
                    act.activation(dst, ps[:, bank, :], func).then_inc(S(want), 1)

            gdn_mid(1)
            for t in range(TT):
                act.wait_ge(S("dec_z"), t + 1)
                d = decT[:, GH * t:GH * (t + 1), :]
                act.activation(d, d, ACT.Exp).then_inc(S("dec_exp"), 1)
            act.wait_ge(S("egc_diff"), 2)
            for i in (0, 2):
                act.activation(egc[:, i, :], egc[:, i, :], ACT.Exp).then_inc(S("egc_exp"), 1)
            gdn_silu(0)
            gdn_silu(1)
            gdn_mid(2)
            gdn_silu(2)
            fsum_out(0)
            hi_until(G0 + 6)
            token_squares(0)
            token_squares(1)
            gdn_mid(3)
            gdn_silu(3)
            fsum_out(1)
            gdn_mid(4)
            gdn_silu(4)
            fsum_out(2)
            hi_until(G0 + 8)
            token_squares(2)
            token_squares(3)
            gdn_mid(5)
            gdn_silu(5)
            fsum_out(3)
            hi_until(at["fox"][0] + 3)
            for h in range(GH):
                act.wait_ge(S("gT_mm"), h + 1)
                act.copy(gT[:, h].rearrange("p a t -> p (a t)"), ps[:, 4 + h, :]).then_inc(S("gT_ready"), 1)
            fox_evac(0)
            fox_evac(1)

            def v_out(t):
                g0 = at["fox_v"][0]
                hi_until(g0 + 3 + t)
                if t == 0:
                    act.wait_ge(S("first_tile"), 1)
                else:
                    act.wait_ge(group_used, g0 + 2)
                bank_out(fox_v[:, t, :], 3, "fox_v_out")

            def z_out(t):
                g0 = at["z"][0]
                hi_until(g0 + 3 + t)
                if t == 0:
                    act.wait_ge(S("first_tile"), 2)
                else:
                    act.wait_ge(group_used, g0 + 2)
                bank_out(zs[:, t, :], 3, "z_out")

            hi_until(at["fox_v"][0] + 3)
            for t in range(TT):
                act.wait_ge(S("invT_T"), t + 1)
                bank_out(inv[:, GH * t:GH * (t + 1), :].rearrange("p h t -> p (h t)"), 4 + t, "inv0_ready")
            act.wait_ge(S("q_expT_mm"), 1)
            bank_out(q_expT[:].rearrange("p h t -> p (h t)"), 6, "q_expT_ready")

            def fox_exp(h):
                act.wait_ge(S("fox_max"), h + 1)
                act.wait_ge(S("logit_masked"), 2 * h + 2)
                for t, part in ((0, slice(0, P)), (1, slice(P, 3 * P))):
                    row = logit[:, h % 2, part]
                    act.activation(row, row, ACT.Exp, bias=fsum[:, h % 2, t:t + 1],
                                   accum_out=fsum[:, h % 2, 2 + t:3 + t]).then_inc(S("prob2_ready"), 1)

            def prT_out(h):
                act.wait_ge(S("prT_mm"), h + 1)
                if h >= 2:
                    act.wait_ge(S("fox_mm"), h - 1)
                act.copy(prT[:, h % 2, :], ps[:, 1, 0:3 * P]).then_inc(S("prT_ready"), 1)

            between = (lambda: v_out(1), lambda: fox_evac(2), lambda: fox_evac(3), lambda: z_out(0), lambda: z_out(1),
                       lambda: None)
            fox_exp(0)
            v_out(0)
            for i in range(len(LEVELS)):
                for t in range(TT):
                    act.wait_ge(S("xs_mm"), TT * i + t + 1)
                    if i:
                        act.wait_ge(S("y_mm"), TT * (i - 1) + t + 1)
                    bank_out(xs[:, GH * t:GH * (t + 1), :].rearrange("p h t -> p (h t)"), 4 + t, "xs_ready")
                prT_out(i)
                fox_exp(i + 1)
                between[i]()
            fox_exp(len(LEVELS) + 1)
            prT_out(len(LEVELS))
            for t in range(TT):
                act.activation(zs[:, t, :], zs[:, t, :], ACT.Silu).then_inc(S("z_silu"), 1)
            hi_until(at["z"][0] + 5)
            act.wait_ge(S("u_mm"), 1)
            bank_out(u_tok[:, 0, :], 4, "u_out")
            act.wait_ge(S("u_mm"), 2)
            bank_out(u_tok[:, 1, :], 5, "u_out")
            act.wait_ge(S("w_mm"), 1)
            bank_out(wT, 6, "wT_ready")
            act.wait_ge(S("st_mm"), 1)
            bank_out(st1, 7, "st_ready")
            prT_out(len(LEVELS) + 1)
            order = [*range(KD // 2, KD), *range(KD // 2)]
            for t in range(TT):
                act.wait_ge(S("o_mm"), t + 1)
                for h in range(GH):
                    sum_sq(ps[:, t, h * GD:(h + 1) * GD], SS["gdn"] + GH * t + h)
            hi_T("mix", 2, scale=lambda k: pcol("gdn_norm", 0) if k < GH else None, order=order)
            hi_until(at["att_out"][1] + 4)
            if STOP == "E":
                return
            norm("norm4", 8, False)
            load(p_tok[:], I["p_2"][0, 0].rearrange("(t p) n -> p t n", p=P), "last_in")
            load(gp3[:], I["final_norm_w_2"].partition_broadcast(P), "last_in")
            hi_T("norm4", scale=lambda k: pcol("ffn_norm", k))
            for j in range(PAIRS):
                g = at["gate_up"][2 * j]
                hi_until(g + 3)
                act.wait_ge(group_used, g + 1)
                if j >= 2:
                    act.wait_ge(S("act_full"), PAIRS + j - 1)
                act.activation(sil[:, j % 2], ps[:, 2 * (j % 3), :].rearrange("p (f t) -> p f t", f=2), ACT.Silu)\
                    .then_inc(S("silu_ready"), 1)
                hi_until(g + 5)
                act.wait_ge(S("act_full"), PAIRS + j + 1)
                act.copy(act2_hi[:, 2 * j:2 * j + 2, :], actf2[:, j % 2]).then_inc(S("act_hi_ready"), 1)
            act.wait_ge(S("pT_ready"), 1)
            act.copy(p_hi[:], pT[:]).then_inc(S("p_hi"), 1)
            hi_until(at["down2"][1] + 6 + 2)
            norm("norm5", 12, False)
            hi_until(at["ple_p"][0] + 3)
            act.wait_ge(group_used, at["ple_p"][0] + 1)
            for n in range(2):
                for t in range(TT):
                    bank_out(pgate[:, t, n * NB:(n + 1) * NB], 2 * n + t, "p_out")
            hi_T("norm5", 4, scale=lambda k: pcol("ple_norm", k))
            for n in range(2):
                hi_until(at["ple_g"][n] + 4)
                for t in range(TT):
                    i = TT * n + t
                    if t == 0:
                        act.wait_ge(S("ple_mm"), n + 1)
                    else:
                        act.wait_ge(group_used, at["ple_g"][n] + 2)
                    if i >= 2:
                        act.wait_ge(S("x_upd"), 16 + i - 1)
                    bank_out(tmp[:, i % 2, :], i, "sig_ready", ACT.Sigmoid)
            norm("final", 16, False)


        @block.vector
        def _(dve):
            link = chained(dve, "dve_chain")
            s_next, a_next = [0], [0]

            def ada2_group():
                i = a_next[0]
                v, n, half = i // 4, i // 2 % 2, i % 2
                acc = ada_acc[v][:, n * NB:(n + 1) * NB]
                raw_arrived(dve, ada2[i])
                for k in range(4):
                    w, c = raw_view(ada2[i])[:, k, :], cpad[:, 4 * half + k, 0:1]
                    if half == 0 and k == 0:
                        ins = dve.tensor_scalar(acc, w, c, None, ALU.mult)
                    else:
                        ins = dve.scalar_tensor_tensor(acc, w, c, acc, ALU.mult, ALU.add)
                    if k < 3:
                        link(ins)
                ins.then_inc(ada2_used, 1)
                dve.wait_ge(ada2_used, i + 1)
                a_next[0] += 1

            def lo_until(n):
                while s_next[0] < min(n, n_split):
                    s = s_next[0]
                    while a_next[0] < len(ada2) and ada2[a_next[0]] < split[s]:
                        ada2_group()
                    dve.wait_ge(hi_ready, s + 1)
                    dve.tensor_tensor(part_view(w_lo, s), raw_view(split[s]), part_view(w_hi, s).bitcast(F32),
                                      ALU.subtract).then_inc(lo_ready, 1)
                    s_next[0] += 1

            def lo_part(lo, src, hi, want):
                dve.tensor_tensor(lo, src, hi.bitcast(F32), ALU.subtract).then_inc(S(want), 1)

            def transposed(name, scale=None, shift=None, bank0=0, order=range(KD)):
                for i, k in enumerate(order):
                    dve.wait_ge(S("hi"), base("hi", name) + i + 1)
                    src, hi = ps[:, bank0 + i % 4, 0:T], h_hi[:, k, :].bitcast(F32)
                    a = scale(k) if scale else None
                    if shift:
                        link(dve.tensor_scalar(full[:, k, :], src, a, shift(k), ALU.mult, ALU.add))
                        src, a = full[:, k, :], None
                    if a is None:
                        ins = dve.tensor_tensor(h_lo[:, k, :], src, hi, ALU.subtract)
                    else:
                        ins = dve.scalar_tensor_tensor(h_lo[:, k, :], src, a, hi, ALU.mult, ALU.subtract)
                    ins.then_inc(S("hT"), 1)

            def diagonal(name):
                dve.wait_ge(S("rstd"), base("rstd", name) + 1)
                for t in range(TT):
                    c = SS[name] + t
                    dve.tensor_scalar(diag[:, t, :], ident[:], rstd[:, c:c + 1], None, ALU.mult).then_inc(S("diag"), 1)

            def post_residual(name, gain):
                for n in range(2):
                    for t in range(TT):
                        dve.wait_ge(S("ss"), base("ss", name) + TT * n + t + 1)
                        c = slice(n * NB, (n + 1) * NB)
                        link(dve.tensor_tensor(yg[:, t, c], ps[:, 4 + 2 * n + t, :], gain[:, c], ALU.mult))
                dve.wait_ge(S("rstd"), base("rstd", name) + 1)
                for t in range(TT):
                    for n in range(2):
                        c = slice(n * NB, (n + 1) * NB)
                        r = SS[name] + t
                        dve.scalar_tensor_tensor(x[:, t, c], yg[:, t, c], rstd[:, r:r + 1], x[:, t, c], ALU.mult, ALU.add)\
                            .then_inc(S("x_upd"), 1)

            def residual(name, nk=2, banks=(4, 6)):
                for n in range(2):
                    lo_until(at[name][n] + nk + 2)
                    dve.wait_ge(group_used, at[name][n] + nk)
                    c = slice(n * NB, (n + 1) * NB)
                    for t in range(TT):
                        dve.tensor_tensor(x[:, t, c], x[:, t, c], ps[:, banks[n] + t, :], ALU.add).then_inc(S("x_upd"), 1)

            def ada1_rows(n):
                dve.wait_ge(ada1_used, 2 * n + 2)
                dve.tensor_copy(ada_rows[:, n, :], ps[:, n % 2, :]).then_inc(S("ada_rows"), 1)

            def first_diagonals(c):
                dve.wait_ge(S("rstd"), c + 1)
                for t in (TT * c, TT * c + 1):
                    dve.tensor_scalar(diag[:, t, :], ident[:], rstd[:, t:t + 1], None, ALU.mult).then_inc(S("diag"), 1)

            ada1_rows(0)
            first_diagonals(0)
            ada1_rows(1)
            first_diagonals(1)
            for i in range(4):
                dve.wait_ge(S("tr"), 4 + i + 1)
                dve.tensor_copy(cfull[:, 2 * i:2 * i + 2, :], ps[:, 2 + i, :].rearrange("p (k t) -> p k t", k=2))\
                    .then_inc(S("ctx_out"), 1)
            dve.wait_ge(S("vec_T"), 4)
            dve.tensor_copy(cols[:], ps[:, 7, 2 * KD:2 * KD + n_col]).then_inc(S("cols_ready"), 1)
            ada1_rows(2)
            lo_until(1)
            ada1_rows(3)
            dve.wait_ge(S("ada_T"), 4)
            dve.wait_ge(S("cols_ready"), 1)
            link(dve.tensor_tensor(mod[:], ps[:, 6, 0:4 * KD].rearrange("p (j c) -> p j c", c=2),
                                   cols[:, col["ada_b"]:col["ada_b"] + 2 * KD].unsqueeze(2).to_broadcast([P, 2 * KD, 2]),
                                   ALU.add))
            gain = cols[:, col["pre_mix"]:col["pre_mix"] + KD].unsqueeze(2).to_broadcast([P, KD, 2])
            dve.scalar_tensor_tensor(mod[:, KD:], mod[:, KD:], 1.0, gain, ALU.add, ALU.mult).then_inc(S("mod_ready"), 1)
            dve.wait_ge(S("mod_ready"), 1)
            pending = []
            for i, (lo, src, pair) in enumerate(first_pairs(h_lo, c_lo)):
                if src is full:
                    for k in (pair.start, pair.start + 1):
                        ins = dve.tensor_scalar(full[:, k, :], full[:, k, :], mod[:, KD + k, 0:1], mod[:, k, 0:1],
                                                ALU.mult, ALU.add)
                        if k == pair.start:
                            link(ins)
                    ins.then_inc(S("full_x"), 1)
                pending.append((lo, src, h_hi if src is full else c_hi, pair))
                if i:
                    lo, src, hi, pair = pending[i - 1]
                    dve.wait_ge(S("hi"), i)
                    lo_part(lo[:, pair, :], src[:, pair, :], hi[:, pair, :], "hT")
            lo, src, hi, pair = pending[-1]
            dve.wait_ge(S("hi"), KD)
            lo_part(lo[:, pair, :], src[:, pair, :], hi[:, pair, :], "hT")
            lo_until(2)

            dve.wait_ge(S("gate_mm"), 1)
            dve.wait_ge(S("wg_in"), 32)
            link(dve.tensor_tensor(gate[:], ps[:, 4, 0:2 * TT * 16].rearrange("p (t g) -> p t g", t=2 * TT),
                                   bg[:].unsqueeze(1).to_broadcast([P, 2 * TT, 16]), ALU.add))
            dve.scalar_tensor_tensor(sp1[:], gate_v[:, :, 1, :], -1.0, gate_v[:, :, 1, :], ALU.mult, ALU.max).then_inc(S("gate_abs"), 1)
            lo_until(3)
            dve.wait_ge(S("gate_ln"), 1)
            dve.scalar_tensor_tensor(lf[:], gate_v[:, :, 1, :], 0.0, sp1[:], ALU.min, ALU.subtract).then_inc(S("lf_ready"), 1)
            lo_until(4)

            def bias_of(i):
                dve.wait_ge(S(f"bias_in{i % 2}"), 16 * (i // 2 + 1))
                return bias[:, i % 2, :]

            dve.wait_ge(group_used, at["k"][0] + 2)
            for i, dst in enumerate((qk_tok[:, 1, 0, :], qk_tok[:, 1, 1, :], k_ctx[:, 0, :], k_ctx[:, 1, :])):
                dve.tensor_tensor(dst, ps[:, i, :], bias_of(0), ALU.add).then_inc(S("k_done"), 1)
            lo_until(5)
            dve.wait_ge(S("cum_mm"), 1)
            n_td = TT * 2
            link(dve.tensor_copy(b_col[:], ps[:, 4, 0:16].rearrange("p (a h) -> p a h", h=MH)))
            dve.tensor_tensor(u_col[:], gate_v[:, 0:n_td, 0, :], b_col[:], ALU.subtract).then_inc(S("u_ready"), 1)
            dve.tensor_tensor(gs_col[:], ps[:, 4, 16:32].rearrange("p (a h) -> p a h", h=MH), gate_v[:, n_td:, 0, :],
                              ALU.add).then_inc(S("u_ready"), 1)
            dve.tensor_copy(b_ctx[:], ps[0:MH, 4, 32:34]).then_inc(S("u_ready"), 1)
            dve.wait_ge(group_used, at["q"][0] + 2)
            for t in range(TT):
                dve.tensor_tensor(qk_tok[:, 0, t, :], ps[:, 5 + t, :], bias_of(1), ALU.add).then_inc(S("q_done"), 1)
            dve.wait_ge(S("u_rows"), 1)
            link(dve.tensor_copy(u_row, ps[0:MH, 7, :].rearrange("p (d t) -> p d t", d=2)))
            link(dve.tensor_reduce(m_ctx[:, 0:2], ps[0:MH, 4, :].rearrange("p (d t) -> p d t", d=2), AX_X, ALU.max))
            link(dve.tensor_tensor(m_ctx[:, 0:2], m_ctx[:, 0:2], b_ctx[:], ALU.max))
            link(dve.tensor_scalar(m_ctx[:, 2:4], m_ctx[:, 0:2], -1.0, None, ALU.mult))
            dve.tensor_tensor_scan(m_row[:, 0, :], u_row[:, 0, :], u_row[:, 0, :], m_ctx[:, 0:1], ALU.max, ALU.max)\
                .then_inc(S("mrow_ready"), 1)
            dve.tensor_tensor_scan(m_row[:, 1, ::-1], u_row[:, 1, ::-1], u_row[:, 1, ::-1], m_ctx[:, 1:2], ALU.max, ALU.max)\
                .then_inc(S("mrow_ready"), 1)
            lo_until(6)
            dve.wait_ge(S("m_cols"), 1)
            dve.tensor_tensor(emt[:], ps[:, 7, 0:16].rearrange("p (a h) -> p a h", h=MH), b_col[:], ALU.add)\
                .then_inc(S("mt_ready"), 1)
            dve.tensor_copy(ws_col[:], ps[:, 7, 16:32].rearrange("p (a h) -> p a h", h=MH)).then_inc(S("ws_out"), 1)
            link(dve.memset(vaug[:, :, :, DV:DV + 1], 1.0))

            def exponents(h):
                for d in range(2):
                    dve.wait_ge(S("m_bcast"), 2 * h + d + 1)
                    pr = prob[:, h, d, :]
                    one = slice(P, T) if d == 0 else slice(0, P)
                    for part, tt, tok in ((slice(0, T), d, slice(0, T)), (slice(T, 3 * P), 1 - d, one)):
                        dve.tensor_scalar(pr[:, part], ps[:, 5 + d, tok], u_col[:, 2 * tt + d, h:h + 1], 0.0,
                                          ALU.subtract, ALU.max).then_inc(S("z_ready"), 1)
                    dve.tensor_tensor(qTw[:, h, d, :], qkT[:, h, 0, :], ps[:, 5 + d, T:2 * T], ALU.mult)\
                        .then_inc(S("qTw_ready"), 1)

            def weigh_scores(h):
                dve.wait_ge(S("score_mm"), h + 1)
                bank = (4, 7)[h % 2]
                for d in range(2):
                    dve.wait_ge(S("decay_ready"), 2 * h + d + 1)
                    pr = prob[:, h, d, :]
                    link(dve.tensor_tensor(pr[:, 0:T], pr[:, 0:T], ps[:, bank, d * T:(d + 1) * T], ALU.mult))
                    one = (1 - d) * T + (1 - d) * P
                    dve.tensor_tensor(pr[:, T:], pr[:, T:], ps[:, bank, one:one + P], ALU.mult).then_inc(S("prob_full"), 1)

            def v_evac(n):
                dve.wait_ge(group_used, at["v"][n] + 2)
                for i in range(2 * TT):
                    dve.tensor_tensor(vaug[:, i, 2 * n:2 * n + 2, 0:DV], ps[:, i, :].rearrange("p (h e) -> p h e", h=2),
                                      bias_of(2 + n).rearrange("p (h e) -> p h e", h=2), ALU.add).then_inc(S("v_done"), 1)

            lo_until(7)
            v_evac(0)
            exponents(0)
            lo_until(8)
            weigh_scores(0)
            lo_until(9)
            exponents(1)
            weigh_scores(1)
            lo_until(10)
            exponents(2)
            v_evac(1)
            weigh_scores(2)
            lo_until(11)
            exponents(3)
            weigh_scores(3)
            lo_until(12)

            def o_evac(n):
                dve.wait_ge(group_used, at["o"][n] + 2)
                for t in range(TT):
                    dve.tensor_tensor(so[:, t, n * NB:(n + 1) * NB], ps[:, 2 * n + t, :], bias_of(4 + n), ALU.add)\
                        .then_inc(S("o_done"), 1)

            def head_out(h):
                if h == 0:
                    dve.wait_ge(S("emt_ready"), 1)
                dve.wait_ge(S("out_mm"), h + 1)
                num_den = ps[:, 4:8, DV].rearrange("p (d t) -> p d t", d=2)
                by_d = den[:, 0, :].rearrange("p (d t) -> p d t", d=2)
                floor = emt[:].rearrange("p (t d) h -> p d t h", d=2)[:, :, :, h]
                link(dve.scalar_tensor_tensor(by_d, num_den, -1.0, floor, ALU.mult, ALU.max))
                link(dve.tensor_tensor(by_d, by_d, num_den, ALU.max))
                link(dve.reciprocal(den[:, 1, :], den[:, 0, :]))
                for t in range(TT):
                    hs = hsum[:, t, h * DV:(h + 1) * DV]
                    link(dve.tensor_scalar(hs, ps[:, 4 + t, 0:DV], den[:, 1, t:t + 1], None, ALU.mult))
                    dve.scalar_tensor_tensor(hs, ps[:, 6 + t, 0:DV], den[:, 1, TT + t:TT + t + 1], hs, ALU.mult, ALU.add)\
                        .then_inc(S("h_sum"), 1)

            def times_gate(bank, gp):
                for n in range(2):
                    c = slice(n * NB, (n + 1) * NB)
                    dve.tensor_tensor(gp[:, c], gp[:, c], ps[:, bank + n, :], ALU.mult).then_inc(S("mods_out"), 1)

            def gated_head(h):
                dve.wait_ge(S("so_ready"), 4)
                dve.wait_ge(S("rstd"), base("rstd", "head") + h + 1)
                for t in range(TT):
                    c = slice(h * DV, (h + 1) * DV)
                    r = SS["head"] + TT * h + t
                    dve.scalar_tensor_tensor(ymix[:, t, c], hsum[:, t, c], rstd[:, r:r + 1], so[:, t, c], ALU.mult, ALU.mult)\
                        .then_inc(S("y1_ready"), 1)

            lo_until(13)
            o_evac(0)
            lo_until(14)
            o_evac(1)
            head_out(0)
            dve.wait_ge(S("small_in"), 32)
            dve.wait_ge(S("ada_sum"), 1)
            times_gate(0, gp1)
            head_out(1)
            dve.wait_ge(S("ada_sum"), 2)
            bias2 = cols[:, col["ada_b"] + 3 * KD:col["ada_b"] + 5 * KD]
            link(dve.tensor_tensor(mod2[:], ps[:, 2, 0:2 * KD], bias2, ALU.add))
            dve.scalar_tensor_tensor(mod2[:, KD:], mod2[:, KD:], 1.0, cols[:, col["pre_ffn"]:col["pre_ffn"] + KD],
                                     ALU.add, ALU.mult).then_inc(S("mods_out"), 1)
            head_out(2)
            lo_until(15)
            gated_head(0)
            gated_head(1)
            head_out(3)
            gated_head(2)
            gated_head(3)
            transposed("y1", lambda k: pcol("m_norm", k))
            lo_until(at["mix_out"][1] + 4)
            post_residual("post1", gp1)
            if STOP == "B":
                return
            diagonal("norm2")
            transposed("norm2", lambda k: mod2[:, KD + k:KD + k + 1], lambda k: mod2[:, k:k + 1])

            def up_half(j):
                return ps[:, 2 * (j % 3) + 1, :].rearrange("p (f t) -> p f t", f=2)

            for j in range(PAIRS):
                g = at["up"][2 * j]
                lo_until(g + 3)
                for f in range(2):
                    k = 2 * j + f
                    dve.wait_ge(S("conv_mid"), 2 * j + 2)
                    rows = cv[:, j % 2, f, :].rearrange("p (r w) -> p r w", w=GRID_W)
                    src = ps[:, 2 * (j % 3), f * T:(f + 1) * T].rearrange("p (r w) -> p r w", w=GRID_W)
                    link(dve.scalar_tensor_tensor(rows[:, :, 1:], src[:, :, :-1], pcol("conv_w", k), rows[:, :, 1:],
                                                  ALU.mult, ALU.add))
                    dve.scalar_tensor_tensor(rows[:, :, :-1], src[:, :, 1:], pcol("conv_w", 2 * KF + k), rows[:, :, :-1],
                                             ALU.mult, ALU.add).then_inc(S("conv_done"), 1)
                lo_until(g + 4)
                dve.wait_ge(S("silu_ready"), j + 1)
                dve.wait_ge(group_used, g + 2)
                dve.tensor_tensor(actf[:, j % 2], cv[:, j % 2], up_half(j), ALU.mult).then_inc(S("act_full"), 1)
                lo_until(g + 5)
                dve.wait_ge(S("act_hi_ready"), j + 1)
                pair = slice(2 * j, 2 * j + 2)
                lo_part(act_lo[:, pair, :], actf[:, j % 2], act_hi[:, pair, :], "act_lo")
            lo_until(at["down"][1] + 2)
            dve.wait_ge(S("ada_sum"), 3)
            times_gate(0, gp2)
            lo_until(at["down"][1] + 6)
            post_residual("post2", gp2)
            if STOP == "D":
                return

            lo_until(at["down"][1] + 6 + 1)
            diagonal("norm3")
            transposed("norm3", lambda k: pcol("attn_norm", k))
            G0 = at["gdn"][0]

            def gdn(j):
                lo_until(at["gdn"][j] + 3)
                dve.wait_ge(S("conv2_mid"), 2 * j + 2)
                for f in (2 * j, 2 * j + 1):
                    for back in (1, 2, 3):
                        src = ps[:, j % 2, (f % 2) * T:(f % 2) * T + T - back]
                        ins = dve.scalar_tensor_tensor(r5[:, f, back:], src, pcol("conv2", 12 * (3 - back) + f),
                                                       r5[:, f, back:], ALU.mult, ALU.add)
                        if back < 3:
                            link(ins)
                    ins.then_inc(S("conv2_done"), 1)

            gdn(0)
            dve.wait_ge(S("sgate_mm"), 1)
            dve.wait_ge(S("small_in"), 16 * 7)
            pre = ps[:, 4, 0:TT * 16].rearrange("p (t g) -> p t g", t=TT)
            for c in (slice(0, GH), slice(2 * GH, 16)):
                link(dve.tensor_tensor(sm[:, :, c], pre[:, :, c],
                                       gprm[:, c].unsqueeze(1).to_broadcast([P, TT, c.stop - c.start]), ALU.add))
                link(dve.scalar_tensor_tensor(sp2[:, :, c], sm[:, :, c], -1.0, sm[:, :, c], ALU.mult, ALU.max))
            dve.tensor_copy(sp2[:, :, GH:2 * GH], pre[:, :, GH:2 * GH]).then_inc(S("gate_abs"), 1)
            dve.wait_ge(S("gate_exp"), 3)
            link(dve.tensor_scalar(beta[:], sp2[:, :, GH:2 * GH], 1.0, None, ALU.add))
            dve.reciprocal(beta[:], beta[:]).then_inc(S("beta_ready"), 1)
            dve.wait_ge(S("gate_ln"), 2)
            link(dve.scalar_tensor_tensor(g_dec[:], sm[:, :, 0:GH], 0.0, sp2[:, :, 0:GH], ALU.max, ALU.add))
            dve.scalar_tensor_tensor(g_dec[:], g_dec[:], -1.0, gprm[:, GH:2 * GH].unsqueeze(1).to_broadcast([P, TT, GH]),
                                     ALU.mult, ALU.mult).then_inc(S("sgate_ready"), 1)
            dve.scalar_tensor_tensor(lf2[:], sm[:, :, 2 * GH:], 0.0, sp2[:, :, 2 * GH:], ALU.min, ALU.subtract)\
                .then_inc(S("sgate_ready"), 1)

            def heads(a):
                return a.rearrange("p (h n) -> p h n", h=GH)

            def per_head(a):
                return a.unsqueeze(2).to_broadcast([P, GH, GD])

            def token_norm(i):
                a, t = i // 2, i % 2
                c = SS["l2"] + GH * i
                dve.wait_ge(S("sq_ready"), i + 1)
                dve.tensor_reduce(ss[:, c:c + GH], heads(sq[:, i % 2, :]), AX_X, ALU.add).then_inc(S("ss_l2"), 1)
                dve.wait_ge(S("rstd_l2"), i + 1)
                dve.tensor_tensor(heads(qk_n[:, a, t, :]), heads(ps[:, (4, 5, 6, 4)[i], :]), per_head(rstd[:, c:c + GH]),
                                  ALU.mult).then_inc(S("tok_out"), 1)

            gdn(1)
            dve.wait_ge(S("decay_mm"), 1)
            link(dve.tensor_copy(gc[:], ps[:, 4, 0:3 * GH].rearrange("p (a h) -> p a h", h=GH)))
            dve.tensor_copy(egc[:, 0, :], gc[:, 1, :]).then_inc(S("egc_diff"), 1)
            dve.tensor_tensor(egc[:, 2, :], gc[:, 2, :], gc[:, 0, :], ALU.subtract).then_inc(S("egc_diff"), 1)
            for t in range(TT):
                dve.wait_ge(S("decay_mm"), 1 + t + 1)
                for h in range(GH):
                    ins = dve.tensor_scalar(decT[:, GH * t + h, :], ps[:, 5 + t, h * P:(h + 1) * P], gc[:, t, h:h + 1], 0.0,
                                            ALU.subtract, ALU.min)
                    if h < GH - 1:
                        link(ins)
                ins.then_inc(S("dec_z"), 1)
            dve.wait_ge(S("egc_exp"), 2)
            dve.tensor_tensor(egc[:, 1, :], egc[:, 0, :], beta[:, 1, :], ALU.mult).then_inc(S("egc_ready"), 1)
            gdn(2)
            lo_until(G0 + 6)
            token_norm(0)
            token_norm(1)
            gdn(3)
            gdn(4)
            lo_until(G0 + 8)
            token_norm(2)
            token_norm(3)
            gdn(5)

            def all_heads(a, t):
                return a[:, GH * t:GH * (t + 1), :]

            def bank(b):
                return heads(ps[:, b, :])

            lo_until(at["fox"][1] + 3)
            dve.wait_ge(S("dec_ready"), TT)
            for t in range(TT):
                dve.wait_ge(S("kk_mm"), t + 1)
                link(dve.tensor_tensor(all_heads(cT, t), bank(4 + t), all_heads(decT, t), ALU.mult))
            for t in range(TT):
                dve.wait_ge(S("beta_mm"), t + 1)
                dve.tensor_tensor(all_heads(cT, t), all_heads(cT, t), bank(2 + t), ALU.mult).then_inc(S("cT_full"), 1)
            dve.wait_ge(S("level_ready"), 1)
            dve.wait_ge(S("cT_full"), TT)
            for t in range(TT):
                d = all_heads(invT, t)
                link(dve.tensor_tensor(d, all_heads(cT, t), level[:, 0, :].unsqueeze(1).to_broadcast([P, GH, P]), ALU.mult))
                dve.tensor_tensor(d, ident[:].unsqueeze(1).to_broadcast([P, GH, P]), d, ALU.subtract)\
                    .then_inc(S("inv_ready"), 1)
            for t in range(TT):
                dve.wait_ge(S("kk_mm"), TT + t + 1)
                dve.tensor_tensor(all_heads(qkT2, t), bank(6 + t), all_heads(decT, t), ALU.mult)\
                    .then_inc(S("qkT2_ready"), 1)
            for t in range(TT):
                dve.wait_ge(S("tok_T"), 4 + t + 1)
                dve.tensor_tensor(heads(vb[:, t, :]), heads(ps[:, 2 + t, :]), per_head(beta[:, t, :]), ALU.mult)\
                    .then_inc(S("tok_out"), 1)
            lo_until(at["fox_v"][0] + 3)

            def fox_logits(h):
                dve.wait_ge(S("logit_mm"), h + 1)
                if h >= 2:
                    dve.wait_ge(S("prT_mm"), h - 1)
                for t, part in ((0, slice(0, P)), (1, slice(P, 3 * P))):
                    dve.scalar_tensor_tensor(logit[:, h % 2, part], ps[:, 0, part], FD ** -0.5,
                                             neg_c[:, h, 0:(t + 1) * P], ALU.mult, ALU.add).then_inc(S("logit_ready"), 1)

            def fox_max(h):
                dve.wait_ge(S("logit_masked"), 2 * h + 2)
                for t, part in ((0, slice(0, P)), (1, slice(P, 3 * P))):
                    link(dve.tensor_reduce(fsum[:, h % 2, t:t + 1], logit[:, h % 2, part], AX_X, ALU.max))
                dve.tensor_scalar(fsum[:, h % 2, 0:2], fsum[:, h % 2, 0:2], -1.0, None, ALU.mult).then_inc(S("fox_max"), 1)

            def fox_done(h):
                dve.wait_ge(S("fox_mm"), h + 1)
                link(dve.reciprocal(fsum[:, h % 2, 2:4], fsum[:, h % 2, 2:4]))
                for t in range(TT):
                    c = GH * GD + FD * h
                    dve.tensor_scalar(mix[:, t, c:c + FD], ps[:, 2, t * FD:(t + 1) * FD], fsum[:, h % 2, 2 + t:3 + t], None,
                                      ALU.mult).then_inc(S("fox_done"), 1)

            fox_logits(0)
            fox_max(0)
            lo_next = (at["fox_v"][0] + 4, at["fox"][2] + 3, at["fox"][3] + 3, at["z"][0] + 3, at["z"][0] + 4, at["z"][0] + 4)
            for i in range(len(LEVELS)):
                fox_logits(i + 1)
                if i == 1:
                    dve.wait_ge(S("q_exp_ready"), 1)
                    dve.wait_ge(S("k_beta_ready"), 1)
                    dve.wait_ge(S("k_dec_ready"), 1)
                    dve.wait_ge(S("gT_mm"), GH)
                if i:
                    fox_done(i - 1)
                for t in range(TT):
                    dve.wait_ge(S("y_mm"), TT * i + t + 1)
                    if i < len(LEVELS) - 1:
                        link(dve.tensor_tensor(all_heads(inv, t), all_heads(inv, t), bank(6 + t), ALU.subtract))
                    dve.tensor_tensor(all_heads(invT, t), all_heads(invT, t), bank(4 + t), ALU.subtract)\
                        .then_inc(S("inv_ready"), 1)
                fox_max(i + 1)
                lo_until(lo_next[i])
            h = len(LEVELS)
            fox_logits(h + 1)
            fox_done(h - 1)
            fox_max(h + 1)
            fox_done(h)
            fox_done(h + 1)
            dve.wait_ge(S("u_out"), 2)
            dve.wait_ge(S("ws_mm"), 1)
            dve.tensor_tensor(v_new, u_tok[:, 1, :], ps[:, 6, :], ALU.subtract).then_inc(S("v_new_ready"), 1)
            dve.wait_ge(S("z_silu"), TT)
            for t in range(TT):
                dve.wait_ge(S("rstd"), base("rstd", "gdn") + t + 1)
                c = SS["gdn"] + GH * t
                link(dve.tensor_tensor(heads(og[:, t, :]), bank(t), per_head(rstd[:, c:c + GH]), ALU.mult))
                dve.tensor_tensor(mix[:, t, 0:GH * GD], og[:, t, :], zs[:, t, :], ALU.mult).then_inc(S("mix_ready"), 1)
            transposed("mix", lambda k: pcol("gdn_norm", 0) if k < GH else None,
                       bank0=2, order=[*range(KD // 2, KD), *range(KD // 2)])
            residual("att_out", banks=(6, 0))
            if STOP == "E":
                return
            diagonal("norm4")
            transposed("norm4", lambda k: pcol("ffn_norm", k))
            for j in range(PAIRS):
                g = at["gate_up"][2 * j]
                lo_until(g + 4)
                dve.wait_ge(S("silu_ready"), PAIRS + j + 1)
                dve.wait_ge(group_used, g + 2)
                dve.tensor_tensor(actf2[:, j % 2], sil[:, j % 2], up_half(j), ALU.mult).then_inc(S("act_full"), 1)
                lo_until(g + 5)
                dve.wait_ge(S("act_hi_ready"), PAIRS + j + 1)
                pair = slice(2 * j, 2 * j + 2)
                lo_part(act2_lo[:, pair, :], actf2[:, j % 2], act2_hi[:, pair, :], "act_lo")
            dve.wait_ge(S("p_T"), 1)
            dve.tensor_copy(pT[:].rearrange("p k t -> p (k t)"), ps[:, 6, :]).then_inc(S("pT_ready"), 1)
            dve.wait_ge(S("p_hi"), 1)
            lo_part(p_lo[:], pT[:], p_hi[:], "p_lo")
            residual("down2", 6)
            lo_until(at["ple_p"][0] + 3)
            diagonal("norm5")
            transposed("norm5", lambda k: pcol("ple_norm", k), bank0=4)
            lo_until(n_split)
            dve.wait_ge(S("p_out"), 4)
            for n in range(2):
                for t in range(TT):
                    i = TT * n + t
                    c = slice(n * NB, (n + 1) * NB)
                    dve.wait_ge(S("sig_ready"), i + 1)
                    link(dve.tensor_tensor(pgate[:, t, c], pgate[:, t, c], tmp[:, i % 2, :], ALU.mult))
                    dve.tensor_tensor(x[:, t, c], x[:, t, c], pgate[:, t, c], ALU.add).then_inc(S("x_upd"), 1)
            dve.wait_ge(S("last_in"), 32)
            for t in range(TT):
                dve.wait_ge(S("rstd"), base("rstd", "final") + t + 1)
                dve.scalar_tensor_tensor(pgate[:, t, :], x[:, t, :], rstd[:, SS["final"] + t:SS["final"] + t + 1], gp3[:], ALU.mult, ALU.mult)\
                    .then_inc(S("result"), 1)

        @block.tensor
        def _(pe):
            def mm3(dst, left, right, first, last):
                (l_hi, l_lo), (r_hi, r_lo) = left, right
                pe.matmul(dst, l_hi, r_hi, start=first, stop=False)
                pe.matmul(dst, l_hi, r_lo, start=False, stop=False)
                return pe.matmul(dst, l_lo, r_hi, start=False, stop=last)

            def weights(s):
                pe.wait_ge(lo_ready, s + 1)
                return part_view(w_hi, s), part_view(w_lo, s)

            def token_group(s, g0, nk, source, ready=None, first=0):
                a_hi, a_lo, t, bank = source
                hi, lo = part_view(w_hi, s), part_view(w_lo, s)
                tok = slice(t * P, (t + 1) * P)
                k0 = (4 * (s - g0) + first) % nk if first else 4 * (s - g0)
                for i, k in enumerate(range(k0, min(k0 + 4, nk))):
                    if ready is not None:
                        ready(k, t)
                    ins = mm3(ps[:, bank, :], (a_hi[:, k, tok], a_lo[:, k, tok]), (hi[:, i, :], lo[:, i, :]),
                              s == g0 and i == 0, 4 * (s - g0) + i == nk - 1)
                return ins

            def token_block(g0, sources, nk=KD, after_first=None, ready=None, free=None, done=None, first=0):
                last = g0 + (nk + 3) // 4 - 1
                for s in range(g0, last + 1):
                    weights(s)
                    for i, source in enumerate(sources):
                        if free is not None and s == g0:
                            free(i)
                        ins = token_group(s, g0, nk, source, ready, first)
                        if done is not None and s == last and i < len(sources) - 1:
                            ins.then_inc(S(done), 1)
                    ins.then_inc(group_used, 1)
                    if after_first is not None and s == g0:
                        after_first()

            def feature_tiles(s, bank):
                hi, lo = weights(s)
                for f in range(2):
                    fs_ = slice(f * P, (f + 1) * P)
                    for k in range(KD):
                        ins = mm3(ps[:, bank, f * T:(f + 1) * T], (hi[:, k, fs_], lo[:, k, fs_]),
                                  (h_hi[:, k, :], h_lo[:, k, :]), k == 0, k == KD - 1)
                ins.then_inc(group_used, 1)

            def transposed(name, src, by_diag, bank0=0, ready=None, order=range(KD)):
                for i, k in enumerate(order):
                    if i >= 4:
                        pe.wait_ge(S("hT"), base("hT", name) + i - 3)
                    if ready is not None:
                        ready(k)
                    for t in range(TT):
                        if by_diag and i == 0:
                            pe.wait_ge(S("diag"), base("diag", name) + t + 1)
                        dst = ps[:, bank0 + i % 4, t * P:(t + 1) * P]
                        if by_diag:
                            ins = pe.matmul(dst, src[:, t, k * P:(k + 1) * P], diag[:, t, :], start=True, stop=True)
                        else:
                            ins = pe.transpose(dst, src[:, t, k * P:(k + 1) * P], ident[:])
                    ins.then_inc(S("tr"), 1)

            def hT(name, first=0):
                return lambda k, t: pe.wait_ge(S("hT"), base("hT", name) + (k + first) % KD + 1) if t == 0 else None

            def flip(dst, src):
                n = src.shape[0]
                return pe.transpose(dst, src, ident[0:n, 0:n])

            X0, X1 = (h_hi, h_lo, 0), (h_hi, h_lo, 1)
            C0, C1 = (c_hi, c_lo, 0), (c_hi, c_lo, 1)

            pe.wait_ge(S("const_ready"), 1)
            pe.wait_ge(S("c_in"), 32)
            flip(ps[:, 7, 0:2 * KD], c_rows[:]).then_inc(S("vec_T"), 1)

            def ada1_group(i):
                n, half = i // 2, i % 2
                raw_arrived(pe, ada1[i])
                if half == 0 and n >= 2:
                    pe.wait_ge(S("ada_rows"), n - 1)
                for kk in range(4):
                    ins = pe.matmul(ps[32 * kk:32 * kk + 32, n % 2, :], cpad[:, 4 * half + kk, :],
                                    raw_view(ada1[i])[:, kk, :], start=half == 0, stop=half == 1)
                ins.then_inc(ada1_used, 1)

            def ada1_columns(n):
                if n == 0:
                    pe.wait_ge(S("const_ready"), 2)
                pe.wait_ge(S("ada_rows"), n + 1)
                for j in range(4 * n, 4 * n + 4):
                    ins = pe.matmul(ps[:, 6, 2 * j:2 * j + 2], ada_rows[:, n, (j % 4) * P:(j % 4 + 1) * P], row_of[:],
                                    start=True, stop=True)
                ins.then_inc(S("ada_T"), 1)

            def first_transposed(c, i):
                if c:
                    pe.wait_ge(S("x_out"), i + 1)
                for k in (2 * i, 2 * i + 1):
                    for t in range(TT):
                        if i == 0 and k == 0:
                            pe.wait_ge(S("diag"), TT * c + t + 1)
                        dst = ps[:, 2 + i, k % 2 * T + t * P:k % 2 * T + (t + 1) * P]
                        ins = pe.matmul(dst, (ctx_tok if c else x)[:, t, k * P:(k + 1) * P], diag[:, TT * c + t, :],
                                        start=True, stop=True)
                ins.then_inc(S("tr"), 1)

            pe.wait_ge(S("c_ready"), 1)
            for i in range(8):
                ada1_group(i)
                if i >= 2 and i % 2 == 0:
                    ada1_columns(i // 2 - 1)
                if i == 2:
                    for pair in range(4):
                        first_transposed(0, pair)
                if i in (4, 5):
                    for pair in (2 * (i - 4), 2 * (i - 4) + 1):
                        first_transposed(1, pair)
                if i == 5:
                    pe.wait_ge(S("vec_in"), 16 * (len(VEC) + 3))
                    at_col = 2 * KD
                    for rows in vec_rows:
                        n = rows.shape[0]
                        flip(ps[:, 7, at_col:at_col + n], rows).then_inc(S("vec_T"), 1)
                        at_col += n
            ada1_columns(3)

            def gates():
                pe.wait_ge(S("hT"), KD)
                pe.wait_ge(S("wg_in"), 32)
                for t in range(2 * TT):
                    src = full if t < TT else cfull
                    for k in range(KD):
                        ins = pe.matmul(ps[:, 4, 16 * t:16 * t + 16], src[:, k, (t % TT) * P:(t % TT + 1) * P], wg[:, k, :],
                                        start=k == 0, stop=k == KD - 1)
                ins.then_inc(S("gate_mm"), 1)

            every = [(*X0, 0), (*X1, 1), (*C0, 2), (*C1, 3)]
            pairs = {id(h_hi): (1, 2, 5, 6), id(c_hi): (3, 4, 7, 8)}
            g0 = at["k"][0]
            for s in (g0, g0 + 1):
                weights(s)
                for source in every:
                    ins = token_group(s, g0, KD, source,
                                      lambda k, t: pe.wait_ge(S("hT"), pairs[id(source[0])][k // 2]) if t == 0 else None)
                ins.then_inc(group_used, 1)
                if s == g0:
                    gates()

            pe.wait_ge(S("lf_ready"), 1)

            def lf_of(tile, d):
                return lf[:, 2 * tile + d, :]

            for a in range(2):
                for t in range(TT):
                    for d in range(2):
                        dst = ps[:, 4, 16 * a + 8 * t + 4 * d:16 * a + 8 * t + 4 * d + 4]
                        tri = ((s_le_t, s_ge_t), (s_gt_t, s_lt_t))[a][d]
                        other = t != (a + d) % 2
                        pe.matmul(dst, tri[:], lf_of(TT * a + t, d), start=True, stop=not other)
                        if other:
                            pe.matmul(dst, ones[:], lf_of(TT * a + 1 - t, d), start=False, stop=True)
            for d in range(2):
                for t in range(TT):
                    ins = pe.matmul(ps[0:MH, 4, 32 + d:33 + d], lf_of(TT + t, d), ones[:, 0:1], start=t == 0, stop=t == 1)
            ins.then_inc(S("cum_mm"), 1)

            def exponent_rows():
                pe.wait_ge(S("u_ready"), 3)
                for bank, src in ((7, u_col), (4, gs_col)):
                    for t in range(TT):
                        for d in range(2):
                            ins = flip(ps[0:MH, bank, d * T + t * P:d * T + (t + 1) * P], src[:, 2 * t + d, :])
                ins.then_inc(S("u_rows"), 1)

            token_block(at["q"][0], [(*X0, 5), (*X1, 6)], after_first=exponent_rows)

            def qk_by_channel():
                pe.wait_ge(S("k_done"), 4)
                pe.wait_ge(S("q_done"), 2)
                for h in range(MH):
                    if h >= 2:
                        pe.wait_ge(S("qkT_ready"), 2 * (h - 1))
                    for a in range(2):
                        for t in range(TT):
                            ins = flip(ps[:, 5 + h % 2, a * T + t * P:a * T + (t + 1) * P],
                                       qk_tok[:, a, t, h * DK:(h + 1) * DK])
                    ins.then_inc(S("qk_T"), 1)
                pe.wait_ge(S("mrow_ready"), 2)
                pe.wait_ge(S("ws_row"), 2)
                for i, src in enumerate((m_row, ws_row)):
                    for t in range(TT):
                        for d in range(2):
                            c = 16 * i + 8 * t + 4 * d
                            ins = flip(ps[:, 7, c:c + 4], src[:, d, t * P:(t + 1) * P])
                ins.then_inc(S("m_cols"), 1)

            def scores(h):
                if h == 0:
                    pe.wait_ge(S("w_row"), 2)
                    pe.wait_ge(S("qkT_ready"), 2 * MH)
                if h == 1:
                    pe.wait_ge(S("ws_out"), 1)
                if h >= 2:
                    pe.wait_ge(S("prob_full"), 2 * (h - 1))
                for t in range(TT):
                    ins = pe.matmul(ps[:, (4, 7)[h % 2], t * T:(t + 1) * T], qkT[:, h, 1, t * P:(t + 1) * P], qkT[:, h, 0, :],
                                    start=True, stop=True)
                ins.then_inc(S("score_mm"), 1)
                for d in range(2):
                    if h:
                        pe.wait_ge(S("qTw_ready"), 2 * (h - 1) + d + 1)
                    pe.matmul(ps[:, 5 + d, 0:T], sel[:, h, :], m_row[:, d, :], start=True, stop=True)
                    pe.matmul(ps[:, 5 + d, T:2 * T], sel[:, h, :], w_row[:, d, :], start=True, stop=True)\
                        .then_inc(S("m_bcast"), 1)

            pe.wait_ge(S("k_done"), 4)
            token_block(at["v"][0], every, after_first=qk_by_channel)
            scores(0)
            token_block(at["v"][1], every, after_first=lambda: scores(1),
                        free=lambda i: pe.wait_ge(S("v_done"), i + 1))
            scores(2)

            def ctx_state(h):
                pe.wait_ge(S("kw_ready"), h + 1)
                pe.wait_ge(S("v_done"), 8)
                if h < 2:
                    pe.wait_ge(S("prob_full"), 2 * (h + 3))
                    pe.wait_ge(S("qTw_ready"), 2 * MH)
                if h >= 2:
                    pe.wait_ge(S("state_out"), 2 * (h - 1))
                for d in range(2):
                    for t in range(TT):
                        ins = pe.matmul(ps[:, 4 + 2 * (h % 2) + d, 0:DV + 1], kw[:, h % 2, t, d, :], vaug[:, TT + t, h, :],
                                        start=t == 0, stop=t == 1)
                    ins.then_inc(S("state_mm"), 1)

            def outputs(h):
                pe.wait_ge(S("prob_ready"), 2 * h + 2)
                pe.wait_ge(S("state_out"), 2 * MH)
                if h:
                    pe.wait_ge(S("h_sum"), 2 * h)
                for d in range(2):
                    pr = prob[:, h, d, :]
                    for t in range(TT):
                        dst = ps[:, 4 + 2 * d + t, 0:DV + 1]
                        pe.matmul(dst, qTw[:, h, d, t * P:(t + 1) * P], state[:, h, d, :], start=True, stop=False)
                        if t != d:
                            pe.matmul(dst, pr[:, T:T + P], vaug[:, 1 - d, h, :], start=False, stop=False)
                        ins = pe.matmul(dst, pr[:, t * P:(t + 1) * P], vaug[:, d, h, :], start=False, stop=True)
                ins.then_inc(S("out_mm"), 1)

            def gate_vector(v, bank):
                for n in range(2):
                    pe.matmul(ps[:, bank + n, :], ones[:], ada_acc[v][:, n * NB:(n + 1) * NB], start=True, stop=False)
                    for j in range(4):
                        c = col["ada_b"] + (2 + v) * KD + 4 * n + j
                        ins = pe.matmul(ps[:, bank + n, j * P:(j + 1) * P], cols[:, c:c + 1].to_broadcast([P, P]), ident[:],
                                        start=False, stop=j == 3)
                ins.then_inc(S("ada_sum"), 1)

            def out_states(h):
                ctx_state(h)
                ctx_state(h + 1)

            token_block(at["o"][0], [(*X0, 0), (*X1, 1)], free=lambda i: pe.wait_ge(S("v_done"), 4 + i + 1),
                        after_first=lambda: scores(3))
            out_states(0)
            token_block(at["o"][1], [(*X0, 2), (*X1, 3)], free=lambda i: pe.wait_ge(S("v_done"), 6 + i + 1),
                        after_first=lambda: out_states(2))
            outputs(0)
            pe.wait_ge(S("o_done"), 2)
            pe.wait_ge(ada2_used, len(ada2) - 4)
            gate_vector(0, 0)
            outputs(1)
            pe.wait_ge(S("o_done"), 3)
            for j in range(2 * KD):
                ins = pe.matmul(ps[:, 2, j:j + 1], ada_acc[1 + j // KD][:, (j % KD) * P:(j % KD + 1) * P], ones[:, 0:1],
                                start=True, stop=True)
            ins.then_inc(S("ada_sum"), 1)
            outputs(2)
            outputs(3)
            pe.wait_ge(S("o_done"), 4)
            pe.wait_ge(S("mods_out"), 3)
            transposed("y1", ymix, False, ready=lambda k: pe.wait_ge(S("y1_ready"), TT * (k // 2 + 1)))
            pe.wait_ge(S("h_sum"), 2 * MH)
            for n in range(2):
                token_block(at["mix_out"][n], [(*X0, 4 + 2 * n), (*X1, 5 + 2 * n)], ready=hT("y1") if n == 0 else None)
            if STOP == "B":
                return

            done = {"up": 0, "gate_up": PAIRS}

            def ffn(name, norm):
                pe.wait_ge(S("hT"), base("hT", norm) + KD)
                for j in range(PAIRS):
                    if j >= 3:
                        pe.wait_ge(S("act_full"), done[name] + j - 2)
                    for half in range(2):
                        feature_tiles(at[name][2 * j + half], 2 * (j % 3) + half)

            def second(name, first, hi, lo, before_last=None):
                pe.wait_ge(S("act_full"), done[first] + PAIRS - 2)
                for n in range(2):
                    token_block(at[name][n], [(hi, lo, 0, 4 + 2 * n), (hi, lo, 1, 5 + 2 * n)], nk=KF,
                                ready=lambda k, t: pe.wait_ge(S("act_lo"), done[first] + k // 2 + 1) if not n and not t else None)
                    if n == 0 and before_last is not None:
                        before_last()

            def gate2():
                pe.wait_ge(ada2_used, len(ada2))
                pe.wait_ge(S("act_full"), PAIRS)
                gate_vector(3, 0)

            transposed("norm2", x, True)
            ffn("up", "norm2")
            second("down", "up", act_hi, act_lo, gate2)
            if STOP == "D":
                return

            transposed("norm3", x, True)
            def small_gates():
                pe.wait_ge(S("full_ready"), 4)
                pe.wait_ge(S("small_in"), 16 * 7)
                for t in range(TT):
                    for k in range(KD):
                        ins = pe.matmul(ps[:, 4, 16 * t:16 * t + 16], full[:, k, t * P:(t + 1) * P], wsm[:, k, :],
                                        start=k == 0, stop=k == KD - 1)
                ins.then_inc(S("sgate_mm"), 1)

            def gdn_tiles(j):
                if j >= 2:
                    pe.wait_ge(S("conv2_done"), 2 * (j - 1))
                feature_tiles(at["gdn"][j], j % 2)

            def to_tokens(i, t, bank):
                pe.wait_ge(S("conv2_silu"), 4 * i + 4)
                for h in range(GH):
                    ins = flip(ps[:, bank, h * GD:(h + 1) * GD], r5[:, 4 * i + h, t * P:(t + 1) * P])
                ins.then_inc(S("tok_T"), 1)

            def decay_sums():
                pe.wait_ge(S("sgate_ready"), 1)
                for t in range(TT):
                    pe.matmul(ps[:, 4, 4 * t:4 * t + 4], s_le_t[:], g_dec[:, t, :], start=True, stop=True)
                pe.matmul(ps[:, 4, 8:12], ones[:], g_dec[:, 0, :], start=True, stop=True).then_inc(S("decay_mm"), 1)
                for t in range(TT):
                    for h in range(GH):
                        ins = pe.matmul(ps[:, 5 + t, h * P:(h + 1) * P], g_dec[:, t, h:h + 1].to_broadcast([P, P]),
                                        s_le_t[:], start=True, stop=True)
                    ins.then_inc(S("decay_mm"), 1)

            def forget_sums(i):
                if i == 0:
                    pe.wait_ge(S("sgate_ready"), 2)
                else:
                    pe.wait_ge(S("neg_c_out"), i)
                for b in range(2):
                    f0, f1 = (lf2[:, t, 2 * i + b:2 * i + b + 1].to_broadcast([P, P]) for t in range(TT))
                    c = b * T
                    pe.matmul(ps[:, 7, c:c + P], f0, s_le_t[:], start=True, stop=True)
                    pe.matmul(ps[:, 7, c + P:c + T], f0, ones[:], start=True, stop=False)
                    ins = pe.matmul(ps[:, 7, c + P:c + T], f1, s_le_t[:], start=False, stop=True)
                ins.then_inc(S("fsum_mm"), 1)

            pe.wait_ge(S("hT"), base("hT", "norm3") + 4)
            def fox_tiles(m):
                if m < 2:
                    pe.wait_ge(S("conv2_done"), 8 + 2 * (m + 1))
                elif m == 2:
                    pe.wait_ge(S("fox_v_out"), TT)
                else:
                    pe.wait_ge(S("fox_T"), 2 * m)
                feature_tiles(at["fox"][m], m if m < 2 else 3)

            pe.wait_ge(S("hT"), base("hT", "norm3") + KD)
            gdn_tiles(0)
            small_gates()
            gdn_tiles(1)
            decay_sums()
            gdn_tiles(2)
            forget_sums(0)
            pe.wait_ge(S("dec_z"), TT)
            to_tokens(0, 0, 4)
            to_tokens(0, 1, 5)
            gdn_tiles(3)
            forget_sums(1)
            gdn_tiles(4)
            forget_sums(2)
            to_tokens(1, 0, 6)
            pe.wait_ge(S("tok_out"), 1)
            to_tokens(1, 1, 4)
            gdn_tiles(5)
            forget_sums(3)

            pe.wait_ge(S("tok_out"), 4)
            pe.wait_ge(S("neg_c_out"), 4)
            for h in range(GH):
                for a in range(2):
                    for t in range(TT):
                        ins = flip(ps[:, 4 + h, a * T + t * P:a * T + (t + 1) * P], qk_n[:, a, t, h * GD:(h + 1) * GD])
                ins.then_inc(S("gT_mm"), 1)
            fox_tiles(0)
            pe.wait_ge(S("gT_ready"), GH)
            for a, bank in ((1, 4), (0, 6)):
                for t in range(TT):
                    tok = slice(t * P, (t + 1) * P)
                    for h in range(GH):
                        ins = pe.matmul(ps[:, bank + t, h * P:(h + 1) * P], gT[:, h, 1, tok], gT[:, h, a, tok],
                                        start=True, stop=True)
                    ins.then_inc(S("kk_mm"), 1)
            for t in range(TT):
                for h in range(GH):
                    ins = pe.matmul(ps[:, 2 + t, h * P:(h + 1) * P], beta[:, t, h:h + 1].to_broadcast([P, P]), ident[:],
                                    start=True, stop=True)
                ins.then_inc(S("beta_mm"), 1)
            fox_tiles(1)
            pe.wait_ge(S("cT_full"), TT)
            to_tokens(2, 0, 2)
            to_tokens(2, 1, 3)

            def by_token(name, t):
                g0 = at[name][0]
                for s in (g0, g0 + 1):
                    weights(s)
                    ins = token_group(s, g0, KD, (h_hi, h_lo, t, 3))
                    if t == 1:
                        ins.then_inc(group_used, 1)
                if t == 0:
                    ins.then_inc(S("first_tile"), 1)

            def fox_v_tile(t):
                if t == 0:
                    pe.wait_ge(S("tok_out"), 6)
                else:
                    pe.wait_ge(S("fox_v_out"), 1)
                by_token("fox_v", t)

            def z_tile(t):
                if t == 0:
                    pe.wait_ge(S("fox_T"), 8)
                else:
                    pe.wait_ge(S("z_out"), 1)
                by_token("z", t)

            def fox_logits(h):
                if h == 0:
                    pe.wait_ge(S("fox_T"), 4)
                else:
                    pe.wait_ge(S("logit_ready"), 2 * h)
                if h == FH // 2:
                    pe.wait_ge(S("fox_T"), 8)
                row = slice(FD * (h % 2), FD * (h % 2) + FD)
                q, k = foxT[row, h // 2, :], foxT[row, FH // 2 + h // 2, :]
                pe.matmul(ps[:, 0, 0:P], q[:, 0:P], k[:, 0:P], start=True, stop=True)
                pe.matmul(ps[:, 0, P:3 * P], q[:, P:T], k, start=True, stop=True).then_inc(S("logit_mm"), 1)

            def fox_transpose(h):
                pe.wait_ge(S("prob2_ready"), 2 * h + 2)
                if h:
                    pe.wait_ge(S("prT_ready"), h)
                for i in range(3):
                    ins = flip(ps[:, 1, i * P:(i + 1) * P], logit[:, h % 2, i * P:(i + 1) * P])
                ins.then_inc(S("prT_mm"), 1)

            def fox_out(h):
                pe.wait_ge(S("prT_ready"), h + 1)
                if h == 0:
                    pe.wait_ge(S("fox_v_out"), TT)
                else:
                    pe.wait_ge(S("fox_done"), 2 * h)
                v = fox_v[:, :, h * FD:(h + 1) * FD]
                pe.matmul(ps[:, 2, 0:FD], prT[:, h % 2, 0:P], v[:, 0], start=True, stop=True)
                pe.matmul(ps[:, 2, FD:2 * FD], prT[:, h % 2, P:2 * P], v[:, 0], start=True, stop=False)
                pe.matmul(ps[:, 2, FD:2 * FD], prT[:, h % 2, 2 * P:], v[:, 1], start=False, stop=True)\
                    .then_inc(S("fox_mm"), 1)

            def fox_step(i):
                if i < FH:
                    fox_logits(i)
                if 1 <= i <= FH:
                    fox_transpose(i - 1)
                if 2 <= i <= FH + 1:
                    fox_out(i - 2)

            fox_step(0)
            for t in range(TT):
                pe.wait_ge(S("inv_ready"), t + 1)
                for h in range(GH):
                    ins = flip(ps[:, 4 + t, h * P:(h + 1) * P], invT[:, GH * t + h, :])
                ins.then_inc(S("invT_T"), 1)
            pe.wait_ge(S("q_exp_ready"), 1)
            pe.wait_ge(S("qkT2_ready"), TT)
            for h in range(GH):
                ins = flip(ps[:, 6, h * P:(h + 1) * P], q_exp[:, h * GD:(h + 1) * GD])
            ins.then_inc(S("q_expT_mm"), 1)
            fox_v_tile(0)
            between = (lambda: fox_v_tile(1), lambda: fox_tiles(2), lambda: fox_tiles(3), lambda: z_tile(0),
                       lambda: z_tile(1), lambda: fox_step(len(LEVELS) + 1))
            for i in range(len(LEVELS)):
                last = i == len(LEVELS) - 1
                pe.wait_ge(S("cTl_ready"), i + 1)
                for t in range(TT):
                    pe.wait_ge(S("inv_ready"), TT * i + t + 1)
                    if i == 0:
                        pe.wait_ge(S("inv0_ready"), t + 1)
                    for h in range(GH):
                        a = GH * t + h
                        ins = pe.matmul(ps[:, 4 + t, h * P:(h + 1) * P], cTl[:, i % 2, a, :], inv[:, a, :],
                                        start=True, stop=True)
                    ins.then_inc(S("xs_mm"), 1)
                fox_step(i + 1)
                for t in range(TT):
                    pe.wait_ge(S("xs_ready"), TT * i + t + 1)
                    if i == 0 and t == 0:
                        pe.wait_ge(S("q_expT_ready"), 1)
                    if not last:
                        for h in range(GH):
                            a = GH * t + h
                            pe.matmul(ps[:, 6 + t, h * P:(h + 1) * P], invT[:, a, :], xs[:, a, :], start=True, stop=True)
                    for h in range(GH):
                        a = GH * t + h
                        ins = pe.matmul(ps[:, 4 + t, h * P:(h + 1) * P], xs[:, a, :], invT[:, a, :], start=True, stop=True)
                    ins.then_inc(S("y_mm"), 1)
                between[i]()
            for t in range(TT):
                pe.wait_ge(S("inv_ready"), TT * len(LEVELS) + t + 1)
                pe.wait_ge(S("inv_ready"), TT * (len(LEVELS) + 1))
                for h in range(GH):
                    ins = pe.matmul(ps[:, 4 + t, h * P:(h + 1) * P], invT[:, GH * t + h, :], vb[:, t, h * GD:(h + 1) * GD],
                                    start=True, stop=True)
                ins.then_inc(S("u_mm"), 1)
            pe.wait_ge(S("k_beta_ready"), 1)
            for h in range(GH):
                ins = pe.matmul(ps[:, 6, h * P:(h + 1) * P], k_beta[:, h * GD:(h + 1) * GD], invT[:, GH + h, :],
                                start=True, stop=True)
            ins.then_inc(S("w_mm"), 1)
            pe.wait_ge(S("k_dec_ready"), 1)
            pe.wait_ge(S("u_out"), 1)
            for h in range(GH):
                hs = slice(h * GD, (h + 1) * GD)
                ins = pe.matmul(ps[:, 7, hs], k_dec[:, hs], u_tok[:, 0, hs], start=True, stop=True)
            ins.then_inc(S("st_mm"), 1)
            fox_step(len(LEVELS) + 2)
            fox_step(len(LEVELS) + 3)
            pe.wait_ge(S("logit_ready"), 2 * FH)
            for h in range(GH):
                hs = slice(h * GD, (h + 1) * GD)
                ins = pe.matmul(ps[:, 0, hs], qkT2[:, h, :], u_tok[:, 0, hs], start=True, stop=True)
            ins.then_inc(S("o_mm"), 1)
            pe.wait_ge(S("st_ready"), 1)
            pe.wait_ge(S("wT_ready"), 1)
            for h in range(GH):
                hs = slice(h * GD, (h + 1) * GD)
                ins = pe.matmul(ps[:, 6, hs], wT[:, hs], st1[:, hs], start=True, stop=True)
            ins.then_inc(S("ws_mm"), 1)
            pe.wait_ge(S("v_new_ready"), 1)
            for h in range(GH):
                hs = slice(h * GD, (h + 1) * GD)
                pe.matmul(ps[:, 1, hs], q_expT[:, h, :], st1[:, hs], start=True, stop=False)
                ins = pe.matmul(ps[:, 1, hs], qkT2[:, GH + h, :], v_new[:, hs], start=False, stop=True)
            ins.then_inc(S("o_mm"), 1)
            order = [*range(KD // 2, KD), *range(KD // 2)]
            pe.wait_ge(S("z_out"), TT)
            pe.wait_ge(S("u_out"), TT)
            transposed("mix", mix, False, bank0=2, order=order,
                       ready=lambda k: pe.wait_ge(S("mix_ready"), TT) if k < GH else pe.wait_ge(S("fox_done"), TT * FH))
            for n in range(2):
                token_block(at["att_out"][n], [(*X0, (6, 0)[n]), (*X1, (7, 1)[n])],
                            ready=hT("mix", KD // 2) if n == 0 else None, first=KD // 2)
            if STOP == "E":
                return
            pe.wait_ge(S("x_upd"), 12)
            transposed("norm4", x, True)
            ffn("gate_up", "norm4")
            pe.wait_ge(S("last_in"), 32)
            for k in range(2):
                for t in range(TT):
                    ins = flip(ps[:, 6, k * T + t * P:k * T + (t + 1) * P], p_tok[:, t, k * P:(k + 1) * P])
            ins.then_inc(S("p_T"), 1)
            second("down2", "gate_up", act2_hi, act2_lo, lambda: pe.wait_ge(S("pT_ready"), 1))
            pe.wait_ge(S("act_full"), 2 * PAIRS)
            pe.wait_ge(S("p_lo"), 1)
            s = at["ple_p"][0]
            hi, lo = weights(s)
            for n in range(2):
                for t in range(TT):
                    for k in range(2):
                        tok, c = slice(t * P, (t + 1) * P), slice(n * NB, (n + 1) * NB)
                        ins = mm3(ps[:, 2 * n + t, :], (p_hi[:, k, tok], p_lo[:, k, tok]), (hi[:, k, c], lo[:, k, c]),
                                  k == 0, k == 1)
            ins.then_inc(group_used, 1)
            pe.wait_ge(S("x_upd"), 16)
            transposed("norm5", x, True, bank0=4)
            pe.wait_ge(S("p_out"), 4)
            for n in range(2):
                token_block(at["ple_g"][n], [(*X0, 2 * n), (*X1, 2 * n + 1)], ready=hT("norm5") if n == 0 else None,
                            done="ple_mm")

_INS = ['x', 'c', 'ctx', 'c_ctx', 'ada_w', 'ada_b', 'pre_mix_g', 'post_mix_g', 'pre_ffn_g', 'post_ffn_g', 'ffn_up_w',
        'ffn_conv_w', 'ffn_conv_b', 'ffn_down_w', 'm_in_w', 'm_in_b', 'm_norm_g', 'm_out_w', 'p_2', 'attn_norm_w_2',
        'w_in_2', 'conv_w_2', 'a_log_2', 'dt_bias_2', 'gdn_norm_w_2', 'fox_f_bias_2', 'w_out_2', 'ffn_norm_w_2',
        'w_gate_up_2', 'w_down_2', 'ple_norm_w_2', 'w_ple_gate_2', 'w_ple_proj_2', 'final_norm_w_2']


def kernel(**inputs):
    import numpy as _np
    import concourse.bacc as _bacc
    from concourse import mybir as _mybir
    from concourse.bass_utils import run_bass_kernel_spmd as _run

    nc = _bacc.Bacc("TRN2", target_bir_lowering=False, num_devices=1, dynamic_dma_scratch_size=1024)
    arrays, tensors = {}, {}
    for name in _INS:
        a = _np.ascontiguousarray(inputs[name])
        arrays[f"in_{name}"] = a
        tensors[name] = nc.dram_tensor(f"in_{name}", a.shape, _mybir.dt.from_np(a.dtype), kind="ExternalInput").ap()
    out = nc.dram_tensor("out", (1, T, D), F32, kind="ExternalOutput").ap()
    two_blocks(nc, tensors, out)
    r = _run(nc, [arrays], core_ids=[0])
    return r.results[0]["out"]
```

```python
from contextlib import ExitStack

import concourse.bass as bass
from concourse import mybir

F32 = mybir.dt.float32
F32R = mybir.dt.float32r
ALU = mybir.AluOpType
ACT = mybir.ActivationFunctionType
AX_X = mybir.AxisListType.X

P = 128
T = 256
TT = T // P
D = 1024
KD = D // P
ADA_BANKS = (0, 1, 0, 5)
NB = 512
EPS = 1e-6
RING = 3
GROUP = 2048

MH, DK, DV = 4, 128, 256
FF = 2816
KF = FF // P
PAIRS = KF // 2
ROUND = 3
ROUNDS = PAIRS // ROUND
GRID_W = 64
GH, GD = 4, 128
OUT_BANKS = ((7, 1), (2, 3))
FOX_ORDER = (0, 2, 1, 3)
FH, FD = 8, 64
PLE = 256
LEVELS = (2, 4, 8, 16, 32, 64)
FOX_STEPS = ((1, None), (2, None), (3, 4), (5, 6), (7, 8), (9, None))
NORM_BANKS = {"norm2": (0, 1, 6, 7), "norm3": (0, 1, 2, 3), "norm4": (0, 4, 5, 6), "norm5": (4, 5, 6, 7)}
TOKEN_BANKS = (4, 5, 6, 3)
MIX_PAIRS = (2, 3, 0, 1)
NEG = -1.0e30


def plan_groups(I):
    groups, split, at = [], [], {}

    def add(w, k0, nk, c0, ncol, consumer="split"):
        if consumer == "split":
            split.append(len(groups))
        groups.append((w[k0 * P:(k0 + nk) * P, c0:c0 + ncol].rearrange("(k p) n -> p k n", p=P), nk, ncol, consumer))

    def block(name, w, c0, nk=KD, ada_after=()):
        at.setdefault(name, []).append(len(split))
        for i, k0 in enumerate(range(0, nk, 4)):
            add(w, k0, min(4, nk - k0), c0, NB)
            if i < len(ada_after):
                (ada1 if name == "k" else ada2)(ada_after[i])

    def tiles(name, w, c0):
        at.setdefault(name, []).append(len(split))
        add(w, 0, KD, c0, 2 * P)

    def ada_groups(v0, n_vec):
        return iter([(k0, v * D + n * NB) for v in range(v0, v0 + n_vec) for n in range(D // NB) for k0 in (0, 4)])

    ada_early, ada_late = ada_groups(0, 2), ada_groups(2, 4)

    def ada1(count):
        for _ in range(count):
            k0, c0 = next(ada_early)
            add(I["ada_w"][0], k0, 4, c0, NB, "ada1")

    def ada2(count):
        for _ in range(count):
            k0, c0 = next(ada_late)
            add(I["ada_w"][0], k0, 4, c0, NB, "ada2")

    m_in, w_in = I["m_in_w"][0], I["w_in_2"][0]
    v0, o0 = 2 * MH * DK, 2 * MH * DK + MH * DV
    fox0 = 4 * GH * GD + 2 * GH
    ada1(6)
    block("k", m_in, MH * DK, ada_after=(2,))
    block("q", m_in, 0, ada_after=(1, 1))
    block("v", m_in, v0, ada_after=(1, 2))
    block("v", m_in, v0 + NB, ada_after=(1, 2))
    block("o", m_in, o0, ada_after=(1, 1))
    block("o", m_in, o0 + NB, ada_after=(1, 1))
    for n in range(2):
        block("mix_out", I["m_out_w"][0], n * NB)
    for j in range(PAIRS):
        tiles("up", I["ffn_up_w"][0], FF + 2 * j * P)
        tiles("up", I["ffn_up_w"][0], 2 * j * P)
    for n in range(2):
        block("down", I["ffn_down_w"][0], n * NB, KF, ada_after=(0, 0, 1, 1, 1, 1) if n == 0 else ())
    for j in range(6):
        tiles("gdn", w_in, 2 * j * P)
    for j in FOX_ORDER[:2]:
        tiles("fox", w_in, fox0 + 2 * j * P)
    block("fox_v", w_in, fox0 + 2 * FH * FD)
    for j in FOX_ORDER[2:]:
        tiles("fox", w_in, fox0 + 2 * j * P)
    block("z", w_in, 3 * GH * GD)
    at["att_out"] = [len(split)]
    for k0 in (GH, 0):
        for n in range(2):
            add(I["w_out_2"][0], k0, GH, n * NB, NB)
    for j in range(PAIRS):
        tiles("gate_up", I["w_gate_up_2"][0], 2 * j * P)
        tiles("gate_up", I["w_gate_up_2"][0], FF + 2 * j * P)
    for n in range(2):
        block("down2", I["w_down_2"][0], n * NB, KF)
    at["ple_p"] = [len(split)]
    add(I["w_ple_proj_2"][0], 0, 2, 0, D)
    for n in range(2):
        block("ple_g", I["w_ple_gate_2"][0], n * NB)
    return groups, split, at


def two_blocks(nc, I, out):
    groups, split, at = plan_groups(I)
    ada1 = [g for g, x in enumerate(groups) if x[3] == "ada1"]
    ada2 = [g for g, x in enumerate(groups) if x[3] == "ada2"]
    n_split = len(split)

    with ExitStack() as ctx:
        sems = {}

        def S(name):
            if name not in sems:
                sems[name] = ctx.enter_context(nc.semaphore(name))
            return sems[name]

        FAMILY = {
            "ss": (("norm1", 4), ("head", 8), ("post1", 8), ("post2", 8), ("gdn", 8), ("norm4", 4), ("norm5", 4),
                   ("final", 4)),
            "rstd": (("norm1", 2), ("head", 4), ("post1", 4), ("post2", 4), ("gdn", 2), ("norm4", 2), ("norm5", 2),
                     ("final", 2)),
            "t0_done": (("mix_out", 1), ("down", 1), ("att_out", 1), ("ple_g", 1)),
            "diag": (("norm1", 4), ("norm2", 2), ("norm3", 2), ("norm4", 2), ("norm5", 2)),
        }
        FAMILY["act_full"] = (("up", ROUND + PAIRS), ("gate_up", ROUND + PAIRS))
        for kind in ("conv_mid", "conv_done", "silu_ready", "act_hi_ready", "act_lo"):
            FAMILY[kind] = (("up", PAIRS), ("gate_up", PAIRS))
        for kind, n in (("tr", KD // 2), ("hi", KD), ("hT", KD)):
            FAMILY[kind] = (("norm1", KD), ("y1", n), ("norm2", n), ("norm3", n), ("mix", KD // 2), ("norm4", n),
                            ("norm5", n))
        SS = {"norm1": 0, "head": 4, "post1": 12, "norm2": 16, "post2": 20, "norm3": 24, "l2": 28, "gdn": 44,
              "norm4": 52, "norm5": 56, "final": 60}

        def base(kind, name):
            before = 0
            for stage, n in FAMILY[kind]:
                if stage == name:
                    return before
                before += n

        def sb(scope, name, shape, dt=F32):
            return scope.enter_context(nc.sbuf_tensor(name, shape, dt))

        ps = ctx.enter_context(nc.psum_tensor("ps", [P, 8, NB], F32))
        raw = sb(ctx, "raw", [P, RING, GROUP])
        w_hi = sb(ctx, "w_hi", [P, RING, GROUP], F32R)
        w_lo = sb(ctx, "w_lo", [P, RING, GROUP], F32R)
        x = sb(ctx, "x", [P, TT, D])
        full = sb(ctx, "full", [P, KD, T])
        yg = full[:].rearrange("p k t -> p (k t)").rearrange("p (t n) -> p t n", t=TT)
        h_hi = sb(ctx, "h_hi", [P, KD, T], F32R)
        h_lo = sb(ctx, "h_lo", [P, KD, T], F32R)
        ident = sb(ctx, "ident", [P, P])
        s_le_t = sb(ctx, "s_le_t", [P, P])
        s_ge_t = sb(ctx, "s_ge_t", [P, P])
        s_lt_t = sb(ctx, "s_lt_t", [P, P])
        s_gt_t = sb(ctx, "s_gt_t", [P, P])
        ones = sb(ctx, "ones", [P, P])
        diag = sb(ctx, "diag", [P, 2 * TT, P])
        VEC = (("ada_b", I["ada_b"][0]), ("pre_mix", I["pre_mix_g"][0]),
               ("pre_ffn", I["pre_ffn_g"][0]), ("attn_norm", I["attn_norm_w_2"][0]), ("ffn_norm", I["ffn_norm_w_2"][0]),
               ("ple_norm", I["ple_norm_w_2"][0]), ("m_norm", I["m_norm_g"][0]), ("gdn_norm", I["gdn_norm_w_2"][0]))
        col, n_vec = {}, 0
        for name, src in VEC:
            col[name] = n_vec
            n_vec += src.shape[0] // P
        col["conv_w"], col["conv_b"], col["conv2"] = n_vec, n_vec + 3 * KF, n_vec + 4 * KF
        n_col = n_vec + 4 * KF + 48
        cols = sb(ctx, "cols", [P, n_col])

        def pcol(name, k):
            return cols[:, bass.ds(col[name] + k, 1)]

        c_rows = sb(ctx, "c_rows", [2 * KD, P])
        cpad = sb(ctx, "cpad", [P, KD, 32])
        row_of = sb(ctx, "row_of", [P, 2])
        mod = sb(ctx, "mod", [P, 2 * KD, 2])
        mod2 = sb(ctx, "mod2", [P, 2 * KD])
        mhalf = sb(ctx, "mhalf", [P, 16])
        ss = sb(ctx, "ss", [P, 64])
        rstd = sb(ctx, "rstd", [P, 64])
        wg_parts = sb(ctx, "wg_parts", [P, KD, 32], F32R)
        gate_rows = sb(ctx, "gate_rows", [32, 2 * T])
        fold = sb(ctx, "fold", [32, 16])
        junk = sb(ctx, "junk", [P, D])
        tmp = sb(ctx, "tmp", [P, 2, NB])

        with ExitStack() as b1:
            gp1 = sb(b1, "gp1", [P, D])
            gp2 = sb(b1, "gp2", [P, D])
            acc2 = sb(b1, "acc2", [P, 2, D])
            acc1 = full[:].rearrange("p k t -> p (k t)").rearrange("p (a n) -> p a n", a=2)
            ada_acc = (acc1[:, 0], acc1[:, 1], acc2[:, 0], acc2[:, 1])
            with ExitStack() as mx:
                with ExitStack() as early:
                    c_hi = sb(early, "c_hi", [P, KD, T], F32R)
                    c_lo = sb(early, "c_lo", [P, KD, T], F32R)
                late = sb(mx, "late", [P, MH * 2 * (DV + 1) + TT * D])
                state = late[:, 0:MH * 2 * (DV + 1)].rearrange("p (h d e) -> p h d e", h=MH, d=2)
                hsum = late[:, MH * 2 * (DV + 1):].rearrange("p (t n) -> p t n", t=TT)
                r2 = sb(mx, "r2", [P, TT * D])
                cfull = r2[:].rearrange("p (k t) -> p k t", k=KD)
                qk_tok = r2[:].rearrange("p (a t n) -> p a t n", a=2, t=TT)
                so = r2[:].rearrange("p (t n) -> p t n", t=TT)
                r3 = sb(mx, "r3", [P, 2 * TT * MH * (DV + 1)])
                vaug = r3[:].rearrange("p (t h e) -> p t h e", t=2 * TT, h=MH)
                u_row = r3[0:MH, 2048:2048 + 2 * T].rearrange("p (d t) -> p d t", d=2)
                ws_row = r3[0:MH, 2560:2560 + 2 * T].rearrange("p (d t) -> p d t", d=2)
                ada_rows = r3[:, 0:4 * NB].rearrange("p (n c) -> p n c", n=4)
                vec_rows = (r3[0:n_vec, 2048:2048 + P], r3[0:4 * KF, 2048 + P:2048 + 2 * P],
                            r3[0:48, 2048 + 2 * P:2048 + 3 * P])
                qkT = sb(mx, "qkT", [P, MH, 2, T])
                prob = sb(mx, "prob", [P, MH, 2, 3 * P])
                prob_flat = prob[:].rearrange("p h d n -> p (h d n)")
                ctx_tok = prob_flat[:, 0:TT * D].rearrange("p (t n) -> p t n", t=TT)
                ymix = ctx_tok
                qTw = sb(mx, "qTw", [P, MH, 2, T])
                r4 = sb(mx, "r4", [P, 2 * TT * 2 * P])
                kw = r4[:].rearrange("p (b t d n) -> p b t d n", b=2, t=TT, d=2)
                m_row = junk[0:MH, 0:2 * T].rearrange("p (d t) -> p d t", d=2)
                w_row = junk[0:MH, 2 * T:4 * T].rearrange("p (d t) -> p d t", d=2)
                k_ctx = sb(mx, "k_ctx", [P, TT, NB])
                bias = sb(mx, "bias", [P, 2, NB])
                wg = sb(mx, "wg", [P, KD, 16])
                bg = sb(mx, "bg", [P, 16])
                gate = sb(mx, "gate", [P, 2 * TT, 16])
                gate_v = gate[:].rearrange("p t (d x h) -> p (t d) x h", d=2, x=2)
                lf = sb(mx, "lf", [P, 2 * TT * 2, MH])
                sp1 = sb(mx, "sp1", [P, 2 * TT * 2, MH])
                b_col = sb(mx, "b_col", [P, TT * 2, MH])
                u_col = sb(mx, "u_col", [P, TT * 2, MH])
                gs_col = sb(mx, "gs_col", [P, TT * 2, MH])
                ws_col = sb(mx, "ws_col", [P, TT * 2, MH])
                emt = sb(mx, "emt", [P, TT * 2, MH])
                b_ctx = sb(mx, "b_ctx", [MH, 2])
                m_ctx = sb(mx, "m_ctx", [MH, 4])
                sel = sb(mx, "sel", [MH, MH, P])
                den = sb(mx, "den", [P, 2, 4])
            with ExitStack() as fs:
                act_hi = sb(fs, "act_hi", [P, KF, T], F32R)
                act_lo = sb(fs, "act_lo", [P, KF, T], F32R)
                cv = sb(fs, "cv", [P, ROUND, 2, T])
                actf = sb(fs, "actf", [P, ROUND, 2, T])
        with ExitStack() as b2:
            r5 = sb(b2, "r5", [P, 12, T])
            r5f = r5[:].rearrange("p f t -> p (f t)")
            inv = r5f[:, 0:1024].rearrange("p (a i) -> p a i", i=P)
            invT = r5f[:, 1024:2048].rearrange("p (a i) -> p a i", i=P)
            qk_n = sb(b2, "qk_n", [P, 2, TT, NB])
            mix = qk_n[:].rearrange("p a t n -> p (a t n)").rearrange("p (t n) -> p t n", t=TT)
            vb = sb(b2, "vb", [P, TT, NB])
            k_beta = sb(b2, "k_beta", [P, NB])
            k_dec = sb(b2, "k_dec", [P, NB])
            q_exp = sb(b2, "q_exp", [P, NB])
            q_expT = sb(b2, "q_expT", [P, GH, P])
            gT = sb(b2, "gT", [P, GH, 2, T])
            gTf = gT[:].rearrange("p h a t -> p (h a t)")
            st1 = gTf[:, 0:NB]
            wT = gTf[:, NB:2 * NB]
            v_new = gTf[:, 2 * NB:3 * NB]
            decT = sb(b2, "decT", [P, TT * GH, P])
            u_tok = decT[:].rearrange("p (t h) i -> p t (h i)", t=TT)
            cT = sb(b2, "cT", [P, TT * GH, P])
            cTl = sb(b2, "cTl", [P, 2, TT * GH, P])
            qkT2 = sb(b2, "qkT2", [P, TT * GH, P])
            neg_c = sb(b2, "neg_c", [P, FH, T])
            foxT = sb(b2, "foxT", [P, 8, T])
            fox_v = sb(b2, "fox_v", [P, TT, NB])
            zs = sb(b2, "zs", [P, TT, NB])
            r6 = sb(b2, "r6", [P, 4, 3 * P])
            logit = r6[:, 0:2]
            prT = r6[:, 2:4]
            sq = r6[:].rearrange("p a n -> p (a n)")[:, 0:2 * NB].rearrange("p (t n) -> p t n", t=TT)
            level = sb(b2, "level", [P, 7, P])
            wsm = sb(b2, "wsm", [P, KD, 16])
            sm = sb(b2, "sm", [P, TT, 16])
            gprm = sb(b2, "gprm", [P, 16])
            g_dec = sb(b2, "g_dec", [P, TT, GH])
            beta = sb(b2, "beta", [P, TT, GH])
            lf2 = sb(b2, "lf2", [P, TT, FH])
            sp2 = sb(b2, "sp2", [P, TT, 16])
            gc = sb(b2, "gc", [P, 3, GH])
            egc = sb(b2, "egc", [P, 3, GH])
            fsum = sb(b2, "fsum", [P, 2, 4])
            og = sb(b2, "og", [P, TT, NB])
            xs = og[:].rearrange("p t (h i) -> p (t h) i", i=P)
        with ExitStack() as b3:
            act2_hi = sb(b3, "act2_hi", [P, KF, T], F32R)
            act2_lo = sb(b3, "act2_lo", [P, KF, T], F32R)
            sil = sb(b3, "sil", [P, ROUND, 2, T])
            actf2 = sb(b3, "actf2", [P, ROUND, 2, T])
            p_tok = sb(b3, "p_tok", [P, TT, PLE])
            pT = sb(b3, "pT", [P, 2, T])
            p_hi = sb(b3, "p_hi", [P, 2, T], F32R)
            p_lo = sb(b3, "p_lo", [P, 2, T], F32R)
            gp3 = sb(b3, "gp3", [P, D])
            pgate = sb(b3, "pgate", [P, TT, D])

        raw_in = [S(f"raw_in{i}") for i in range(RING)]
        hi_ready, lo_ready, group_used = S("hi_ready"), S("lo_ready"), S("group_used")
        ada1_used, ada2_used = S("ada1_used"), S("ada2_used")

        def raw_view(g):
            _, nk, ncol, _ = groups[g]
            return raw[:, g % RING, :nk * ncol].rearrange("p (k n) -> p k n", k=nk)

        def part_view(part, s):
            _, nk, ncol, _ = groups[split[s]]
            return part[:, s % RING, :nk * ncol].rearrange("p (k n) -> p k n", k=nk)

        def raw_arrived(eng, g, r=0):
            eng.wait_ge(raw_in[g % RING], 16 * (g // RING + 1) + 16 * (2 * ROUND // RING) * r)

        def in_round(s, r):
            return (s + 2 * ROUND * r, 0) if isinstance(r, int) else (s, r)

        def rounds(eng, step):
            with eng.Fori(0, ROUNDS) as r:
                for u in range(ROUND):
                    step(r, u)
            for u in range(PAIRS - ROUND * ROUNDS):
                step(ROUNDS, u)

        def chained(eng, name):
            count = [0]

            def link(ins):
                count[0] += 1
                ins.then_inc(S(name), 1)
                eng.wait_ge(S(name), count[0])

            return link

        def first_pairs():
            for two in (0, 2):
                for part, whole in ((h_hi, full), (c_hi, cfull)):
                    for i in (two, two + 1):
                        yield part, whole, slice(2 * i, 2 * i + 2)

        block = ctx.enter_context(nc.Block())


        @block.sync
        def _(sp):
            sp.dma_start(c_rows[0:KD, :], I["c"][0].rearrange("(k p) -> k p", p=P)).then_inc(S("c_in"), 16)

            def load(g):
                if g >= RING:
                    old = g - RING
                    consumer = groups[old][3]
                    if consumer == "ada1":
                        sp.wait_ge(ada1_used, ada1.index(old) + 1)
                    elif consumer == "ada2":
                        sp.wait_ge(ada2_used, ada2.index(old) + 1)
                    else:
                        sp.wait_ge(lo_ready, split.index(old) + 1)
                sp.dma_start(raw_view(g), groups[g][0]).then_inc(raw_in[g % RING], 16)

            def loads(name, w, halves):
                def step(r, u):
                    starts = [h + 2 * P * (ROUND * r + u) for h in halves]
                    if r is not ROUNDS:
                        for c0 in starts:
                            sp.lower_val(4 * c0)
                    for half, c0 in enumerate(starts):
                        s, later = in_round(at[name][2 * u + half], r)
                        sp.wait_ge(lo_ready, s - RING + 1 + 2 * ROUND * later)
                        sp.dma_start(raw_view(split[s]), w[:, bass.ds(c0, 2 * P)].rearrange("(k p) n -> p k n", p=P))\
                            .then_inc(raw_in[split[s] % RING], 16)

                rounds(sp, step)

            first, last = split[at["up"][0]], split[at["up"][-1]]
            first2, last2 = split[at["gate_up"][0]], split[at["gate_up"][-1]]
            for g in range(first):
                load(g)
            loads("up", I["ffn_up_w"][0], (FF, 0))
            for g in range(last + 1, first2):
                load(g)
            loads("gate_up", I["w_gate_up_2"][0], (0, FF))
            for g in range(last2 + 1, len(groups)):
                load(g)
            for t in range(TT):
                for n in range(2):
                    c = slice(n * NB, (n + 1) * NB)
                    sp.wait_ge(S(f"result{n}"), t + 1)
                    sp.dma_start(out[0, t * P:(t + 1) * P, c], pgate[:, t, c]).then_inc(S("out_done"), 16)
            sp.wait_ge(S("out_done"), 16 * 2 * TT)

        @block.gpsimd
        def _(pool):
            link = chained(pool, "pool_chain")

            def rms_scale(name, c0, n, scale=1.0, halves=False):
                s = ss[:, c0:c0 + n]
                if halves:
                    link(pool.tensor_scalar(s, s, ss[:, c0 + TT:c0 + TT + 1], EPS, ALU.add, ALU.add))
                else:
                    link(pool.tensor_scalar(s, s, scale, EPS, ALU.mult, ALU.add))
                pool.tensor_tensor(rstd[:, c0:c0 + n], s, mhalf[:, 0:n], ALU.pow).then_inc(S("rstd"), 1)

            def keep(a, op, pattern, channel, fill=0.0, base=0):
                return pool.affine_select(out=a, in_=a, compare_op=op, fill=fill, base=base, pattern=pattern,
                                          channel_multiplier=channel)

            link(pool.memset(ident[:], 0.0))
            link(pool.memset(cpad[:], 0.0))
            keep(ident[:], ALU.not_equal, [[-1, P]], 1, fill=1.0).then_inc(S("const_ready"), 1)
            link(pool.memset(row_of[:], 0.0))
            for m in (s_le_t, s_ge_t, s_lt_t, s_gt_t, ones, sel):
                link(pool.memset(m[:], 1.0))
            link(pool.memset(mhalf[:], -0.5))
            link(pool.memset(fold[:], 0.0))
            for part in range(2):
                link(keep(fold[:], ALU.not_equal, [[-1, 16]], 1, fill=1.0, base=-16 * part))
            for j in range(4):
                link(keep(row_of[:], ALU.not_equal, [[-1, 2]], 1, fill=1.0, base=-32 * j))
            link(keep(s_le_t[:], ALU.is_ge, [[1, P]], -1))
            link(keep(s_ge_t[:], ALU.is_ge, [[-1, P]], 1))
            link(keep(s_lt_t[:], ALU.is_gt, [[1, P]], -1))
            link(keep(s_gt_t[:], ALU.is_gt, [[-1, P]], 1))
            keep(sel[:], ALU.is_equal, [[-1, MH], [0, P]], 1).then_inc(S("const_ready"), 1)

            for i in range(2):
                pool.wait_ge(S("ss"), TT * (i + 1))
                rms_scale("norm1", SS["norm1"] + TT * i, TT)

            for k in range(KD):
                if k % 4 == 0:
                    pool.wait_ge(S("mod_ready"), k // 4 + 1)
                if k % 2 == 0:
                    pool.wait_ge(S("x_out"), 4 + k // 2 + 1)
                ins = pool.tensor_scalar(cfull[:, k, :], cfull[:, k, :], mod[:, KD + k, 1:2], mod[:, k, 1:2], ALU.mult, ALU.add)
                if k % 2:
                    ins.then_inc(S("full_c"), 1)
                else:
                    link(ins)

            def causal(h):
                for d in range(2):
                    pool.wait_ge(S("prob_full"), 2 * h + d + 1)
                    sign = 1 - 2 * d
                    pr = prob[:, h, d, :]
                    link(keep(pr[:, d * P:(d + 1) * P], ALU.is_ge, [[sign, P]], -sign))
                    keep(pr[:, 2 * P:], ALU.is_ge, [[sign, P]], -sign).then_inc(S("prob_ready"), 1)

            def weighted_keys(h):
                if h >= 2:
                    pool.wait_ge(S("state_mm"), 2 * (h - 1))
                for t in range(TT):
                    for d in range(2):
                        ins = pool.tensor_scalar(kw[:, h % 2, t, d, :], k_ctx[:, t, h * DK:(h + 1) * DK],
                                                 ws_col[:, 2 * t + d, h:h + 1], None, ALU.mult)
                        if t == 0 or d == 0:
                            link(ins)
                ins.then_inc(S("kw_ready"), 1)

            pool.wait_ge(S("ws_out"), 1)
            pool.wait_ge(S("k_done"), 4)
            weighted_keys(0)
            weighted_keys(1)
            for h in range(MH):
                causal(h)
            weighted_keys(2)
            weighted_keys(3)
            for h in range(MH):
                pool.wait_ge(S("ss"), base("ss", "head") + TT * (h + 1))
                rms_scale("head", SS["head"] + TT * h, TT)

            def post_norm(post, norm):
                for t in range(TT):
                    pool.wait_ge(S("ss"), base("ss", post) + 3 * (t + 1))
                    rms_scale(post, SS[post] + t, 1, halves=True)
                    pool.wait_ge(S("ss"), base("ss", post) + 3 * (t + 1) + 2)
                    rms_scale(norm, SS[norm] + t, 1, halves=True)

            post_norm("post1", "norm2")
            post_norm("post2", "norm3")

            pool.wait_ge(S("x_upd"), 8)
            link(pool.memset(level[:], 1.0))
            for i in range(6):
                b = 2 << i
                view = level[:, i, :].rearrange("p (n b) -> p n b", b=b)
                link(keep(view, ALU.is_ge, [[-b, P // b], [0, b]], 1))
                link(keep(view, ALU.is_ge, [[b, P // b], [0, b]], -1, base=b - 1))
            for i in range(6, 0, -1):
                link(pool.tensor_tensor(level[:, i, :], level[:, i, :], level[:, i - 1, :], ALU.subtract))
            pool.tensor_tensor(level[:, 0, :], level[:, 0, :], ident[:], ALU.subtract).then_inc(S("level_ready"), 1)

            for i in range(4):
                pool.wait_ge(S("ss_l2"), i + 1)
                c = slice(SS["l2"] + GH * i, SS["l2"] + GH * (i + 1))
                s = ss[:, c]
                link(pool.tensor_scalar(s, s, EPS, float(GD) if i < 2 else 1.0, ALU.add, ALU.mult))
                pool.tensor_tensor(rstd[:, c], s, mhalf[:, 0:GH], ALU.pow).then_inc(S("rstd_l2"), 1)
                if i < 2:
                    pool.wait_ge(S("dec_exp"), i + 1)
                    keep(decT[:, GH * i:GH * (i + 1), :], ALU.is_ge, [[0, GH], [1, P]], -1).then_inc(S("dec_ready"), 1)

            def by_head(out_, in_, scale, want):
                pool.tensor_tensor(out_.rearrange("p (h n) -> p h n", h=GH), in_.rearrange("p (h n) -> p h n", h=GH),
                                   scale.unsqueeze(2).to_broadcast([P, GH, GD]), ALU.mult).then_inc(S(want), 1)

            pool.wait_ge(S("tok_out"), 4)
            pool.wait_ge(S("egc_ready"), 1)
            by_head(q_exp[:], qk_n[:, 0, 1, :], egc[:, 0, :], "q_exp_ready")
            def level_of(i):
                if i >= 2:
                    pool.wait_ge(S("xs_mm"), TT * (i - 1))
                pool.tensor_tensor(cTl[:, i % 2], cT[:], level[:, i + 1, :].unsqueeze(1).to_broadcast([P, TT * GH, P]),
                                   ALU.mult).then_inc(S("cTl_ready"), 1)

            def fox_mask(h):
                pool.wait_ge(S("logit_ready"), TT * (h + 1))
                for c in (0, 2 * P):
                    keep(logit[:, h % 2, c:c + P], ALU.is_ge, [[-1, P]], 1, fill=NEG).then_inc(S("logit_masked"), 1)

            pool.wait_ge(S("cT_full"), TT)
            pool.wait_ge(S("level_ready"), 1)
            level_of(0)
            fox_mask(0)
            level_of(1)
            by_head(k_beta[:], qk_n[:, 1, 1, :], egc[:, 1, :], "k_beta_ready")
            by_head(k_dec[:], qk_n[:, 1, 0, :], egc[:, 2, :], "k_dec_ready")
            for i in range(1, FH):
                fox_mask(i)
                if i + 1 < len(LEVELS):
                    level_of(i + 1)
            for t in range(TT):
                pool.wait_ge(S("ss"), base("ss", "gdn") + GH * (t + 1))
                rms_scale("gdn", SS["gdn"] + GH * t, GH, 1.0 / GD)
            for name, counts in (("norm4", (2, 4)), ("norm5", (3, 4)), ("final", (3, 4))):
                for t in range(TT):
                    pool.wait_ge(S("ss"), base("ss", name) + counts[t])
                    rms_scale(name, SS[name] + t, 1, halves=True)



        @block.scalar
        def _(act):
            s_next = [0]

            def hi_until(n):
                while s_next[0] < min(n, n_split):
                    s = s_next[0]
                    raw_arrived(act, split[s])
                    if s >= RING:
                        act.wait_ge(group_used, s - RING + 1)
                    act.copy(part_view(w_hi, s), raw_view(split[s])).then_inc(hi_ready, 1)
                    s_next[0] += 1

            def hi_ahead(s0, r, u):
                s, r = in_round(s0 + 2 * u, r)
                raw_arrived(act, split[s], r)
                act.wait_ge(group_used, s - RING + 1 + 2 * ROUND * r)
                act.copy(part_view(w_hi, s), raw_view(split[s])).then_inc(hi_ready, 1)

            def load(dst, src, sem_name):
                act.dma_start(dst, src).then_inc(S(sem_name), 16)

            n_sums = [0]

            def sum_sq(src, c, width=D):
                n_sums[0] += 1
                act.activation(junk[:, 0:src.shape[-1]], src, ACT.Square, scale=width ** -0.5, accum_out=ss[:, c:c + 1]).then_inc(S("ss"), 1)
                act.wait_ge(S("ss"), n_sums[0])

            def norm_half(name, updates, i, t, n):
                act.wait_ge(S("x_upd"), updates + i + 1)
                sum_sq(x[:, t, n * NB:(n + 1) * NB], SS[name] + TT * n + t)

            def post_norm(post, norm, product, bank0, updates):
                for n in range(2):
                    done = at[product][n] + at[product][1] - at[product][0]
                    hi_until(done + 2 - n)
                    for t in range(TT):
                        if n == 1 and t == 0:
                            act.wait_ge(S("t0_done"), base("t0_done", product) + 1)
                        else:
                            act.wait_ge(group_used, done)
                        sum_sq(ps[:, bank0 + 2 * n + t, :], SS[post] + TT * n + t)
                        if n == 1:
                            for half in range(2):
                                norm_half(norm, updates, 2 * t + half, t, half)
                hi_until(done + 2)

            def hi_T(name, banks, scale, shift=None, pairs=range(KD // 2)):
                for i in pairs:
                    act.wait_ge(S("tr"), base("tr", name) + i + 1)
                    for k in (2 * i, 2 * i + 1):
                        src = ps[:, banks[i], k % 2 * T:(k % 2 + 1) * T]
                        if shift is None:
                            ins = act.activation(h_hi[:, k, :], src, ACT.Copy, scale=scale(k))
                        else:
                            ins = act.activation(h_hi[:, k, :], src, ACT.Identity, scale=scale(k), bias=shift(k))
                        ins.then_inc(S("hi"), 1)

            load(c_rows[KD:, :], I["c_ctx"].rearrange("(k p) -> k p", p=P), "c_in")
            load(x[:], I["x"][0].rearrange("(t p) n -> p t n", p=P), "x_in")
            act.wait_ge(S("const_ready"), 1)
            act.wait_ge(S("vec_T"), 1)
            act.activation(cpad[:, :, 0:2], ps[:, 7, 0:2 * KD].rearrange("p (c k) -> p k c", c=2), ACT.Silu)\
                .then_inc(S("c_ready"), 1)
            load(ctx_tok, I["ctx"][0].rearrange("(t p) n -> p t n", p=P), "ctx_in")
            for name, src in VEC:
                n = src.shape[0] // P
                load(vec_rows[0][col[name]:col[name] + n, :], src.rearrange("(k p) -> k p", p=P), "vec_in")
            load(vec_rows[1][0:3 * KF, :], I["ffn_conv_w"][0].rearrange("w (a b) -> (w a) b", b=P), "vec_in")
            load(vec_rows[1][3 * KF:4 * KF, :], I["ffn_conv_b"][0].rearrange("(a b) -> a b", b=P), "vec_in")
            load(vec_rows[2], I["conv_w_2"][0].rearrange("w (a b) -> (w a) b", b=P), "vec_in")
            gate0 = 2 * MH * DK + 2 * MH * DV
            load(wg[:], I["m_in_w"][0][:, gate0:gate0 + 16].rearrange("(k p) n -> p k n", p=P), "wg_in")
            load(bg[:], I["m_in_b"][0][gate0:gate0 + 16].partition_broadcast(P), "wg_in")
            act.wait_ge(S("x_in"), 16)
            for t in range(TT):
                sum_sq(x[:, t, :], SS["norm1"] + t)
            for i in range(4):
                act.wait_ge(S("tr"), i + 1)
                act.copy(full[:, 2 * i:2 * i + 2, :], ps[:, 2 + i, :].rearrange("p (k t) -> p k t", k=2)).then_inc(S("x_out"), 1)
            act.wait_ge(S("ctx_in"), 16)
            for t in range(TT):
                sum_sq(ctx_tok[:, t, :], SS["norm1"] + TT + t)
            bias_cols = (MH * DK, 0, 2 * MH * DK, 2 * MH * DK + NB, 2 * MH * DK + MH * DV, 2 * MH * DK + MH * DV + NB)

            def load_bias(i):
                load(bias[:, i % 2, :], I["m_in_b"][0][bias_cols[i]:bias_cols[i] + NB].partition_broadcast(P),
                     f"bias_in{i % 2}")

            act.wait_ge(S("wg_in"), 32)
            act.copy(wg_parts[:, :, 0:16], wg[:]).then_inc(S("wg_hi"), 1)

            def gate_rows_out(i, n):
                act.wait_ge(S("gate_rows_mm"), i)
                act.copy(gate_rows[:, 0:n], ps[0:32, 4, 0:n]).then_inc(S("gate_rows"), 1)

            hi_until(1)
            for i, (hi, src, pair) in enumerate(first_pairs()):
                if i == 2:
                    for n in range(4):
                        act.wait_ge(S("tr"), 4 + n + 1)
                        act.copy(cfull[:, 2 * n:2 * n + 2, :], ps[:, 2 + n, :].rearrange("p (k t) -> p k t", k=2))\
                            .then_inc(S("x_out"), 1)
                act.wait_ge(S("full_x" if src is full else "full_c"), 2 * (i // 4) + i % 2 + 1)
                act.copy(hi[:, pair, :], src[:, pair, :]).then_inc(S("hi"), 1)
                if i == 3:
                    hi_until(2)
            act.wait_ge(S("hi"), KD)
            load_bias(0)
            load_bias(1)
            act.wait_ge(hi_ready, 2)
            gate_rows_out(1, 2 * T)
            load(gp1[:], I["post_mix_g"][0].partition_broadcast(P), "small_in")
            load(gp2[:], I["post_ffn_g"][0].partition_broadcast(P), "small_in")
            hi_until(3)
            act.wait_ge(S("gate_abs"), 1)
            act.activation(sp1[:], sp1[:], ACT.Exp, scale=-1.0).then_inc(S("gate_exp"), 1)
            act.wait_ge(S("gate_exp"), 1)
            act.activation(sp1[:], sp1[:], ACT.Ln, bias=ones[:, 0:1]).then_inc(S("gate_ln"), 1)
            hi_until(4)
            act.wait_ge(S("k_done"), 4)
            load_bias(2)
            hi_until(5)
            act.wait_ge(S("mrow_ready"), 2)
            for d in range(2):
                act.activation(ws_row[:, d, :], ps[0:MH, 4, d * T:(d + 1) * T], ACT.Exp, bias=m_ctx[:, 2 + d:3 + d])\
                    .then_inc(S("ws_row"), 1)
            for d in range(2):
                act.activation(w_row[:, d, :], m_row[:, d, :], ACT.Exp, bias=m_ctx[:, d:d + 1], scale=-1.0)\
                    .then_inc(S("w_row"), 1)
            act.wait_ge(S("q_done"), 2)
            load_bias(3)
            hi_until(6)
            for h in range(MH):
                act.wait_ge(S("qk_T"), h + 1)
                bank = ps[:, 5 + h % 2, :]
                act.activation(qkT[:, h, 0, :], bank[:, 0:T], ACT.Copy, scale=DK ** -0.5).then_inc(S("qkT_ready"), 1)
                act.copy(qkT[:, h, 1, :], bank[:, T:2 * T]).then_inc(S("qkT_ready"), 1)
            act.wait_ge(S("mt_ready"), 1)
            act.activation(emt[:], emt[:], ACT.Exp, scale=-1.0).then_inc(S("emt_ready"), 1)
            hi_until(7)

            def decay(h):
                for d in range(2):
                    act.wait_ge(S("z_ready"), 2 * (2 * h + d) + 2)
                    act.activation(prob[:, h, d, :], prob[:, h, d, :], ACT.Exp, scale=-1.0).then_inc(S("decay_ready"), 1)

            def state_out(h):
                for d in range(2):
                    act.wait_ge(S("state_mm"), 2 * h + d + 1)
                    act.copy(state[:, h, d, :], ps[:, 4 + 2 * (h % 2) + d, 0:DV + 1]).then_inc(S("state_out"), 1)

            decay(0)
            hi_until(8)
            act.wait_ge(S("v_done"), 4)
            load_bias(4)
            hi_until(9)
            decay(1)
            hi_until(10)
            decay(2)
            hi_until(11)
            act.wait_ge(S("v_done"), 8)
            load_bias(5)
            decay(3)
            hi_until(12)
            state_out(0)
            state_out(1)
            hi_until(13)

            def gate_o(n):
                for t in range(TT):
                    act.wait_ge(S("o_done"), TT * n + t + 1)
                    o = so[:, t, n * NB:(n + 1) * NB]
                    act.activation(o, o, ACT.Sigmoid).then_inc(S("so_ready"), 1)

            def head_squares(h):
                for t in range(TT):
                    act.wait_ge(S("h_sum"), TT * h + t + 1)
                    sum_sq(hsum[:, t, h * DV:(h + 1) * DV], SS["head"] + TT * h + t, DV)

            state_out(2)
            state_out(3)
            hi_until(14)
            gate_o(0)
            gate_o(1)
            hi_until(15)
            for h in range(MH):
                head_squares(h)
                if h == 1:
                    hi_T("y1", (0, 1, 0, 1), lambda k: pcol("m_norm", k), pairs=range(0, 2))
            hi_T("y1", (0, 1, 0, 1), lambda k: pcol("m_norm", k), pairs=range(2, MH))
            post_norm("post1", "norm2", "mix_out", 2, 0)
            hi_T("norm2", NORM_BANKS["norm2"], scale=lambda k: mod2[:, KD + k:KD + k + 1], shift=lambda k: mod2[:, k:k + 1])

            U0 = at["up"][0]
            hi_until(U0 + 3)

            def up_step(r, u):
                j = ROUND * r + u
                act.wait_ge(group_used, U0 + 2 * j + 1)
                act.wait_ge(S("act_full"), j + 1)
                for f in range(2):
                    k = 2 * j + f
                    act.activation(cv[:, u, f, :], ps[:, 2 * u, f * T:(f + 1) * T], ACT.Identity,
                                   bias=pcol("conv_b", k), scale=pcol("conv_w", KF + k)).then_inc(S("conv_mid"), 1)
                hi_ahead(U0 + 3, r, u)
                act.wait_ge(S("conv_done"), 2 * j + 2)
                act.activation(cv[:, u], cv[:, u], ACT.Silu).then_inc(S("silu_ready"), 1)
                hi_ahead(U0 + 4, r, u)
                act.wait_ge(S("act_full"), ROUND + j + 1)
                act.copy(act_hi[:, bass.ds(2 * j, 2), :], actf[:, u]).then_inc(S("act_hi_ready"), 1)

            rounds(act, up_step)
            s_next[0] = U0 + 2 * PAIRS + 3
            post_norm("post2", "norm3", "down", 4, 4)

            load(wsm[:, :, 0:8], I["w_in_2"][0][:, 4 * GH * GD:4 * GH * GD + 2 * GH].rearrange("(k p) n -> p k n", p=P),
                 "small_in")
            f0 = 4 * GH * GD + 2 * GH + 3 * FH * FD
            load(wsm[:, :, 8:16], I["w_in_2"][0][:, f0:f0 + FH].rearrange("(k p) n -> p k n", p=P), "small_in")
            load(gprm[:, 0:4], I["dt_bias_2"][0].partition_broadcast(P), "small_in")
            load(gprm[:, 4:8], I["a_log_2"][0].partition_broadcast(P), "small_in")
            load(gprm[:, 8:16], I["fox_f_bias_2"][0].partition_broadcast(P), "small_in")
            hi_T("norm3", NORM_BANKS["norm3"], lambda k: pcol("attn_norm", k))
            G0 = at["gdn"][0]
            hi_until(G0 + 3)
            act.wait_ge(S("small_in"), 16 * 7)
            act.copy(wg_parts[:, :, 0:16], wsm[:]).then_inc(S("wg_hi"), 1)

            def gdn_mid(j, ahead=True):
                s = at["gdn"][j]
                hi_until(s + 3)
                act.wait_ge(group_used, s + 1)
                for f in range(2):
                    act.activation(r5[:, 2 * j + f, :], ps[:, j % 2, f * T:(f + 1) * T], ACT.Copy,
                                   scale=pcol("conv2", 36 + 2 * j + f)).then_inc(S("conv2_mid"), 1)
                if ahead:
                    hi_until(s + 4)

            def gdn_silu(j):
                for f in (2 * j, 2 * j + 1):
                    act.wait_ge(S("conv2_done"), f + 1)
                    act.activation(r5[:, f, :], r5[:, f, :], ACT.Silu).then_inc(S("conv2_silu"), 1)

            gdn_mid(0, ahead=False)
            gate_rows_out(2, T)
            hi_until(G0 + 4)
            act.wait_ge(S("gate_abs"), 2)
            act.activation(sp2[:], sp2[:], ACT.Exp, scale=-1.0).then_inc(S("gate_exp"), 1)
            act.activation(gprm[:, 4:8], gprm[:, 4:8], ACT.Exp).then_inc(S("gate_exp"), 1)
            act.wait_ge(S("gate_exp"), 3)
            act.wait_ge(S("beta_ready"), 1)
            act.activation(sp2[:], sp2[:], ACT.Ln, bias=ones[:, 0:1]).then_inc(S("gate_ln"), 1)

            def fsum_out(i):
                act.wait_ge(S("fsum_mm"), i + 1)
                act.activation(neg_c[:, 2 * i:2 * i + 2, :], ps[:, 7, :].rearrange("p (b t) -> p b t", b=2), ACT.Copy,
                               scale=-1.0).then_inc(S("neg_c_out"), 1)

            def token_squares(i):
                act.wait_ge(S("tok_T"), i + 1)
                if i >= 2:
                    act.wait_ge(S("ss_l2"), i - 1)
                act.activation(sq[:, i % 2, :], ps[:, TOKEN_BANKS[i], :], ACT.Square).then_inc(S("sq_ready"), 1)

            def fox_evac(m):
                s, j = at["fox"][m], FOX_ORDER[m]
                hi_until(s + 3)
                act.wait_ge(group_used, s + 1)
                act.copy(foxT[:, 2 * j:2 * j + 2, :], ps[:, m if m < 2 else 3, :].rearrange("p (f t) -> p f t", f=2))\
                    .then_inc(S("fox_T"), 2)
                hi_until(s + 4)

            def bank_out(dst, bank, want, func=None):
                if func is None:
                    act.copy(dst, ps[:, bank, :]).then_inc(S(want), 1)
                else:
                    act.activation(dst, ps[:, bank, :], func).then_inc(S(want), 1)

            gdn_mid(1)
            gdn_mid(2, ahead=False)
            for t in range(TT):
                act.wait_ge(S("dec_z"), t + 1)
                d = decT[:, GH * t:GH * (t + 1), :]
                act.activation(d, d, ACT.Exp).then_inc(S("dec_exp"), 1)
            act.wait_ge(S("egc_diff"), 2)
            for i in (0, 2):
                act.activation(egc[:, i, :], egc[:, i, :], ACT.Exp).then_inc(S("egc_exp"), 1)
            gdn_silu(0)
            gdn_silu(1)
            fsum_out(0)
            hi_until(at["gdn"][2] + 4)
            gdn_silu(2)
            gdn_mid(3)
            gdn_silu(3)
            token_squares(0)
            token_squares(1)
            fsum_out(1)
            gdn_mid(4, ahead=False)
            fsum_out(2)
            token_squares(2)
            token_squares(3)
            hi_until(at["gdn"][4] + 4)
            fsum_out(3)
            gdn_silu(4)
            gdn_mid(5)
            gdn_silu(5)
            for h in range(GH):
                act.wait_ge(S("gT_mm"), h + 1)
                act.copy(gT[:, h].rearrange("p a t -> p (a t)"), ps[:, 4 + h, :]).then_inc(S("gT_ready"), 1)
            fox_evac(0)
            fox_evac(1)

            def v_out(t):
                g0 = at["fox_v"][0]
                hi_until(g0 + 3 + t)
                if t == 0:
                    act.wait_ge(S("first_tile"), 1)
                else:
                    act.wait_ge(group_used, g0 + 2)
                bank_out(fox_v[:, t, :], 3, "fox_v_out")

            def z_out(t):
                g0 = at["z"][0]
                hi_until(g0 + 3 + t)
                if t == 0:
                    act.wait_ge(S("first_tile"), 2)
                else:
                    act.wait_ge(group_used, g0 + 2)
                bank_out(zs[:, t, :], 3, "z_out")
                if t == TT - 1:
                    hi_until(g0 + 5)

            hi_until(at["fox_v"][0] + 3)
            for t in range(TT):
                act.wait_ge(S("invT_T"), t + 1)
                bank_out(inv[:, GH * t:GH * (t + 1), :].rearrange("p h t -> p (h t)"), 4 + t, "inv0_ready")
            act.wait_ge(S("q_expT_mm"), 1)
            bank_out(q_expT[:].rearrange("p h t -> p (h t)"), 6, "q_expT_ready")

            def fox_exp(h):
                act.wait_ge(S("fox_max"), h + 1)
                act.wait_ge(S("logit_masked"), 2 * h + 2)
                for t, part in ((0, slice(0, P)), (1, slice(P, 3 * P))):
                    row = logit[:, h % 2, part]
                    act.activation(row, row, ACT.Exp, bias=fsum[:, h % 2, t:t + 1],
                                   accum_out=fsum[:, h % 2, 2 + t:3 + t]).then_inc(S("prob2_ready"), 1)

            def prT_out(h):
                act.wait_ge(S("prT_mm"), h + 1)
                if h >= 2:
                    act.wait_ge(S("fox_mm"), h - 1)
                act.copy(prT[:, h % 2, :], ps[:, 1, 0:3 * P]).then_inc(S("prT_ready"), 1)

            def fox_step(i):
                if 1 <= i <= FH:
                    prT_out(i - 1)
                if i < FH:
                    fox_exp(i)

            between = (lambda: v_out(1), lambda: fox_evac(2), lambda: fox_evac(3), lambda: z_out(0), lambda: z_out(1), None)
            fox_step(0)
            v_out(0)
            for i in range(len(LEVELS)):
                for t in range(TT):
                    act.wait_ge(S("xs_mm"), TT * i + t + 1)
                    if i:
                        act.wait_ge(S("y_mm"), TT * (i - 1) + t + 1)
                    bank_out(xs[:, GH * t:GH * (t + 1), :].rearrange("p h t -> p (h t)"), 4 + t, "xs_ready")
                fox_step(FOX_STEPS[i][0])
                if between[i] is not None:
                    between[i]()
                if FOX_STEPS[i][1] is not None:
                    fox_step(FOX_STEPS[i][1])
            act.wait_ge(S("u_mm"), 1)
            bank_out(u_tok[:, 0, :], 4, "u_out")
            act.wait_ge(S("u_mm"), 2)
            bank_out(u_tok[:, 1, :], 5, "u_out")
            act.wait_ge(S("u_mm"), 3)
            bank_out(wT, 6, "wT_ready")

            def mix_hi(i):
                act.wait_ge(S("tr"), base("tr", "mix") + i + 1)
                k = 2 * MIX_PAIRS[i]
                dst, src = h_hi[:, k:k + 2, :], ps[:, 2 + i, :].rearrange("p (f t) -> p f t", f=2)
                if i < 2:
                    act.copy(dst, src).then_inc(S("hi"), 1)
                else:
                    act.activation(dst, src, ACT.Copy, scale=pcol("gdn_norm", 0)).then_inc(S("hi"), 1)

            mix_hi(0)
            mix_hi(1)
            act.wait_ge(S("st_mm"), 1)
            bank_out(st1, 7, "st_ready")
            for t in range(TT):
                act.activation(zs[:, t, :], zs[:, t, :], ACT.Silu).then_inc(S("z_silu"), 1)
            for t in range(TT):
                act.wait_ge(S("o_mm"), t + 1)
                for h in range(GH):
                    sum_sq(ps[:, (0, 6)[t], h * GD:(h + 1) * GD], SS["gdn"] + GH * t + h, 1)
            mix_hi(2)
            mix_hi(3)
            hi_until(at["att_out"][0] + 5)
            for i in range(4):
                norm_half("norm4", 8, i, i // 2, i % 2)
            hi_until(at["att_out"][0] + 6)
            load(p_tok[:], I["p_2"][0, 0].rearrange("(t p) n -> p t n", p=P), "last_in")
            load(gp3[:], I["final_norm_w_2"].partition_broadcast(P), "last_in")
            hi_T("norm4", NORM_BANKS["norm4"], lambda k: pcol("ffn_norm", k))
            V0 = at["gate_up"][0]
            hi_until(V0 + 3)

            def gate_up_step(r, u):
                j = ROUND * r + u
                act.wait_ge(group_used, V0 + 2 * j + 1)
                act.wait_ge(S("act_full"), base("act_full", "gate_up") + j + 1)
                act.activation(sil[:, u], ps[:, 2 * u, :].rearrange("p (f t) -> p f t", f=2), ACT.Silu)\
                    .then_inc(S("silu_ready"), 1)
                hi_ahead(V0 + 3, r, u)
                hi_ahead(V0 + 4, r, u)
                act.wait_ge(S("act_full"), base("act_full", "gate_up") + ROUND + j + 1)
                act.copy(act2_hi[:, bass.ds(2 * j, 2), :], actf2[:, u]).then_inc(S("act_hi_ready"), 1)

            rounds(act, gate_up_step)
            s_next[0] = V0 + 2 * PAIRS + 3
            act.wait_ge(S("pT_ready"), 1)
            act.copy(p_hi[:], pT[:]).then_inc(S("p_hi"), 1)
            hi_until(at["down2"][1] + 6 + 2)
            for i in range(4):
                norm_half("norm5", 12, i, i % 2, i // 2)
            hi_until(at["ple_p"][0] + 3)
            act.wait_ge(group_used, at["ple_p"][0] + 1)
            for n in range(2):
                for t in range(TT):
                    bank_out(pgate[:, t, n * NB:(n + 1) * NB], 2 * n + t, "p_out")
            hi_T("norm5", NORM_BANKS["norm5"], lambda k: pcol("ple_norm", k))
            hi_until(n_split)
            done = at["ple_g"][0] + 2
            for n in range(2):
                for t in range(TT):
                    i = TT * n + t
                    if t == 1:
                        act.wait_ge(group_used, done + 2 * n)
                    elif n == 0:
                        act.wait_ge(S("ple_mm"), 1)
                    else:
                        act.wait_ge(S("t0_done"), base("t0_done", "ple_g") + 1)
                    if i >= 2:
                        act.wait_ge(S("x_upd"), 16 + i - 1)
                    bank_out(tmp[:, i % 2, :], i, "sig_ready", ACT.Sigmoid)
                    if n == 1:
                        norm_half("final", 16, i, t, n)
                        act.wait_ge(S("rstd"), base("rstd", "final") + t + 1)
                        act.wait_ge(S("gained"), t + 1)
                        r = SS["final"] + t
                        act.activation(pgate[:, t, 0:NB], pgate[:, t, 0:NB], ACT.Copy, scale=rstd[:, r:r + 1])\
                            .then_inc(S("result0"), 1)
                if n == 0:
                    for t in range(TT):
                        norm_half("final", 16, t, t, n)


        @block.vector
        def _(dve):
            link = chained(dve, "dve_chain")
            s_next, a_next = [0], [0]

            def ada2_group():
                i = a_next[0]
                v, n, half = i // 4, i // 2 % 2, i % 2
                acc = ada_acc[v][:, n * NB:(n + 1) * NB]
                raw_arrived(dve, ada2[i])
                for k in range(4):
                    w, c = raw_view(ada2[i])[:, k, :], cpad[:, 4 * half + k, 0:1]
                    if half == 0 and k == 0:
                        ins = dve.tensor_scalar(acc, w, c, None, ALU.mult)
                    else:
                        ins = dve.scalar_tensor_tensor(acc, w, c, acc, ALU.mult, ALU.add)
                    if k < 3:
                        link(ins)
                ins.then_inc(ada2_used, 1)
                dve.wait_ge(ada2_used, i + 1)
                a_next[0] += 1

            def lo_until(n):
                while s_next[0] < min(n, n_split):
                    s = s_next[0]
                    while a_next[0] < len(ada2) and ada2[a_next[0]] < split[s]:
                        ada2_group()
                    dve.wait_ge(hi_ready, s + 1)
                    dve.tensor_tensor(part_view(w_lo, s), raw_view(split[s]), part_view(w_hi, s).bitcast(F32),
                                      ALU.subtract).then_inc(lo_ready, 1)
                    s_next[0] += 1

            def lo_ahead(s0, r, u):
                s, r = in_round(s0 + 2 * u, r)
                dve.wait_ge(hi_ready, s + 1 + 2 * ROUND * r)
                dve.tensor_tensor(part_view(w_lo, s), raw_view(split[s]), part_view(w_hi, s).bitcast(F32),
                                  ALU.subtract).then_inc(lo_ready, 1)

            def lo_part(lo, src, hi, want):
                dve.tensor_tensor(lo, src, hi.bitcast(F32), ALU.subtract).then_inc(S(want), 1)

            def transposed(name, banks, scale, shift=None, pairs=range(KD // 2)):
                for k in range(2 * pairs.start, 2 * pairs.stop):
                    dve.wait_ge(S("hi"), base("hi", name) + k // 2 * 2 + 2)
                    src, hi = ps[:, banks[k // 2], k % 2 * T:(k % 2 + 1) * T], h_hi[:, k, :].bitcast(F32)
                    if shift:
                        link(dve.tensor_scalar(full[:, k, :], src, scale(k), shift(k), ALU.mult, ALU.add))
                        ins = dve.tensor_tensor(h_lo[:, k, :], full[:, k, :], hi, ALU.subtract)
                    else:
                        ins = dve.scalar_tensor_tensor(h_lo[:, k, :], src, scale(k), hi, ALU.mult, ALU.subtract)
                    ins.then_inc(S("hT"), 1)

            def diagonal(name, t, count):
                dve.wait_ge(S("rstd"), count)
                c = SS[name] + t
                dve.tensor_scalar(diag[:, t, :], ident[:], rstd[:, c:c + 1], None, ALU.mult).then_inc(S("diag"), 1)

            def post_norm(post, norm, gain, bank0):
                def gained(n, t, count):
                    dve.wait_ge(S("ss"), base("ss", post) + count)
                    c = slice(n * NB, (n + 1) * NB)
                    link(dve.tensor_tensor(yg[:, t, c], ps[:, bank0 + 2 * n + t, :], gain[:, c], ALU.mult))

                gained(0, 0, 1)
                gained(0, 1, 2)
                for t in range(TT):
                    gained(1, t, 3 * (t + 1))
                    dve.wait_ge(S("rstd"), base("rstd", post) + 2 * t + 1)
                    for n in range(2):
                        c = slice(n * NB, (n + 1) * NB)
                        r = SS[post] + t
                        dve.scalar_tensor_tensor(x[:, t, c], yg[:, t, c], rstd[:, r:r + 1], x[:, t, c], ALU.mult, ALU.add)\
                            .then_inc(S("x_upd"), 1)
                    diagonal(norm, t, base("rstd", post) + 2 * t + 2)

            def residual(name, nk):
                for n in range(2):
                    lo_until(at[name][n] + nk + 2)
                    dve.wait_ge(group_used, at[name][n] + nk)
                    c = slice(n * NB, (n + 1) * NB)
                    for t in range(TT):
                        dve.tensor_tensor(x[:, t, c], x[:, t, c], ps[:, 4 + 2 * n + t, :], ALU.add).then_inc(S("x_upd"), 1)

            def ada1_rows(n):
                dve.wait_ge(ada1_used, 2 * n + 2)
                dve.tensor_copy(ada_rows[:, n, :], ps[:, ADA_BANKS[n], :]).then_inc(S("ada_rows"), 1)

            def first_diagonals(c):
                dve.wait_ge(S("rstd"), c + 1)
                for t in (TT * c, TT * c + 1):
                    dve.tensor_scalar(diag[:, t, :], ident[:], rstd[:, t:t + 1], None, ALU.mult).then_inc(S("diag"), 1)

            ada1_rows(0)
            first_diagonals(0)
            ada1_rows(1)
            first_diagonals(1)
            dve.wait_ge(S("vec_T"), 4)
            dve.tensor_copy(cols[:], ps[:, 7, 2 * KD:2 * KD + n_col]).then_inc(S("cols_ready"), 1)
            ada1_rows(2)
            def gate_weights_lo(i, src):
                dve.wait_ge(S("wg_hi"), i)
                lo_part(wg_parts[:, :, 16:], src[:], wg_parts[:, :, 0:16], "wg_lo")

            gate_weights_lo(1, wg)
            dve.wait_ge(S("cols_ready"), 1)

            def modulation(half):
                dve.wait_ge(S("ada_T"), 3 + half)
                k = slice(half * KD // 2, (half + 1) * KD // 2)
                by_v = mod[:].rearrange("p (v k) c -> p v k c", v=2)
                bias = cols[:, col["ada_b"]:col["ada_b"] + 2 * KD].rearrange("p (v k) -> p v k", v=2)
                for v in range(2):
                    link(dve.tensor_tensor(by_v[:, v, k, :], ps[:, 6, 0:4 * KD].rearrange("p (v k c) -> p v k c", v=2, c=2)[:, v, k, :],
                                           bias[:, v, k].unsqueeze(2).to_broadcast([P, KD // 2, 2]), ALU.add))
                gain = cols[:, col["pre_mix"]:col["pre_mix"] + KD][:, k].unsqueeze(2).to_broadcast([P, KD // 2, 2])
                dve.scalar_tensor_tensor(by_v[:, 1, k, :], by_v[:, 1, k, :], 1.0, gain, ALU.add, ALU.mult)\
                    .then_inc(S("mod_ready"), 1)
                dve.wait_ge(S("mod_ready"), half + 1)

            for half in range(2):
                if half == 1:
                    ada1_rows(3)
                modulation(half)
                for i in (2 * half, 2 * half + 1):
                    for k in (2 * i, 2 * i + 1):
                        ins = dve.tensor_scalar(full[:, k, :], full[:, k, :], mod[:, KD + k, 0:1], mod[:, k, 0:1],
                                                ALU.mult, ALU.add)
                        if k % 2 == 0:
                            link(ins)
                    ins.then_inc(S("full_x"), 1)
                if half == 0:
                    lo_until(1)
                for c, (lo, src, hi) in enumerate(((h_lo, full, h_hi), (c_lo, cfull, c_hi))):
                    for i in range(2):
                        pair = slice(4 * half + 2 * i, 4 * half + 2 * i + 2)
                        dve.wait_ge(S("hi"), 4 * half + 2 * c + i + 1)
                        lo_part(lo[:, pair, :], src[:, pair, :], hi[:, pair, :], "hT")
            lo_until(2)

            dve.wait_ge(S("gate_mm"), 1)
            dve.wait_ge(S("wg_in"), 32)
            link(dve.tensor_tensor(gate[:], ps[:, 4, 0:2 * TT * 16].rearrange("p (t g) -> p t g", t=2 * TT),
                                   bg[:].unsqueeze(1).to_broadcast([P, 2 * TT, 16]), ALU.add))
            dve.scalar_tensor_tensor(sp1[:], gate_v[:, :, 1, :], -1.0, gate_v[:, :, 1, :], ALU.mult, ALU.max).then_inc(S("gate_abs"), 1)
            lo_until(3)
            dve.wait_ge(S("gate_ln"), 1)
            dve.scalar_tensor_tensor(lf[:], gate_v[:, :, 1, :], 0.0, sp1[:], ALU.min, ALU.subtract).then_inc(S("lf_ready"), 1)
            lo_until(4)

            def bias_of(i):
                dve.wait_ge(S(f"bias_in{i % 2}"), 16 * (i // 2 + 1))
                return bias[:, i % 2, :]

            dve.wait_ge(group_used, at["k"][0] + 2)
            for i, dst in enumerate((qk_tok[:, 1, 0, :], qk_tok[:, 1, 1, :], k_ctx[:, 0, :], k_ctx[:, 1, :])):
                dve.tensor_tensor(dst, ps[:, i, :], bias_of(0), ALU.add).then_inc(S("k_done"), 1)
            dve.wait_ge(S("cum_mm"), 1)
            n_td = TT * 2
            link(dve.tensor_copy(b_col[:], ps[:, 4, 0:16].rearrange("p (a h) -> p a h", h=MH)))
            dve.tensor_tensor(u_col[:], gate_v[:, 0:n_td, 0, :], b_col[:], ALU.subtract).then_inc(S("u_ready"), 1)
            dve.tensor_tensor(gs_col[:], ps[:, 4, 16:32].rearrange("p (a h) -> p a h", h=MH), gate_v[:, n_td:, 0, :],
                              ALU.add).then_inc(S("u_ready"), 1)
            dve.tensor_copy(b_ctx[:], ps[0:MH, 4, 32:34]).then_inc(S("u_ready"), 1)
            lo_until(5)
            dve.wait_ge(group_used, at["q"][0] + 2)
            for t in range(TT):
                dve.tensor_tensor(qk_tok[:, 0, t, :], ps[:, 5 + t, :], bias_of(1), ALU.add).then_inc(S("q_done"), 1)
            dve.wait_ge(S("u_rows"), 1)
            link(dve.tensor_copy(u_row, ps[0:MH, 7, :].rearrange("p (d t) -> p d t", d=2)))
            link(dve.tensor_reduce(m_ctx[:, 0:2], ps[0:MH, 4, :].rearrange("p (d t) -> p d t", d=2), AX_X, ALU.max))
            link(dve.tensor_tensor(m_ctx[:, 0:2], m_ctx[:, 0:2], b_ctx[:], ALU.max))
            link(dve.tensor_scalar(m_ctx[:, 2:4], m_ctx[:, 0:2], -1.0, None, ALU.mult))
            dve.tensor_tensor_scan(m_row[:, 0, :], u_row[:, 0, :], u_row[:, 0, :], m_ctx[:, 0:1], ALU.max, ALU.max)\
                .then_inc(S("mrow_ready"), 1)
            dve.tensor_tensor_scan(m_row[:, 1, ::-1], u_row[:, 1, ::-1], u_row[:, 1, ::-1], m_ctx[:, 1:2], ALU.max, ALU.max)\
                .then_inc(S("mrow_ready"), 1)
            lo_until(6)
            dve.wait_ge(S("m_cols"), 1)
            dve.tensor_tensor(emt[:], ps[:, 7, 0:16].rearrange("p (a h) -> p a h", h=MH), b_col[:], ALU.add)\
                .then_inc(S("mt_ready"), 1)
            dve.tensor_copy(ws_col[:], ps[:, 7, 16:32].rearrange("p (a h) -> p a h", h=MH)).then_inc(S("ws_out"), 1)
            link(dve.memset(vaug[:, :, :, DV:DV + 1], 1.0))

            def exponents(h):
                for d in range(2):
                    dve.wait_ge(S("m_bcast"), 2 * h + d + 1)
                    pr = prob[:, h, d, :]
                    one = slice(P, T) if d == 0 else slice(0, P)
                    for part, tt, tok in ((slice(0, T), d, slice(0, T)), (slice(T, 3 * P), 1 - d, one)):
                        dve.tensor_scalar(pr[:, part], ps[:, 5 + d, tok], u_col[:, 2 * tt + d, h:h + 1], 0.0,
                                          ALU.subtract, ALU.max).then_inc(S("z_ready"), 1)
                    dve.tensor_tensor(qTw[:, h, d, :], qkT[:, h, 0, :], ps[:, 5 + d, T:2 * T], ALU.mult)\
                        .then_inc(S("qTw_ready"), 1)

            def weigh_scores(h):
                dve.wait_ge(S("score_mm"), h + 1)
                bank = (4, 7)[h % 2]
                for d in range(2):
                    dve.wait_ge(S("decay_ready"), 2 * h + d + 1)
                    pr = prob[:, h, d, :]
                    link(dve.tensor_tensor(pr[:, 0:T], pr[:, 0:T], ps[:, bank, d * T:(d + 1) * T], ALU.mult))
                    one = (1 - d) * T + (1 - d) * P
                    dve.tensor_tensor(pr[:, T:], pr[:, T:], ps[:, bank, one:one + P], ALU.mult).then_inc(S("prob_full"), 1)

            def v_evac(n):
                dve.wait_ge(group_used, at["v"][n] + 2)
                for i in range(2 * TT):
                    dve.tensor_tensor(vaug[:, i, 2 * n:2 * n + 2, 0:DV], ps[:, i, :].rearrange("p (h e) -> p h e", h=2),
                                      bias_of(2 + n).rearrange("p (h e) -> p h e", h=2), ALU.add).then_inc(S("v_done"), 1)

            lo_until(7)
            v_evac(0)
            exponents(0)
            lo_until(8)
            weigh_scores(0)
            lo_until(9)
            exponents(1)
            weigh_scores(1)
            lo_until(10)
            v_evac(1)
            exponents(2)
            weigh_scores(2)
            lo_until(11)
            exponents(3)
            weigh_scores(3)
            lo_until(12)

            def o_evac(n):
                dve.wait_ge(group_used, at["o"][n] + 2)
                for t in range(TT):
                    dve.tensor_tensor(so[:, t, n * NB:(n + 1) * NB], ps[:, 2 * n + t, :], bias_of(4 + n), ALU.add)\
                        .then_inc(S("o_done"), 1)

            def head_out(h):
                if h == 0:
                    dve.wait_ge(S("emt_ready"), 1)
                dve.wait_ge(S("out_mm"), h + 1)
                num_den = ps[:, 4:8, DV].rearrange("p (d t) -> p d t", d=2)
                by_d = den[:, 0, :].rearrange("p (d t) -> p d t", d=2)
                floor = emt[:].rearrange("p (t d) h -> p d t h", d=2)[:, :, :, h]
                link(dve.scalar_tensor_tensor(by_d, num_den, -1.0, floor, ALU.mult, ALU.max))
                link(dve.tensor_tensor(by_d, by_d, num_den, ALU.max))
                link(dve.reciprocal(den[:, 1, :], den[:, 0, :]))
                for t in range(TT):
                    hs = hsum[:, t, h * DV:(h + 1) * DV]
                    link(dve.tensor_scalar(hs, ps[:, 4 + t, 0:DV], den[:, 1, t:t + 1], None, ALU.mult))
                    dve.scalar_tensor_tensor(hs, ps[:, 6 + t, 0:DV], den[:, 1, TT + t:TT + t + 1], hs, ALU.mult, ALU.add)\
                        .then_inc(S("h_sum"), 1)

            def times_gate(bank, gp):
                for n in range(2):
                    c = slice(n * NB, (n + 1) * NB)
                    dve.tensor_tensor(gp[:, c], gp[:, c], ps[:, bank + n, :], ALU.mult).then_inc(S("mods_out"), 1)

            def gated_head(h):
                dve.wait_ge(S("so_ready"), 4)
                dve.wait_ge(S("rstd"), base("rstd", "head") + h + 1)
                for t in range(TT):
                    c = slice(h * DV, (h + 1) * DV)
                    r = SS["head"] + TT * h + t
                    dve.scalar_tensor_tensor(ymix[:, t, c], hsum[:, t, c], rstd[:, r:r + 1], so[:, t, c], ALU.mult, ALU.mult)\
                        .then_inc(S("y1_ready"), 1)

            lo_until(13)
            o_evac(0)
            lo_until(14)
            o_evac(1)
            head_out(0)
            dve.wait_ge(S("small_in"), 32)
            dve.wait_ge(S("ada_sum"), 1)
            times_gate(0, gp1)
            head_out(1)
            dve.wait_ge(S("ada_sum"), 2)
            bias2 = cols[:, col["ada_b"] + 3 * KD:col["ada_b"] + 5 * KD]
            link(dve.tensor_tensor(mod2[:], ps[:, 2, 0:2 * KD], bias2, ALU.add))
            dve.scalar_tensor_tensor(mod2[:, KD:], mod2[:, KD:], 1.0, cols[:, col["pre_ffn"]:col["pre_ffn"] + KD],
                                     ALU.add, ALU.mult).then_inc(S("mods_out"), 1)
            gated_head(0)
            gated_head(1)
            head_out(2)
            transposed("y1", (0, 1, 0, 1), lambda k: pcol("m_norm", k), pairs=range(0, 2))
            lo_until(15)
            gated_head(2)
            head_out(3)
            gated_head(3)
            transposed("y1", (0, 1, 0, 1), lambda k: pcol("m_norm", k), pairs=range(2, MH))
            lo_until(at["mix_out"][1] + 3)
            post_norm("post1", "norm2", gp1, 2)
            dve.sem_inc(S("act_full"), ROUND)
            transposed("norm2", NORM_BANKS["norm2"], lambda k: mod2[:, KD + k:KD + k + 1], lambda k: mod2[:, k:k + 1])

            def up_half(u):
                return ps[:, 2 * u + 1, :].rearrange("p (f t) -> p f t", f=2)

            U0 = at["up"][0]
            lo_until(U0 + 3)

            def up_step(r, u):
                j = ROUND * r + u
                for f in range(2):
                    k = 2 * j + f
                    dve.wait_ge(S("conv_mid"), 2 * j + 2)
                    rows = cv[:, u, f, :].rearrange("p (r w) -> p r w", w=GRID_W)
                    src = ps[:, 2 * u, f * T:(f + 1) * T].rearrange("p (r w) -> p r w", w=GRID_W)
                    dve.scalar_tensor_tensor(rows[:, :, 1:], src[:, :, :-1], pcol("conv_w", k), rows[:, :, 1:],
                                             ALU.mult, ALU.add).then_inc(S("conv_left"), 1)
                    dve.wait_ge(S("conv_left"), k + 1)
                    dve.scalar_tensor_tensor(rows[:, :, :-1], src[:, :, 1:], pcol("conv_w", 2 * KF + k), rows[:, :, :-1],
                                             ALU.mult, ALU.add).then_inc(S("conv_done"), 1)
                lo_ahead(U0 + 3, r, u)
                dve.wait_ge(S("silu_ready"), j + 1)
                dve.wait_ge(group_used, U0 + 2 * j + 2)
                dve.tensor_tensor(actf[:, u], cv[:, u], up_half(u), ALU.mult).then_inc(S("act_full"), 1)
                lo_ahead(U0 + 4, r, u)
                dve.wait_ge(S("act_hi_ready"), j + 1)
                pair = bass.ds(2 * j, 2)
                lo_part(act_lo[:, pair, :], actf[:, u], act_hi[:, pair, :], "act_lo")

            rounds(dve, up_step)
            s_next[0] = U0 + 2 * PAIRS + 3
            lo_until(at["down"][1] + 2)
            dve.wait_ge(S("ada_sum"), 3)
            times_gate(0, gp2)
            lo_until(at["down"][1] + 6 + 1)
            post_norm("post2", "norm3", gp2, 4)

            transposed("norm3", NORM_BANKS["norm3"], lambda k: pcol("attn_norm", k))
            G0 = at["gdn"][0]

            def gdn(j):
                lo_until(at["gdn"][j] + 3)
                dve.wait_ge(S("conv2_mid"), 2 * j + 2)
                for f in (2 * j, 2 * j + 1):
                    for back in (1, 2, 3):
                        src = ps[:, j % 2, (f % 2) * T:(f % 2) * T + T - back]
                        ins = dve.scalar_tensor_tensor(r5[:, f, back:], src, pcol("conv2", 12 * (3 - back) + f),
                                                       r5[:, f, back:], ALU.mult, ALU.add)
                        if back < 3:
                            link(ins)
                    ins.then_inc(S("conv2_done"), 1)
                lo_until(at["gdn"][j] + 4)

            gate_weights_lo(2, wsm)
            gdn(0)
            dve.wait_ge(S("gate_mm"), 2)
            dve.wait_ge(S("small_in"), 16 * 7)
            pre = ps[:, 4, 0:TT * 16].rearrange("p (t g) -> p t g", t=TT)
            for c in (slice(0, GH), slice(2 * GH, 16)):
                link(dve.tensor_tensor(sm[:, :, c], pre[:, :, c],
                                       gprm[:, c].unsqueeze(1).to_broadcast([P, TT, c.stop - c.start]), ALU.add))
                link(dve.scalar_tensor_tensor(sp2[:, :, c], sm[:, :, c], -1.0, sm[:, :, c], ALU.mult, ALU.max))
            dve.tensor_copy(sp2[:, :, GH:2 * GH], pre[:, :, GH:2 * GH]).then_inc(S("gate_abs"), 1)
            dve.wait_ge(S("gate_exp"), 3)
            link(dve.tensor_scalar(beta[:], sp2[:, :, GH:2 * GH], 1.0, None, ALU.add))
            dve.reciprocal(beta[:], beta[:]).then_inc(S("beta_ready"), 1)
            dve.wait_ge(S("gate_ln"), 2)
            link(dve.scalar_tensor_tensor(g_dec[:], sm[:, :, 0:GH], 0.0, sp2[:, :, 0:GH], ALU.max, ALU.add))
            dve.scalar_tensor_tensor(g_dec[:], g_dec[:], -1.0, gprm[:, GH:2 * GH].unsqueeze(1).to_broadcast([P, TT, GH]),
                                     ALU.mult, ALU.mult).then_inc(S("sgate_ready"), 1)
            dve.scalar_tensor_tensor(lf2[:], sm[:, :, 2 * GH:], 0.0, sp2[:, :, 2 * GH:], ALU.min, ALU.subtract)\
                .then_inc(S("sgate_ready"), 1)

            def heads(a):
                return a.rearrange("p (h n) -> p h n", h=GH)

            def per_head(a):
                return a.unsqueeze(2).to_broadcast([P, GH, GD])

            def token_norms(first):
                for i in (first, first + 1):
                    c = SS["l2"] + GH * i
                    dve.wait_ge(S("sq_ready"), i + 1)
                    dve.tensor_reduce(ss[:, c:c + GH], heads(sq[:, i % 2, :]), AX_X, ALU.add).then_inc(S("ss_l2"), 1)
                for i in (first, first + 1):
                    c = SS["l2"] + GH * i
                    dve.wait_ge(S("rstd_l2"), i + 1)
                    dve.tensor_tensor(heads(qk_n[:, i // 2, i % 2, :]), heads(ps[:, TOKEN_BANKS[i], :]),
                                      per_head(rstd[:, c:c + GH]), ALU.mult).then_inc(S("tok_out"), 1)

            gdn(1)
            dve.wait_ge(S("decay_mm"), 1)
            link(dve.tensor_copy(gc[:], ps[:, 4, 0:3 * GH].rearrange("p (a h) -> p a h", h=GH)))
            dve.tensor_copy(egc[:, 0, :], gc[:, 1, :]).then_inc(S("egc_diff"), 1)
            dve.tensor_tensor(egc[:, 2, :], gc[:, 2, :], gc[:, 0, :], ALU.subtract).then_inc(S("egc_diff"), 1)
            for t in range(TT):
                dve.wait_ge(S("decay_mm"), 1 + t + 1)
                for h in range(GH):
                    ins = dve.tensor_scalar(decT[:, GH * t + h, :], ps[:, 5 + t, h * P:(h + 1) * P], gc[:, t, h:h + 1], 0.0,
                                            ALU.subtract, ALU.min)
                    if h < GH - 1:
                        link(ins)
                ins.then_inc(S("dec_z"), 1)
            dve.wait_ge(S("egc_exp"), 2)
            dve.tensor_tensor(egc[:, 1, :], egc[:, 0, :], beta[:, 1, :], ALU.mult).then_inc(S("egc_ready"), 1)
            gdn(2)
            gdn(3)
            token_norms(0)
            token_norms(2)
            gdn(4)
            gdn(5)

            def all_heads(a, t):
                return a[:, GH * t:GH * (t + 1), :]

            def bank(b):
                return heads(ps[:, b, :])

            lo_until(at["fox"][1] + 3)
            dve.wait_ge(S("dec_ready"), TT)
            for t in range(TT):
                dve.wait_ge(S("kk_mm"), t + 1)
                link(dve.tensor_tensor(all_heads(cT, t), bank(4 + t), all_heads(decT, t), ALU.mult))
            for t in range(TT):
                dve.wait_ge(S("beta_mm"), t + 1)
                dve.tensor_tensor(all_heads(cT, t), all_heads(cT, t), bank(2 + t), ALU.mult).then_inc(S("cT_full"), 1)
            dve.wait_ge(S("level_ready"), 1)
            dve.wait_ge(S("cT_full"), TT)
            for t in range(TT):
                d = all_heads(invT, t)
                link(dve.tensor_tensor(d, all_heads(cT, t), level[:, 0, :].unsqueeze(1).to_broadcast([P, GH, P]), ALU.mult))
                dve.tensor_tensor(d, ident[:].unsqueeze(1).to_broadcast([P, GH, P]), d, ALU.subtract)\
                    .then_inc(S("inv_ready"), 1)
            for t in range(TT):
                dve.wait_ge(S("kk_mm"), TT + t + 1)
                dve.tensor_tensor(all_heads(qkT2, t), bank(6 + t), all_heads(decT, t), ALU.mult)\
                    .then_inc(S("qkT2_ready"), 1)
            for t in range(TT):
                dve.wait_ge(S("tok_T"), 4 + t + 1)
                dve.tensor_tensor(heads(vb[:, t, :]), heads(ps[:, 2 + t, :]), per_head(beta[:, t, :]), ALU.mult)\
                    .then_inc(S("tok_out"), 1)
            lo_until(at["fox_v"][0] + 3)

            def fox_logits(h):
                dve.wait_ge(S("logit_mm"), h + 1)
                if h >= 2:
                    dve.wait_ge(S("prT_mm"), h - 1)
                for t, part in ((0, slice(0, P)), (1, slice(P, 3 * P))):
                    dve.scalar_tensor_tensor(logit[:, h % 2, part], ps[:, 0, part], FD ** -0.5,
                                             neg_c[:, h, 0:(t + 1) * P], ALU.mult, ALU.add).then_inc(S("logit_ready"), 1)

            def fox_max(h):
                dve.wait_ge(S("logit_masked"), 2 * h + 2)
                for t, part in ((0, slice(0, P)), (1, slice(P, 3 * P))):
                    link(dve.tensor_reduce(fsum[:, h % 2, t:t + 1], logit[:, h % 2, part], AX_X, ALU.max))
                dve.tensor_scalar(fsum[:, h % 2, 0:2], fsum[:, h % 2, 0:2], -1.0, None, ALU.mult).then_inc(S("fox_max"), 1)

            def fox_done(h):
                dve.wait_ge(S("fox_mm"), h + 1)
                link(dve.reciprocal(fsum[:, h % 2, 2:4], fsum[:, h % 2, 2:4]))
                for t in range(TT):
                    c = GH * GD + FD * h
                    dve.tensor_scalar(mix[:, t, c:c + FD], ps[:, 2, t * FD:(t + 1) * FD], fsum[:, h % 2, 2 + t:3 + t], None,
                                      ALU.mult).then_inc(S("fox_done"), 1)

            def fox_step(i, update=None):
                if i < FH:
                    fox_logits(i)
                if i >= 2:
                    fox_done(i - 2)
                if update is not None:
                    update()
                if i < FH:
                    fox_max(i)

            fox_step(0)
            A0 = at["att_out"][0]
            lo_next = (at["fox_v"][0] + 4, at["fox"][2] + 3, at["fox"][3] + 3, at["z"][0] + 3, A0 + 2, A0 + 2)
            for i in range(len(LEVELS)):
                if i == 1:
                    dve.wait_ge(S("q_exp_ready"), 1)
                    dve.wait_ge(S("k_beta_ready"), 1)
                    dve.wait_ge(S("k_dec_ready"), 1)
                    dve.wait_ge(S("gT_mm"), GH)

                def update():
                    for t in range(TT):
                        dve.wait_ge(S("y_mm"), TT * i + t + 1)
                        if i < len(LEVELS) - 1:
                            link(dve.tensor_tensor(all_heads(inv, t), all_heads(inv, t), bank(6 + t), ALU.subtract))
                        dve.tensor_tensor(all_heads(invT, t), all_heads(invT, t), bank(4 + t), ALU.subtract)\
                            .then_inc(S("inv_ready"), 1)

                fox_step(FOX_STEPS[i][0], update)
                if FOX_STEPS[i][1] is not None and i == 4:
                    fox_step(FOX_STEPS[i][1])
                lo_until(lo_next[i])
                if FOX_STEPS[i][1] is not None and i != 4:
                    fox_step(FOX_STEPS[i][1])

            def mix_lo(i):
                dve.wait_ge(S("hi"), base("hi", "mix") + i + 1)
                k = 2 * MIX_PAIRS[i]
                pair, src = slice(k, k + 2), ps[:, 2 + i, :].rearrange("p (f t) -> p f t", f=2)
                if i < 2:
                    lo_part(h_lo[:, pair, :], src, h_hi[:, pair, :], "hT")
                else:
                    dve.scalar_tensor_tensor(h_lo[:, pair, :], src, pcol("gdn_norm", 0), h_hi[:, pair, :].bitcast(F32),
                                             ALU.mult, ALU.subtract).then_inc(S("hT"), 1)

            mix_lo(0)
            mix_lo(1)
            dve.wait_ge(S("u_out"), TT)
            dve.wait_ge(S("ws_mm"), 1)
            dve.tensor_tensor(v_new, u_tok[:, 1, :], ps[:, 6, :], ALU.subtract).then_inc(S("v_new_ready"), 1)
            lo_until(A0 + 3)
            dve.wait_ge(S("z_silu"), TT)
            for t in range(TT):
                dve.wait_ge(S("ss"), base("ss", "gdn") + GH * (t + 1))
                link(dve.tensor_tensor(og[:, t, :], ps[:, (0, 6)[t], :], zs[:, t, :], ALU.mult))
                dve.wait_ge(S("rstd"), base("rstd", "gdn") + t + 1)
                c = SS["gdn"] + GH * t
                dve.tensor_tensor(heads(mix[:, t, 0:GH * GD]), heads(og[:, t, :]), per_head(rstd[:, c:c + GH]), ALU.mult)\
                    .then_inc(S("mix_ready"), 1)
            mix_lo(2)
            mix_lo(3)
            lo_until(A0 + 5)
            for t in range(TT):
                if t == 0:
                    dve.wait_ge(S("t0_done"), base("t0_done", "att_out") + 1)
                else:
                    dve.wait_ge(group_used, A0 + 4)
                for n in range(2):
                    c = slice(n * NB, (n + 1) * NB)
                    dve.tensor_tensor(x[:, t, c], x[:, t, c], ps[:, OUT_BANKS[n][t], :], ALU.add).then_inc(S("x_upd"), 1)
            for t in range(TT):
                diagonal("norm4", t, base("rstd", "norm4") + t + 1)
            dve.sem_inc(S("act_full"), ROUND)
            transposed("norm4", NORM_BANKS["norm4"], lambda k: pcol("ffn_norm", k))
            V0 = at["gate_up"][0]
            lo_until(V0 + 3)

            def gate_up_step(r, u):
                j = ROUND * r + u
                lo_ahead(V0 + 3, r, u)
                dve.wait_ge(S("silu_ready"), PAIRS + j + 1)
                dve.wait_ge(group_used, V0 + 2 * j + 2)
                dve.tensor_tensor(actf2[:, u], sil[:, u], up_half(u), ALU.mult).then_inc(S("act_full"), 1)
                lo_ahead(V0 + 4, r, u)
                dve.wait_ge(S("act_hi_ready"), PAIRS + j + 1)
                pair = bass.ds(2 * j, 2)
                lo_part(act2_lo[:, pair, :], actf2[:, u], act2_hi[:, pair, :], "act_lo")

            rounds(dve, gate_up_step)
            s_next[0] = V0 + 2 * PAIRS + 3
            dve.wait_ge(S("p_T"), 1)
            dve.tensor_copy(pT[:].rearrange("p k t -> p (k t)"), ps[:, 6, :]).then_inc(S("pT_ready"), 1)
            dve.wait_ge(S("p_hi"), 1)
            lo_part(p_lo[:], pT[:], p_hi[:], "p_lo")
            residual("down2", 6)
            for t in range(TT):
                diagonal("norm5", t, base("rstd", "norm5") + t + 1)
            transposed("norm5", NORM_BANKS["norm5"], lambda k: pcol("ple_norm", k))
            lo_until(n_split)
            dve.wait_ge(S("p_out"), 4)
            dve.wait_ge(S("last_in"), 32)
            for n in range(2):
                for t in range(TT):
                    i = TT * n + t
                    c = slice(n * NB, (n + 1) * NB)
                    dve.wait_ge(S("sig_ready"), i + 1)
                    link(dve.tensor_tensor(pgate[:, t, c], pgate[:, t, c], tmp[:, i % 2, :], ALU.mult))
                    dve.tensor_tensor(x[:, t, c], x[:, t, c], pgate[:, t, c], ALU.add).then_inc(S("x_upd"), 1)
                    dve.wait_ge(S("x_upd"), 16 + i + 1)
                    dve.tensor_tensor(pgate[:, t, c], x[:, t, c], gp3[:, c], ALU.mult).then_inc(S("gained"), 1)
                    if n == 1:
                        dve.wait_ge(S("gained"), i + 1)
                        dve.wait_ge(S("rstd"), base("rstd", "final") + t + 1)
                        r = SS["final"] + t
                        dve.tensor_scalar(pgate[:, t, c], pgate[:, t, c], rstd[:, r:r + 1], None, ALU.mult)\
                            .then_inc(S("result1"), 1)

        @block.tensor
        def _(pe):
            def mm3(dst, left, right, first, last):
                (l_hi, l_lo), (r_hi, r_lo) = left, right
                pe.matmul(dst, l_hi, r_hi, start=first, stop=False)
                pe.matmul(dst, l_hi, r_lo, start=False, stop=False)
                return pe.matmul(dst, l_lo, r_hi, start=False, stop=last)

            def weights(s):
                pe.wait_ge(lo_ready, s + 1)
                return part_view(w_hi, s), part_view(w_lo, s)

            def token_group(s, g0, nk, source, ready=None):
                a_hi, a_lo, t, bank = source
                hi, lo = part_view(w_hi, s), part_view(w_lo, s)
                tok = slice(t * P, (t + 1) * P)
                k0 = 4 * (s - g0)
                for i, k in enumerate(range(k0, min(k0 + 4, nk))):
                    if ready is not None:
                        ready(k, t)
                    ins = mm3(ps[:, bank, :], (a_hi[:, k, tok], a_lo[:, k, tok]), (hi[:, i, :], lo[:, i, :]),
                              k == 0, k == nk - 1)
                return ins

            def token_block(g0, sources, nk=KD, after_first=None, ready=None, free=None, done=None, tail=None):
                last = g0 + (nk + 3) // 4 - 1
                together = range(g0, last - 1 if tail else last + 1)
                for s in together:
                    weights(s)
                    for i, source in enumerate(sources):
                        if free is not None and s == g0:
                            free(i)
                        ins = token_group(s, g0, nk, source, ready)
                        if done is not None and s == last and i < len(sources) - 1:
                            ins.then_inc(S(done), 1)
                    ins.then_inc(group_used, 1)
                    if after_first is not None and s == g0:
                        after_first()
                if tail:
                    for i, source in enumerate(sources):
                        for s in (last - 1, last):
                            weights(s)
                            ins = token_group(s, g0, nk, source, ready)
                            if i == len(sources) - 1:
                                ins.then_inc(group_used, 1)
                            elif s == last:
                                ins.then_inc(S("t0_done"), 1)

            def feature_tiles(s, bank, r=0, ready=None, between=None):
                s, r = in_round(s, r)
                pe.wait_ge(lo_ready, s + 1 + 2 * ROUND * r)
                hi, lo = part_view(w_hi, s), part_view(w_lo, s)
                for f in range(2):
                    if f == 1 and between is not None:
                        between()
                    fs_ = slice(f * P, (f + 1) * P)
                    for k in range(KD):
                        if ready is not None and f == 0:
                            ready(k)
                        ins = mm3(ps[:, bank, f * T:(f + 1) * T], (hi[:, k, fs_], lo[:, k, fs_]),
                                  (h_hi[:, k, :], h_lo[:, k, :]), k == 0, k == KD - 1)
                ins.then_inc(group_used, 1)

            def transposed(name):
                for t in range(TT):
                    pe.wait_ge(S("diag"), base("diag", name) + t + 1)
                    for k in range(KD):
                        dst = ps[:, NORM_BANKS[name][k // 2], k % 2 * T + t * P:k % 2 * T + (t + 1) * P]
                        ins = pe.matmul(dst, x[:, t, k * P:(k + 1) * P], diag[:, t, :], start=True, stop=True)
                        if t == TT - 1 and k % 2:
                            ins.then_inc(S("tr"), 1)

            def pair_of(name):
                return lambda k: pe.wait_ge(S("hT"), base("hT", name) + max(k + 1, 2))

            def hT(name):
                return lambda k, t: pe.wait_ge(S("hT"), base("hT", name) + k + 1) if t == 0 else None

            def flip(dst, src):
                n = src.shape[0]
                return pe.transpose(dst, src, ident[0:n, 0:n])

            X0, X1 = (h_hi, h_lo, 0), (h_hi, h_lo, 1)
            C0, C1 = (c_hi, c_lo, 0), (c_hi, c_lo, 1)

            pe.wait_ge(S("const_ready"), 1)
            pe.wait_ge(S("c_in"), 32)
            flip(ps[:, 7, 0:2 * KD], c_rows[:]).then_inc(S("vec_T"), 1)

            def ada1_group(i):
                n, half = i // 2, i % 2
                raw_arrived(pe, ada1[i])
                if half == 0 and n >= 2:
                    pe.wait_ge(S("ada_rows"), n - 1)
                if n == 3:
                    pe.wait_ge(S("x_out"), 8)
                for kk in range(4):
                    ins = pe.matmul(ps[32 * kk:32 * kk + 32, ADA_BANKS[n], :], cpad[:, 4 * half + kk, :],
                                    raw_view(ada1[i])[:, kk, :], start=half == 0, stop=half == 1)
                ins.then_inc(ada1_used, 1)

            def ada1_columns(n):
                if n == 0:
                    pe.wait_ge(S("const_ready"), 2)
                pe.wait_ge(S("ada_rows"), n + 1)
                for j in range(4 * n, 4 * n + 4):
                    ins = pe.matmul(ps[:, 6, 2 * j:2 * j + 2], ada_rows[:, n, (j % 4) * P:(j % 4 + 1) * P], row_of[:],
                                    start=True, stop=True)
                ins.then_inc(S("ada_T"), 1)

            def first_transposed(c, i):
                if c:
                    pe.wait_ge(S("x_out"), i + 1)
                for k in (2 * i, 2 * i + 1):
                    for t in range(TT):
                        if i == 0 and k == 0:
                            pe.wait_ge(S("diag"), TT * c + t + 1)
                        dst = ps[:, 2 + i, k % 2 * T + t * P:k % 2 * T + (t + 1) * P]
                        ins = pe.matmul(dst, (ctx_tok if c else x)[:, t, k * P:(k + 1) * P], diag[:, TT * c + t, :],
                                        start=True, stop=True)
                ins.then_inc(S("tr"), 1)

            pe.wait_ge(S("c_ready"), 1)
            for i in range(6):
                ada1_group(i)
                if i in (2, 4):
                    ada1_columns(i // 2 - 1)
                if i == 2:
                    for pair in range(4):
                        first_transposed(0, pair)
            pe.wait_ge(S("vec_in"), 16 * (len(VEC) + 3))
            at_col = 2 * KD
            for rows in vec_rows:
                n = rows.shape[0]
                flip(ps[:, 7, at_col:at_col + n], rows).then_inc(S("vec_T"), 1)
                at_col += n
            first_transposed(1, 0)
            ada1_columns(2)
            for pair in range(1, 4):
                first_transposed(1, pair)

            def gates_by_row(i, sides):
                pe.wait_ge(S("wg_lo"), i)
                for c, parts in enumerate(sides):
                    dst = ps[0:32, 4, c * T:(c + 1) * T]
                    for k in range(KD):
                        for part in parts:
                            ins = pe.matmul(dst, wg_parts[:, k, :], part[:, k, :], start=k == 0 and part is parts[0],
                                            stop=k == KD - 1 and part is parts[1])
                ins.then_inc(S("gate_rows_mm"), 1)

            def gates_by_token(i, tiles, want):
                pe.wait_ge(S("gate_rows"), i)
                for t in range(tiles):
                    ins = pe.matmul(ps[:, 4, 16 * t:16 * t + 16], gate_rows[:, t * P:(t + 1) * P], fold[:], start=True, stop=True)
                ins.then_inc(S(want), 1)

            every = [(*X0, 0), (*X1, 1), (*C0, 2), (*C1, 3)]
            pairs = {id(h_hi): (1, 2, 5, 6), id(c_hi): (3, 4, 7, 8)}
            g0 = at["k"][0]

            def k_part(s, sources):
                for source in sources:
                    ins = token_group(s, g0, KD, source,
                                      lambda k, t: pe.wait_ge(S("hT"), pairs[id(source[0])][k // 2]) if t == 0 else None)
                return ins

            ada1_group(6)
            weights(g0)
            k_part(g0, every[:1])
            ada1_group(7)
            k_part(g0, every[1:TT])
            ada1_columns(3)
            k_part(g0, every[TT:]).then_inc(group_used, 1)
            pe.wait_ge(S("hT"), KD)
            gates_by_row(1, ((h_hi, h_lo), (c_hi, c_lo)))
            weights(g0 + 1)
            k_part(g0 + 1, every[:1])
            gates_by_token(1, 2 * TT, "gate_mm")
            k_part(g0 + 1, every[1:]).then_inc(group_used, 1)

            pe.wait_ge(S("lf_ready"), 1)

            def lf_of(tile, d):
                return lf[:, 2 * tile + d, :]

            for a in range(2):
                for t in range(TT):
                    for d in range(2):
                        dst = ps[:, 4, 16 * a + 8 * t + 4 * d:16 * a + 8 * t + 4 * d + 4]
                        tri = ((s_le_t, s_ge_t), (s_gt_t, s_lt_t))[a][d]
                        other = t != (a + d) % 2
                        pe.matmul(dst, tri[:], lf_of(TT * a + t, d), start=True, stop=not other)
                        if other:
                            pe.matmul(dst, ones[:], lf_of(TT * a + 1 - t, d), start=False, stop=True)
            for d in range(2):
                for t in range(TT):
                    ins = pe.matmul(ps[0:MH, 4, 32 + d:33 + d], lf_of(TT + t, d), ones[:, 0:1], start=t == 0, stop=t == 1)
            ins.then_inc(S("cum_mm"), 1)

            def exponent_rows():
                pe.wait_ge(S("u_ready"), 3)
                for bank, src in ((7, u_col), (4, gs_col)):
                    for t in range(TT):
                        for d in range(2):
                            ins = flip(ps[0:MH, bank, d * T + t * P:d * T + (t + 1) * P], src[:, 2 * t + d, :])
                ins.then_inc(S("u_rows"), 1)

            token_block(at["q"][0], [(*X0, 5), (*X1, 6)], after_first=exponent_rows)

            def qk_by_channel():
                pe.wait_ge(S("k_done"), 4)
                pe.wait_ge(S("q_done"), 2)
                for h in range(MH):
                    if h >= 2:
                        pe.wait_ge(S("qkT_ready"), 2 * (h - 1))
                    for a in range(2):
                        for t in range(TT):
                            ins = flip(ps[:, 5 + h % 2, a * T + t * P:a * T + (t + 1) * P],
                                       qk_tok[:, a, t, h * DK:(h + 1) * DK])
                    ins.then_inc(S("qk_T"), 1)
                pe.wait_ge(S("mrow_ready"), 2)
                pe.wait_ge(S("ws_row"), 2)
                for i, src in enumerate((m_row, ws_row)):
                    for t in range(TT):
                        for d in range(2):
                            c = 16 * i + 8 * t + 4 * d
                            ins = flip(ps[:, 7, c:c + 4], src[:, d, t * P:(t + 1) * P])
                ins.then_inc(S("m_cols"), 1)

            def scores(h):
                if h == 0:
                    pe.wait_ge(S("w_row"), 2)
                    pe.wait_ge(S("qkT_ready"), 2 * MH)
                if h == 1:
                    pe.wait_ge(S("ws_out"), 1)
                if h >= 2:
                    pe.wait_ge(S("prob_full"), 2 * (h - 1))
                for t in range(TT):
                    ins = pe.matmul(ps[:, (4, 7)[h % 2], t * T:(t + 1) * T], qkT[:, h, 1, t * P:(t + 1) * P], qkT[:, h, 0, :],
                                    start=True, stop=True)
                ins.then_inc(S("score_mm"), 1)
                for d in range(2):
                    if h:
                        pe.wait_ge(S("qTw_ready"), 2 * (h - 1) + d + 1)
                    pe.matmul(ps[:, 5 + d, 0:T], sel[:, h, :], m_row[:, d, :], start=True, stop=True)
                    pe.matmul(ps[:, 5 + d, T:2 * T], sel[:, h, :], w_row[:, d, :], start=True, stop=True)\
                        .then_inc(S("m_bcast"), 1)

            pe.wait_ge(S("k_done"), 4)
            token_block(at["v"][0], every, after_first=qk_by_channel)
            scores(0)
            token_block(at["v"][1], every, after_first=lambda: scores(1),
                        free=lambda i: pe.wait_ge(S("v_done"), i + 1))
            scores(2)

            def ctx_state(h):
                pe.wait_ge(S("kw_ready"), h + 1)
                pe.wait_ge(S("v_done"), 8)
                if h < 2:
                    pe.wait_ge(S("prob_full"), 2 * (h + 3))
                    pe.wait_ge(S("qTw_ready"), 2 * MH)
                if h >= 2:
                    pe.wait_ge(S("state_out"), 2 * (h - 1))
                for d in range(2):
                    for t in range(TT):
                        ins = pe.matmul(ps[:, 4 + 2 * (h % 2) + d, 0:DV + 1], kw[:, h % 2, t, d, :], vaug[:, TT + t, h, :],
                                        start=t == 0, stop=t == 1)
                    ins.then_inc(S("state_mm"), 1)

            def outputs(h):
                pe.wait_ge(S("prob_ready"), 2 * h + 2)
                pe.wait_ge(S("state_out"), 2 * MH)
                if h:
                    pe.wait_ge(S("h_sum"), 2 * h)
                for d in range(2):
                    pr = prob[:, h, d, :]
                    for t in range(TT):
                        dst = ps[:, 4 + 2 * d + t, 0:DV + 1]
                        pe.matmul(dst, qTw[:, h, d, t * P:(t + 1) * P], state[:, h, d, :], start=True, stop=False)
                        if t != d:
                            pe.matmul(dst, pr[:, T:T + P], vaug[:, 1 - d, h, :], start=False, stop=False)
                        ins = pe.matmul(dst, pr[:, t * P:(t + 1) * P], vaug[:, d, h, :], start=False, stop=True)
                ins.then_inc(S("out_mm"), 1)

            def gate_vector(v, bank):
                for n in range(2):
                    pe.matmul(ps[:, bank + n, :], ones[:], ada_acc[v][:, n * NB:(n + 1) * NB], start=True, stop=False)
                    for j in range(4):
                        c = col["ada_b"] + (2 + v) * KD + 4 * n + j
                        ins = pe.matmul(ps[:, bank + n, j * P:(j + 1) * P], cols[:, c:c + 1].to_broadcast([P, P]), ident[:],
                                        start=False, stop=j == 3)
                ins.then_inc(S("ada_sum"), 1)

            def out_states(h):
                ctx_state(h)
                ctx_state(h + 1)

            token_block(at["o"][0], [(*X0, 0), (*X1, 1)], free=lambda i: pe.wait_ge(S("v_done"), 4 + i + 1),
                        after_first=lambda: scores(3))
            out_states(0)
            token_block(at["o"][1], [(*X0, 2), (*X1, 3)], free=lambda i: pe.wait_ge(S("v_done"), 6 + i + 1),
                        after_first=lambda: out_states(2))
            outputs(0)
            pe.wait_ge(S("o_done"), 2)
            pe.wait_ge(ada2_used, len(ada2) - 4)
            gate_vector(0, 0)
            outputs(1)
            pe.wait_ge(S("o_done"), 3)
            for j in range(2 * KD):
                ins = pe.matmul(ps[:, 2, j:j + 1], ada_acc[1 + j // KD][:, (j % KD) * P:(j % KD + 1) * P], ones[:, 0:1],
                                start=True, stop=True)
            ins.then_inc(S("ada_sum"), 1)
            def y_pair(h):
                pe.wait_ge(S("y1_ready"), TT * (h + 1))
                if h >= 2:
                    pe.wait_ge(S("hT"), base("hT", "y1") + 2 * (h - 1))
                for f in range(2):
                    for t in range(TT):
                        k = 2 * h + f
                        ins = flip(ps[:, h % 2, f * T + t * P:f * T + (t + 1) * P], ymix[:, t, k * P:(k + 1) * P])
                ins.then_inc(S("tr"), 1)

            outputs(2)
            pe.wait_ge(S("mods_out"), 2)
            y_pair(0)
            y_pair(1)
            outputs(3)
            y_pair(2)
            pe.wait_ge(S("o_done"), 4)
            pe.wait_ge(S("mods_out"), 3)
            token_block(at["mix_out"][0], [(*X0, 2), (*X1, 3)], ready=hT("y1"), after_first=lambda: y_pair(MH - 1))
            pe.wait_ge(S("h_sum"), 2 * MH)
            token_block(at["mix_out"][1], [(*X0, 4), (*X1, 5)], tail="t0_done")

            def ffn(name, norm):
                def step(r, u):
                    pe.wait_ge(S("act_full"), base("act_full", name) + ROUND * r + u + 1)
                    for half in range(2):
                        feature_tiles(at[name][2 * u + half], 2 * u + half, r, pair_of(norm) if u == half == 0 else None)

                rounds(pe, step)

            def second(name, first, hi, lo, before_last=None):
                pe.wait_ge(S("act_full"), base("act_full", first) + PAIRS + ROUND - 2)
                for n in range(2):
                    token_block(at[name][n], [(hi, lo, 0, 4 + 2 * n), (hi, lo, 1, 5 + 2 * n)], nk=KF,
                                ready=lambda k, t: pe.wait_ge(S("act_lo"), base("act_lo", first) + k // 2 + 1) if not n and not t else None,
                                tail="t0_done" if n and name == "down" else None)
                    if n == 0 and before_last is not None:
                        before_last()

            def gate2():
                pe.wait_ge(ada2_used, len(ada2))
                pe.wait_ge(S("act_full"), ROUND + PAIRS)
                gate_vector(3, 0)

            transposed("norm2")
            ffn("up", "norm2")
            second("down", "up", act_hi, act_lo, gate2)

            transposed("norm3")
            def gdn_tiles(j, between=None):
                if j >= 2:
                    pe.wait_ge(S("conv2_done"), 2 * (j - 1))
                feature_tiles(at["gdn"][j], j % 2, ready=pair_of("norm3") if j == 0 else None, between=between)

            def to_tokens(i, t, bank):
                pe.wait_ge(S("conv2_silu"), 4 * i + 4)
                for h in range(GH):
                    ins = flip(ps[:, bank, h * GD:(h + 1) * GD], r5[:, 4 * i + h, t * P:(t + 1) * P])
                ins.then_inc(S("tok_T"), 1)

            def decay_sums():
                pe.wait_ge(S("sgate_ready"), 1)
                for t in range(TT):
                    pe.matmul(ps[:, 4, 4 * t:4 * t + 4], s_le_t[:], g_dec[:, t, :], start=True, stop=True)
                pe.matmul(ps[:, 4, 8:12], ones[:], g_dec[:, 0, :], start=True, stop=True).then_inc(S("decay_mm"), 1)
                for t in range(TT):
                    for h in range(GH):
                        ins = pe.matmul(ps[:, 5 + t, h * P:(h + 1) * P], g_dec[:, t, h:h + 1].to_broadcast([P, P]),
                                        s_le_t[:], start=True, stop=True)
                    ins.then_inc(S("decay_mm"), 1)

            def forget_sums(i):
                if i == 0:
                    pe.wait_ge(S("sgate_ready"), 2)
                else:
                    pe.wait_ge(S("neg_c_out"), i)
                for b in range(2):
                    f0, f1 = (lf2[:, t, 2 * i + b:2 * i + b + 1].to_broadcast([P, P]) for t in range(TT))
                    c = b * T
                    pe.matmul(ps[:, 7, c:c + P], f0, s_le_t[:], start=True, stop=True)
                    pe.matmul(ps[:, 7, c + P:c + T], f0, ones[:], start=True, stop=False)
                    ins = pe.matmul(ps[:, 7, c + P:c + T], f1, s_le_t[:], start=False, stop=True)
                ins.then_inc(S("fsum_mm"), 1)

            def fox_tiles(m):
                if m < 2:
                    pe.wait_ge(S("conv2_done"), 8 + 2 * (m + 1))
                elif m == 2:
                    pe.wait_ge(S("fox_v_out"), TT)
                else:
                    pe.wait_ge(S("fox_T"), 2 * m)
                feature_tiles(at["fox"][m], m if m < 2 else 3)

            gdn_tiles(0)
            gates_by_row(2, ((h_hi, h_lo),))
            gdn_tiles(1, between=lambda: gates_by_token(2, TT, "gate_mm"))
            gdn_tiles(2)
            decay_sums()
            forget_sums(0)
            gdn_tiles(3)
            pe.wait_ge(S("dec_z"), TT)
            to_tokens(0, 0, TOKEN_BANKS[0])
            to_tokens(0, 1, TOKEN_BANKS[1])
            forget_sums(1)
            gdn_tiles(4)
            forget_sums(2)
            to_tokens(1, 0, TOKEN_BANKS[2])
            to_tokens(1, 1, TOKEN_BANKS[3])
            forget_sums(3)
            gdn_tiles(5)

            pe.wait_ge(S("tok_out"), 4)
            pe.wait_ge(S("neg_c_out"), 4)
            for h in range(GH):
                for a in range(2):
                    for t in range(TT):
                        ins = flip(ps[:, 4 + h, a * T + t * P:a * T + (t + 1) * P], qk_n[:, a, t, h * GD:(h + 1) * GD])
                ins.then_inc(S("gT_mm"), 1)
            for t in range(TT):
                for h in range(GH):
                    ins = pe.matmul(ps[:, 2 + t, h * P:(h + 1) * P], beta[:, t, h:h + 1].to_broadcast([P, P]), ident[:],
                                    start=True, stop=True)
                ins.then_inc(S("beta_mm"), 1)
            fox_tiles(0)
            pe.wait_ge(S("gT_ready"), GH)
            for a, bank in ((1, 4), (0, 6)):
                for t in range(TT):
                    tok = slice(t * P, (t + 1) * P)
                    for h in range(GH):
                        ins = pe.matmul(ps[:, bank + t, h * P:(h + 1) * P], gT[:, h, 1, tok], gT[:, h, a, tok],
                                        start=True, stop=True)
                    ins.then_inc(S("kk_mm"), 1)
            fox_tiles(1)
            pe.wait_ge(S("cT_full"), TT)
            to_tokens(2, 0, 2)
            to_tokens(2, 1, 3)

            def by_token(name, t):
                g0 = at[name][0]
                for s in (g0, g0 + 1):
                    weights(s)
                    ins = token_group(s, g0, KD, (h_hi, h_lo, t, 3))
                    if t == 1:
                        ins.then_inc(group_used, 1)
                if t == 0:
                    ins.then_inc(S("first_tile"), 1)

            def fox_v_tile(t):
                if t == 0:
                    pe.wait_ge(S("tok_out"), 6)
                else:
                    pe.wait_ge(S("fox_v_out"), 1)
                by_token("fox_v", t)

            def z_tile(t):
                if t == 0:
                    pe.wait_ge(S("fox_T"), 8)
                else:
                    pe.wait_ge(S("z_out"), 1)
                by_token("z", t)

            def fox_logits(h):
                if h == 0:
                    pe.wait_ge(S("fox_T"), 4)
                else:
                    pe.wait_ge(S("logit_ready"), 2 * h)
                if h == FH // 2:
                    pe.wait_ge(S("fox_T"), 8)
                row = slice(FD * (h % 2), FD * (h % 2) + FD)
                q, k = foxT[row, h // 2, :], foxT[row, FH // 2 + h // 2, :]
                pe.matmul(ps[:, 0, 0:P], q[:, 0:P], k[:, 0:P], start=True, stop=True)
                pe.matmul(ps[:, 0, P:3 * P], q[:, P:T], k, start=True, stop=True).then_inc(S("logit_mm"), 1)

            def fox_transpose(h):
                pe.wait_ge(S("prob2_ready"), 2 * h + 2)
                if h:
                    pe.wait_ge(S("prT_ready"), h)
                for i in range(3):
                    ins = flip(ps[:, 1, i * P:(i + 1) * P], logit[:, h % 2, i * P:(i + 1) * P])
                ins.then_inc(S("prT_mm"), 1)

            def fox_out(h):
                pe.wait_ge(S("prT_ready"), h + 1)
                if h == 0:
                    pe.wait_ge(S("fox_v_out"), TT)
                else:
                    pe.wait_ge(S("fox_done"), 2 * h)
                v = fox_v[:, :, h * FD:(h + 1) * FD]
                pe.matmul(ps[:, 2, 0:FD], prT[:, h % 2, 0:P], v[:, 0], start=True, stop=True)
                pe.matmul(ps[:, 2, FD:2 * FD], prT[:, h % 2, P:2 * P], v[:, 0], start=True, stop=False)
                pe.matmul(ps[:, 2, FD:2 * FD], prT[:, h % 2, 2 * P:], v[:, 1], start=False, stop=True)\
                    .then_inc(S("fox_mm"), 1)

            def fox_step(i):
                if i < FH:
                    fox_logits(i)
                if 1 <= i <= FH:
                    fox_transpose(i - 1)
                if 2 <= i <= FH + 1:
                    fox_out(i - 2)

            fox_step(0)
            for t in range(TT):
                pe.wait_ge(S("inv_ready"), t + 1)
                for h in range(GH):
                    ins = flip(ps[:, 4 + t, h * P:(h + 1) * P], invT[:, GH * t + h, :])
                ins.then_inc(S("invT_T"), 1)
            pe.wait_ge(S("q_exp_ready"), 1)
            pe.wait_ge(S("qkT2_ready"), TT)
            for h in range(GH):
                ins = flip(ps[:, 6, h * P:(h + 1) * P], q_exp[:, h * GD:(h + 1) * GD])
            ins.then_inc(S("q_expT_mm"), 1)
            fox_v_tile(0)
            between = (lambda: fox_v_tile(1), lambda: fox_tiles(2), lambda: fox_tiles(3), lambda: z_tile(0),
                       lambda: z_tile(1), None)
            for i in range(len(LEVELS)):
                last = i == len(LEVELS) - 1
                pe.wait_ge(S("cTl_ready"), i + 1)
                for t in range(TT):
                    pe.wait_ge(S("inv_ready"), TT * i + t + 1)
                    if i == 0:
                        pe.wait_ge(S("inv0_ready"), t + 1)
                    for h in range(GH):
                        a = GH * t + h
                        ins = pe.matmul(ps[:, 4 + t, h * P:(h + 1) * P], cTl[:, i % 2, a, :], inv[:, a, :],
                                        start=True, stop=True)
                    ins.then_inc(S("xs_mm"), 1)
                fox_step(FOX_STEPS[i][0])
                for t in range(TT):
                    pe.wait_ge(S("xs_ready"), TT * i + t + 1)
                    if i == 0 and t == 0:
                        pe.wait_ge(S("q_expT_ready"), 1)
                    if not last:
                        for h in range(GH):
                            a = GH * t + h
                            pe.matmul(ps[:, 6 + t, h * P:(h + 1) * P], invT[:, a, :], xs[:, a, :], start=True, stop=True)
                    for h in range(GH):
                        a = GH * t + h
                        ins = pe.matmul(ps[:, 4 + t, h * P:(h + 1) * P], xs[:, a, :], invT[:, a, :], start=True, stop=True)
                    ins.then_inc(S("y_mm"), 1)
                if between[i] is not None:
                    between[i]()
                if FOX_STEPS[i][1] is not None:
                    fox_step(FOX_STEPS[i][1])
            for t in range(TT):
                pe.wait_ge(S("inv_ready"), TT * len(LEVELS) + t + 1)
                pe.wait_ge(S("inv_ready"), TT * (len(LEVELS) + 1))
                for h in range(GH):
                    ins = pe.matmul(ps[:, 4 + t, h * P:(h + 1) * P], invT[:, GH * t + h, :], vb[:, t, h * GD:(h + 1) * GD],
                                    start=True, stop=True)
                ins.then_inc(S("u_mm"), 1)
            pe.wait_ge(S("k_beta_ready"), 1)
            for h in range(GH):
                ins = pe.matmul(ps[:, 6, h * P:(h + 1) * P], k_beta[:, h * GD:(h + 1) * GD], invT[:, GH + h, :],
                                start=True, stop=True)
            ins.then_inc(S("u_mm"), 1)

            def mix_pair(i):
                if i == 0:
                    pe.wait_ge(S("fox_done"), TT * FH)
                    pe.wait_ge(S("z_out"), TT)
                if i == 2:
                    pe.wait_ge(S("mix_ready"), TT)
                    pe.wait_ge(S("u_out"), TT)
                for f in range(2):
                    k = 2 * MIX_PAIRS[i] + f
                    for t in range(TT):
                        ins = flip(ps[:, 2 + i, f * T + t * P:f * T + (t + 1) * P], mix[:, t, k * P:(k + 1) * P])
                ins.then_inc(S("tr"), 1)

            def att_out(i, t):
                half, n = i // 2, i % 2
                k0 = 2 * MIX_PAIRS[2 * half]
                hi, lo = weights(at["att_out"][0] + i)
                tok = slice(t * P, (t + 1) * P)
                for kk in range(GH):
                    if n == 0 and t == 0 and kk % 2 == 0:
                        pe.wait_ge(S("hT"), base("hT", "mix") + 2 * half + kk // 2 + 1)
                    ins = mm3(ps[:, OUT_BANKS[n][t], :], (h_hi[:, k0 + kk, tok], h_lo[:, k0 + kk, tok]),
                              (hi[:, kk, :], lo[:, kk, :]), half == 0 and kk == 0, half == 1 and kk == GH - 1)
                if t == TT - 1:
                    ins.then_inc(group_used, 1)
                elif i == 3:
                    ins.then_inc(S("t0_done"), 1)

            mix_pair(0)
            mix_pair(1)
            pe.wait_ge(S("k_dec_ready"), 1)
            pe.wait_ge(S("u_out"), 1)
            for h in range(GH):
                hs = slice(h * GD, (h + 1) * GD)
                ins = pe.matmul(ps[:, 7, hs], k_dec[:, hs], u_tok[:, 0, hs], start=True, stop=True)
            ins.then_inc(S("st_mm"), 1)
            pe.wait_ge(S("logit_ready"), TT * FH)
            for h in range(GH):
                hs = slice(h * GD, (h + 1) * GD)
                ins = pe.matmul(ps[:, 0, hs], qkT2[:, h, :], u_tok[:, 0, hs], start=True, stop=True)
            ins.then_inc(S("o_mm"), 1)
            pe.wait_ge(S("st_ready"), 1)
            pe.wait_ge(S("wT_ready"), 1)
            for h in range(GH):
                hs = slice(h * GD, (h + 1) * GD)
                ins = pe.matmul(ps[:, 6, hs], wT[:, hs], st1[:, hs], start=True, stop=True)
            ins.then_inc(S("ws_mm"), 1)
            att_out(0, 0)
            pe.wait_ge(S("v_new_ready"), 1)
            for h in range(GH):
                hs = slice(h * GD, (h + 1) * GD)
                pe.matmul(ps[:, 6, hs], q_expT[:, h, :], st1[:, hs], start=True, stop=False)
                ins = pe.matmul(ps[:, 6, hs], qkT2[:, GH + h, :], v_new[:, hs], start=False, stop=True)
            ins.then_inc(S("o_mm"), 1)
            att_out(0, 1)
            att_out(1, 0)
            mix_pair(2)
            mix_pair(3)
            att_out(1, 1)
            for t in range(TT):
                att_out(2, t)
                att_out(3, t)
            transposed("norm4")
            ffn("gate_up", "norm4")
            pe.wait_ge(S("last_in"), 32)
            for k in range(2):
                for t in range(TT):
                    ins = flip(ps[:, 6, k * T + t * P:k * T + (t + 1) * P], p_tok[:, t, k * P:(k + 1) * P])
            ins.then_inc(S("p_T"), 1)
            second("down2", "gate_up", act2_hi, act2_lo, lambda: pe.wait_ge(S("pT_ready"), 1))
            pe.wait_ge(S("act_full"), 2 * (ROUND + PAIRS))
            pe.wait_ge(S("p_lo"), 1)
            s = at["ple_p"][0]
            hi, lo = weights(s)
            for n in range(2):
                for t in range(TT):
                    for k in range(2):
                        tok, c = slice(t * P, (t + 1) * P), slice(n * NB, (n + 1) * NB)
                        ins = mm3(ps[:, 2 * n + t, :], (p_hi[:, k, tok], p_lo[:, k, tok]), (hi[:, k, c], lo[:, k, c]),
                                  k == 0, k == 1)
            ins.then_inc(group_used, 1)
            pe.wait_ge(S("x_upd"), 16)
            transposed("norm5")
            pe.wait_ge(S("p_out"), 4)
            token_block(at["ple_g"][0], [(*X0, 0), (*X1, 1)], ready=hT("norm5"), done="ple_mm")
            token_block(at["ple_g"][1], [(*X0, 2), (*X1, 3)], tail="t0_done")


_INS = ['x', 'c', 'ctx', 'c_ctx', 'ada_w', 'ada_b', 'pre_mix_g', 'post_mix_g', 'pre_ffn_g', 'post_ffn_g', 'ffn_up_w',
        'ffn_conv_w', 'ffn_conv_b', 'ffn_down_w', 'm_in_w', 'm_in_b', 'm_norm_g', 'm_out_w', 'p_2', 'attn_norm_w_2',
        'w_in_2', 'conv_w_2', 'a_log_2', 'dt_bias_2', 'gdn_norm_w_2', 'fox_f_bias_2', 'w_out_2', 'ffn_norm_w_2',
        'w_gate_up_2', 'w_down_2', 'ple_norm_w_2', 'w_ple_gate_2', 'w_ple_proj_2', 'final_norm_w_2']


def kernel(**inputs):
    import numpy as _np
    import concourse.bacc as _bacc
    from concourse import mybir as _mybir
    from concourse.bass_utils import run_bass_kernel_spmd as _run

    nc = _bacc.Bacc("TRN2", target_bir_lowering=False, num_devices=1, dynamic_dma_scratch_size=1024)
    arrays, tensors = {}, {}
    for name in _INS:
        a = _np.ascontiguousarray(inputs[name])
        arrays[f"in_{name}"] = a
        tensors[name] = nc.dram_tensor(f"in_{name}", a.shape, _mybir.dt.from_np(a.dtype), kind="ExternalInput").ap()
    out = nc.dram_tensor("out", (1, T, D), F32, kind="ExternalOutput").ap()
    two_blocks(nc, tensors, out)
    r = _run(nc, [arrays], core_ids=[0])
    return r.results[0]["out"]
```
